# Optimizing a Trainium2 kernel written in Bass

```python
import math
import jax, jax.numpy as jnp
from jax import lax
import numpy as np

D_MODEL = 1024
BATCH = 1
SEQ = 512
DEPTH = 2

POOL_WIDTH = D_MODEL // 4
FOURIER_WIDTH = D_MODEL // 4
ATTN_WIDTH = D_MODEL // 2
POOL_WINDOWS = (2, 4, 8, 16)
N_POOL_GROUPS = len(POOL_WINDOWS)
POOL_GROUP_DIM = POOL_WIDTH // N_POOL_GROUPS
N_FOURIER_GROUPS = 4
FOURIER_GROUP_DIM = FOURIER_WIDTH // N_FOURIER_GROUPS
ATTN_HEADS = 4
ATTN_HEAD_DIM = ATTN_WIDTH // (2 * ATTN_HEADS)
ATTN_V_DIM = 2 * ATTN_HEAD_DIM
Q_BLOCK = 128
D_FF = 2816
IN_COLS = POOL_WIDTH + FOURIER_WIDTH + 3 * ATTN_WIDTH
NORM_EPS = 1e-6


def alibi_slopes(n_heads):
    return jnp.array([2.0 ** (-8.0 * (i + 1) / n_heads) for i in range(n_heads)], dtype=jnp.float32)

def lambda_init_fn(layer_idx):
    return 0.8 - 0.6 * math.exp(-0.3 * layer_idx)

def rmsnorm(x, g):
    xf = x.astype(jnp.float32)
    y = xf * lax.rsqrt(jnp.mean(xf * xf, axis=-1, keepdims=True) + NORM_EPS)
    return (y * g.astype(jnp.float32)).astype(x.dtype)

def swiglu(x, w_gate, w_up, w_down):
    return (jax.nn.silu(x @ w_gate) * (x @ w_up)) @ w_down

def pool_mixer(a, pool_w, pool_scale):
    B, S, _ = a.shape
    af = a.reshape(B, S, N_POOL_GROUPS, POOL_GROUP_DIM).astype(jnp.float32)
    prefix = jnp.concatenate(
        [jnp.zeros((B, 1, N_POOL_GROUPS, POOL_GROUP_DIM), jnp.float32), jnp.cumsum(af, axis=1)], axis=1)
    t = jnp.arange(S)
    outs = []
    for g, w in enumerate(POOL_WINDOWS):
        left = w // 2
        right = w - 1 - left
        hi = jnp.minimum(t + right + 1, S)
        lo = jnp.maximum(t - left, 0)
        pg = prefix[:, :, g]
        win_sum = jnp.take(pg, hi, axis=1) - jnp.take(pg, lo, axis=1)
        cnt = (hi - lo).astype(jnp.float32)[None, :, None]
        outs.append(win_sum / cnt - af[:, :, g])
    m = jnp.stack(outs, axis=2).astype(a.dtype)
    y = jnp.einsum('bsgc,gcd->bsgd', m, pool_w).reshape(B, S, POOL_WIDTH)
    return y * pool_scale

def fourier_mixer(f, fourier_w):
    B, S, _ = f.shape
    f4 = f.reshape(B, S, N_FOURIER_GROUPS, FOURIER_GROUP_DIM).astype(jnp.float32)
    y = jnp.real(jnp.fft.fft2(f4, axes=(1, 3), norm='ortho'))
    y = y.astype(f.dtype).reshape(B, S, FOURIER_WIDTH)
    return y @ fourier_w

def diff_attention(q, k, v, lam, lam_init, head_norm):
    B, S = q.shape[0], q.shape[1]
    n_blk = S // Q_BLOCK
    scale = ATTN_HEAD_DIM ** -0.5
    slopes = alibi_slopes(ATTN_HEADS)
    kpos = jnp.arange(S, dtype=jnp.float32)
    qb = q.reshape(B, n_blk, Q_BLOCK, ATTN_HEADS, 2, ATTN_HEAD_DIM).transpose(1, 0, 2, 3, 4, 5)

    def one_block(args):
        q_blk, i = args
        qpos = (i * Q_BLOCK + jnp.arange(Q_BLOCK)).astype(jnp.float32)
        bias = -slopes[:, None, None] * jnp.abs(qpos[:, None] - kpos[None, :])
        s = jnp.einsum('bqhjd,bkhjd->bhjqk', q_blk, k).astype(jnp.float32) * scale + bias[None, :, None]
        p = jax.nn.softmax(s, axis=-1)
        attn = p[:, :, 0] - lam.astype(jnp.float32) * p[:, :, 1]
        return jnp.einsum('bhqk,bkhe->bqhe', attn.astype(v.dtype), v)

    o = lax.map(one_block, (qb, jnp.arange(n_blk)))
    o = o.transpose(1, 0, 2, 3, 4).reshape(B, S, ATTN_HEADS, ATTN_V_DIM)
    o = rmsnorm(o, head_norm.reshape(ATTN_HEADS, ATTN_V_DIM)) * (1.0 - lam_init)
    return o.reshape(B, S, ATTN_WIDTH)

def first_inputs(seed: int = 0) -> dict:
    key = jax.random.key(seed)
    ks = jax.random.split(key, 24)
    f32 = jnp.float32

    def nrm(k, shape, fan_in):
        return jax.random.normal(k, shape, f32) * (fan_in ** -0.5)

    def gain(k, shape):
        return 1.0 + 0.05 * jax.random.normal(k, shape, f32)

    return {
        "x": jax.random.normal(ks[0], (BATCH, SEQ, D_MODEL), f32),
        "ffn1_norm": gain(ks[1], (DEPTH, D_MODEL)),
        "ffn1_w_gate": nrm(ks[2], (DEPTH, D_MODEL, D_FF), D_MODEL),
        "ffn1_w_up": nrm(ks[3], (DEPTH, D_MODEL, D_FF), D_MODEL),
        "ffn1_w_down": nrm(ks[4], (DEPTH, D_FF, D_MODEL), D_FF),
        "mix_norm": gain(ks[5], (DEPTH, D_MODEL)),
        "w_in": nrm(ks[6], (DEPTH, D_MODEL, IN_COLS), D_MODEL),
        "pool_w": nrm(ks[7], (DEPTH, N_POOL_GROUPS, POOL_GROUP_DIM, POOL_GROUP_DIM), POOL_GROUP_DIM),
        "pool_scale": gain(ks[8], (DEPTH, POOL_WIDTH)),
        "fourier_w": nrm(ks[9], (DEPTH, FOURIER_WIDTH, FOURIER_WIDTH), FOURIER_WIDTH),
        "lam_q1": 0.1 * jax.random.normal(ks[10], (DEPTH, ATTN_HEAD_DIM), f32),
        "lam_k1": 0.1 * jax.random.normal(ks[11], (DEPTH, ATTN_HEAD_DIM), f32),
        "lam_q2": 0.1 * jax.random.normal(ks[12], (DEPTH, ATTN_HEAD_DIM), f32),
        "lam_k2": 0.1 * jax.random.normal(ks[13], (DEPTH, ATTN_HEAD_DIM), f32),
        "attn_head_norm": gain(ks[14], (DEPTH, ATTN_WIDTH)),
        "w_out": nrm(ks[15], (DEPTH, D_MODEL, D_MODEL), D_MODEL),
        "ffn2_norm": gain(ks[16], (DEPTH, D_MODEL)),
        "ffn2_w_gate": nrm(ks[17], (DEPTH, D_MODEL, D_FF), D_MODEL),
        "ffn2_w_up": nrm(ks[18], (DEPTH, D_MODEL, D_FF), D_MODEL),
        "ffn2_w_down": nrm(ks[19], (DEPTH, D_FF, D_MODEL), D_FF),
        "final_norm": gain(ks[20], (D_MODEL,)),
    }

def first_block(x, ffn1_norm, ffn1_w_gate, ffn1_w_up, ffn1_w_down, mix_norm, w_in, pool_w, pool_scale,
              fourier_w, lam_q1, lam_k1, lam_q2, lam_k2, attn_head_norm, w_out,
              ffn2_norm, ffn2_w_gate, ffn2_w_up, ffn2_w_down, final_norm):
    B, S, _ = x.shape
    c0 = POOL_WIDTH
    c1 = c0 + FOURIER_WIDTH
    c2 = c1 + ATTN_WIDTH
    c3 = c2 + ATTN_WIDTH
    for l in range(DEPTH):
        h = rmsnorm(x, ffn1_norm[l])
        x = x + 0.5 * swiglu(h, ffn1_w_gate[l], ffn1_w_up[l], ffn1_w_down[l])

        h = rmsnorm(x, mix_norm[l])
        p = h @ w_in[l]
        a = p[..., :c0]
        f = p[..., c0:c1]
        q = p[..., c1:c2].reshape(B, S, ATTN_HEADS, 2, ATTN_HEAD_DIM)
        k = p[..., c2:c3].reshape(B, S, ATTN_HEADS, 2, ATTN_HEAD_DIM)
        v = p[..., c3:].reshape(B, S, ATTN_HEADS, ATTN_V_DIM)

        lam_init = lambda_init_fn(l)
        lam = (jnp.exp(jnp.sum(lam_q1[l].astype(jnp.float32) * lam_k1[l].astype(jnp.float32)))
               - jnp.exp(jnp.sum(lam_q2[l].astype(jnp.float32) * lam_k2[l].astype(jnp.float32)))
               + lam_init)

        y_pool = pool_mixer(a, pool_w[l], pool_scale[l])
        y_four = fourier_mixer(f, fourier_w[l])
        y_attn = diff_attention(q, k, v, lam, lam_init, attn_head_norm[l]).astype(x.dtype)
        y = jnp.concatenate([y_pool, y_four, y_attn], axis=-1) @ w_out[l]
        x = x + y

        h = rmsnorm(x, ffn2_norm[l])
        x = x + 0.5 * swiglu(h, ffn2_w_gate[l], ffn2_w_up[l], ffn2_w_down[l])
    return rmsnorm(x, final_norm)


HEAD_DIM = 64
N_HEADS_MOBA = 6
N_HEADS_DIL = 6
N_HEADS_MEM = 4
D_MOBA = N_HEADS_MOBA * HEAD_DIM
D_DIL = N_HEADS_DIL * HEAD_DIM
D_MEM = N_HEADS_MEM * HEAD_DIM
D_MIX = D_MOBA + D_DIL + D_MEM
D_IN = 4 * D_MOBA + 4 * D_DIL + 2 * D_MEM
N_MEM = 256
MOBA_BLOCK = 256
MOBA_TOPK = 3
MOBA_Q_CHUNK = 32
DIL_PATTERNS = ((128, 1), (512, 4), (2048, 16))
ROPE_THETA = 10000.0
EPS = 1e-6


def rms_norm(x, g):
    xf = x.astype(jnp.float32)
    y = xf * lax.rsqrt(jnp.mean(xf * xf, axis=-1, keepdims=True) + EPS)
    return (y * g.astype(jnp.float32)).astype(x.dtype)

def rope(x):
    T = x.shape[2]
    half = HEAD_DIM // 2
    inv = ROPE_THETA ** (-jnp.arange(half, dtype=jnp.float32) / half)
    ang = jnp.arange(T, dtype=jnp.float32)[:, None] * inv[None, :]
    cos, sin = jnp.cos(ang), jnp.sin(ang)
    x1 = x[..., :half].astype(jnp.float32)
    x2 = x[..., half:].astype(jnp.float32)
    out = jnp.concatenate([x1 * cos - x2 * sin, x2 * cos + x1 * sin], axis=-1)
    return out.astype(x.dtype)

def to_heads(t, n):
    B, T, _ = t.shape
    return t.reshape(B, T, n, HEAD_DIM).transpose(0, 2, 1, 3)

def from_heads(t):
    B, H, T, dh = t.shape
    return t.transpose(0, 2, 1, 3).reshape(B, T, H * dh)

def moba_attention(q, k, v):
    B, H, T, dh = q.shape
    nb = -(-T // MOBA_BLOCK)
    Tp = nb * MOBA_BLOCK
    pad = ((0, 0), (0, 0), (0, Tp - T), (0, 0))
    q, k, v = jnp.pad(q, pad), jnp.pad(k, pad), jnp.pad(v, pad)
    kb = k.reshape(B, H, nb, MOBA_BLOCK, dh)
    vb = v.reshape(B, H, nb, MOBA_BLOCK, dh)
    k_mean = jnp.mean(kb.astype(jnp.float32), axis=3)
    topk = min(MOBA_TOPK, nb - 1)
    n_chunks = Tp // MOBA_Q_CHUNK
    q_chunks = q.reshape(B, H, n_chunks, MOBA_Q_CHUNK, dh).transpose(2, 0, 1, 3, 4)
    b_ix = jnp.arange(B)[:, None, None, None]
    h_ix = jnp.arange(H)[None, :, None, None]
    scale = dh ** -0.5

    def one_chunk(args):
        ci, qc = args
        start = ci * MOBA_Q_CHUNK
        c = start // MOBA_BLOCK
        q_pos = start + jnp.arange(MOBA_Q_CHUNK)
        k_pos = c * MOBA_BLOCK + jnp.arange(MOBA_BLOCK)
        own_k = lax.dynamic_index_in_dim(kb, c, axis=2, keepdims=False)
        own_v = lax.dynamic_index_in_dim(vb, c, axis=2, keepdims=False)
        s_own = jnp.einsum('bhqd,bhkd->bhqk', qc, own_k).astype(jnp.float32) * scale
        s_own = jnp.where(k_pos[None, :] <= q_pos[:, None], s_own, -jnp.inf)
        if topk == 0:
            p = jax.nn.softmax(s_own, axis=-1).astype(vb.dtype)
            return jnp.einsum('bhqk,bhkd->bhqd', p, own_v)
        gate = jnp.einsum('bhqd,bhnd->bhqn', qc.astype(jnp.float32), k_mean)
        gate = jnp.where(jnp.arange(nb) < c, gate, -jnp.inf)
        _, idx = lax.top_k(gate, topk)
        valid = idx < c
        sel_k = kb[b_ix, h_ix, idx]
        sel_v = vb[b_ix, h_ix, idx]
        s_sel = jnp.einsum('bhqd,bhqnkd->bhqnk', qc, sel_k).astype(jnp.float32) * scale
        s_sel = jnp.where(valid[..., None], s_sel, -jnp.inf)
        s_sel = s_sel.reshape(B, H, MOBA_Q_CHUNK, topk * MOBA_BLOCK)
        p = jax.nn.softmax(jnp.concatenate([s_own, s_sel], axis=-1), axis=-1).astype(vb.dtype)
        p_own = p[..., :MOBA_BLOCK]
        p_sel = p[..., MOBA_BLOCK:].reshape(B, H, MOBA_Q_CHUNK, topk, MOBA_BLOCK)
        return (jnp.einsum('bhqk,bhkd->bhqd', p_own, own_v)
                + jnp.einsum('bhqnk,bhqnkd->bhqd', p_sel, sel_v))

    out = lax.map(one_chunk, (jnp.arange(n_chunks, dtype=jnp.int32), q_chunks))
    return out.transpose(1, 2, 0, 3, 4).reshape(B, H, Tp, dh)[:, :, :T]

def dilated_attention(q, k, v):
    B, H, T, dh = q.shape
    scale = dh ** -0.5
    outs, lses = [], []
    for window, dil in DIL_PATTERNS:
        W = window // dil
        n = -(-T // (W * dil))
        L = n * W * dil
        pad = ((0, 0), (0, 0), (0, L - T), (0, 0))

        def split(t):
            return jnp.pad(t, pad).reshape(B, H, n, W, dil, dh).transpose(0, 1, 4, 2, 3, 5)

        qs, ks, vs = split(q), split(k), split(v)
        prev = ((0, 0), (0, 0), (0, 0), (1, 0), (0, 0), (0, 0))
        k_cat = jnp.concatenate([jnp.pad(ks, prev)[:, :, :, :-1], ks], axis=4)
        v_cat = jnp.concatenate([jnp.pad(vs, prev)[:, :, :, :-1], vs], axis=4)
        s = jnp.einsum('bhrnqd,bhrnkd->bhrnqk', qs, k_cat).astype(jnp.float32) * scale
        i = jnp.arange(W)[:, None]
        j = jnp.arange(2 * W)[None, :]
        band = (j >= i) & (j <= i + W)
        first = (jnp.arange(n)[:, None, None] > 0) | (j[None] >= W)
        s = jnp.where(band[None] & first, s, -jnp.inf)
        lse = jax.nn.logsumexp(s, axis=-1)
        p = jnp.exp(s - lse[..., None]).astype(v.dtype)
        o = jnp.einsum('bhrnqk,bhrnkd->bhrnqd', p, v_cat)
        outs.append(o.transpose(0, 1, 3, 4, 2, 5).reshape(B, H, L, dh)[:, :, :T])
        lses.append(lse.transpose(0, 1, 3, 4, 2).reshape(B, H, L)[:, :, :T])
    w = jax.nn.softmax(jnp.stack(lses, axis=0), axis=0)
    o_all = jnp.stack(outs, axis=0).astype(jnp.float32)
    return jnp.einsum('pbht,pbhtd->bhtd', w, o_all).astype(q.dtype)

def memory_attention(q, k, v):
    s = jnp.einsum('bhqd,bhkd->bhqk', q, k).astype(jnp.float32) * (HEAD_DIM ** -0.5)
    p = jax.nn.softmax(s, axis=-1).astype(v.dtype)
    return jnp.einsum('bhqk,bhkd->bhqd', p, v)

def hybrid_layer(x, mem, norm_g, w_in, w_out, mem_norm_g, w_mem_kv, qk_g):
    h = rms_norm(x, norm_g)
    proj = jnp.einsum('btd,de->bte', h, w_in)
    sizes = [D_MOBA] * 4 + [D_DIL] * 4 + [D_MEM] * 2
    cuts = [int(c) for c in np.cumsum(sizes)[:-1]]
    a_q, a_k, a_v, a_g, b_q, b_k, b_v, b_g, m_q, m_g = jnp.split(proj, cuts, axis=-1)

    qa = rope(rms_norm(to_heads(a_q, N_HEADS_MOBA), qk_g[0]))
    ka = rope(rms_norm(to_heads(a_k, N_HEADS_MOBA), qk_g[1]))
    oa = from_heads(moba_attention(qa, ka, to_heads(a_v, N_HEADS_MOBA)))

    qb = rope(rms_norm(to_heads(b_q, N_HEADS_DIL), qk_g[2]))
    kb = rope(rms_norm(to_heads(b_k, N_HEADS_DIL), qk_g[3]))
    ob = from_heads(dilated_attention(qb, kb, to_heads(b_v, N_HEADS_DIL)))

    mkv = jnp.einsum('bmd,de->bme', rms_norm(mem, mem_norm_g), w_mem_kv)
    m_k, m_v = jnp.split(mkv, 2, axis=-1)
    qm = rms_norm(to_heads(m_q, N_HEADS_MEM), qk_g[4])
    km = rms_norm(to_heads(m_k, N_HEADS_MEM), qk_g[5])
    om = from_heads(memory_attention(qm, km, to_heads(m_v, N_HEADS_MEM)))

    y = jnp.concatenate([oa * jax.nn.silu(a_g), ob * jax.nn.silu(b_g), om * jax.nn.silu(m_g)], axis=-1)
    return x + jnp.einsum('bte,ed->btd', y, w_out)

def second_inputs(seed: int = 0) -> dict:
    key = jax.random.key(seed)
    ks = jax.random.split(key, 10)
    f32 = jnp.float32
    x = jax.random.normal(ks[0], (BATCH, SEQ, D_MODEL), f32)
    mem = jax.random.normal(ks[1], (BATCH, N_MEM, D_MODEL), f32)
    norm_g = 1.0 + 0.02 * jax.random.normal(ks[2], (DEPTH, D_MODEL), f32)
    w_in = jax.random.normal(ks[3], (DEPTH, D_MODEL, D_IN), f32) * D_MODEL ** -0.5
    w_out = jax.random.normal(ks[4], (DEPTH, D_MIX, D_MODEL), f32) * (D_MIX ** -0.5) / math.sqrt(2 * DEPTH)
    mem_norm_g = 1.0 + 0.02 * jax.random.normal(ks[5], (DEPTH, D_MODEL), f32)
    w_mem_kv = jax.random.normal(ks[6], (DEPTH, D_MODEL, 2 * D_MEM), f32) * D_MODEL ** -0.5
    qk_g = 1.0 + 0.02 * jax.random.normal(ks[7], (DEPTH, 6, HEAD_DIM), f32)
    return {"x": x, "mem": mem, "norm_g": norm_g, "w_in": w_in, "w_out": w_out,
            "mem_norm_g": mem_norm_g, "w_mem_kv": w_mem_kv, "qk_g": qk_g}

def second_block(x, mem, norm_g, w_in, w_out, mem_norm_g, w_mem_kv, qk_g):
    for layer in range(DEPTH):
        x = hybrid_layer(x, mem, norm_g[layer], w_in[layer], w_out[layer],
                         mem_norm_g[layer], w_mem_kv[layer], qk_g[layer])
    return x


def setup_inputs(seed=0):
    out = dict(first_inputs(seed))
    for name, value in second_inputs(seed + 1).items():
        if name != "x":
            out[name + "_2"] = value
    return out


def reference(
    x, ffn1_norm, ffn1_w_gate, ffn1_w_up, ffn1_w_down, mix_norm, w_in, pool_w, pool_scale,
    fourier_w, lam_q1, lam_k1, lam_q2, lam_k2, attn_head_norm, w_out, ffn2_norm, ffn2_w_gate,
    ffn2_w_up, ffn2_w_down, final_norm, mem_2, norm_g_2, w_in_2, w_out_2, mem_norm_g_2,
    w_mem_kv_2, qk_g_2,
):
    x = first_block(
        x, ffn1_norm, ffn1_w_gate, ffn1_w_up, ffn1_w_down, mix_norm, w_in, pool_w, pool_scale,
        fourier_w, lam_q1, lam_k1, lam_q2, lam_k2, attn_head_norm, w_out, ffn2_norm,
        ffn2_w_gate, ffn2_w_up, ffn2_w_down, final_norm,
    )
    return second_block(
        x, mem_2, norm_g_2, w_in_2, w_out_2, mem_norm_g_2, w_mem_kv_2, qk_g_2,
    )


_drawn_inputs = setup_inputs


def setup_inputs(seed=0):
    import zlib

    import numpy as np

    out = dict(_drawn_inputs(seed))
    spreads = {}
    factors = {'mem_2': 2.718, 'norm_g_2': 8.0, 'mem_norm_g_2': 8.0, 'qk_g_2': 8.0}
    for name, (base, spread) in spreads.items():
        noise = np.random.default_rng([zlib.crc32(name.encode()), seed]).standard_normal(out[name].shape)
        drawn = base * np.exp(spread * noise) if base else spread * noise
        out[name] = __import__('jax').numpy.asarray(drawn.astype(out[name].dtype))
    for name, factor in factors.items():
        out[name] = (out[name] * factor).astype(out[name].dtype)
    return out
```

```python
from contextlib import ExitStack
import math

import numpy as np
import concourse.bass as bass
from concourse import mybir

F32 = mybir.dt.float32
F32R = mybir.dt.float32r
ALU = mybir.AluOpType
ACT = mybir.ActivationFunctionType
AX_X = mybir.AxisListType.X

P = 128
D = 1024
T = 512
KB = D // P
TB = T // P
LAYERS = 2
FF = 2816
FB = FF // P
PANEL = 2048
EPS = 1e-6
MASKED = -1e30

UP_PANELS = FB
DOWN_PANELS = FB // 2
FFN_PANELS = UP_PANELS + DOWN_PANELS
MIX_PANELS = 12
OUT_PANELS = 4
LAYER1_PANELS = 2 * FFN_PANELS + MIX_PANELS + OUT_PANELS
GROUPS = 8
LAYER2_PANELS = 2 * GROUPS + OUT_PANELS
BASE2 = LAYERS * LAYER1_PANELS
ALL_PANELS = BASE2 + LAYERS * LAYER2_PANELS
SPARE_PANELS = 2

OUT_ORDER = [4, 5, 6, 7, 0, 1, 2, 3]
SUM_BANK = 4

HEADS1 = 4
UNITS1 = HEADS1 * TB
SLOPES = [2.0 ** (-8.0 * (i + 1) / HEADS1) for i in range(HEADS1)]
PAD = 8
WINDOWS = (2, 4, 8, 16)
TOE = 2 * T - P

G_FFN1, G_MIX, G_FFN2, G_POOL, G_HEAD, G_KEEP, G_LAM, NV1 = 0, 8, 16, 24, 26, 30, 31, 32
G_NORM, G_MEM, G_QK, NV2 = 0, 8, 16, 22
C_ID, C_MEAN, C_HALF, C_HEAD, C_ROT, C_ONE, C_EPS = range(7)
NC = 6 * P + 1

MIX_UNITS = (
    [("a", c, c, 0 if c else None) for c in range(2)]
    + [("f", c, 2 + c, 1 if c else None) for c in range(2)]
    + [("q", c, c, 2 + c // 2 if c % 2 else None) for c in range(4)]
    + [("k", c, c, 4 + c // 2 if c % 2 else None) for c in range(4)]
    + [("v", 4 * h + t, 4 * h + t, 6 + h if t == 3 else None) for h in range(2) for t in range(4)]
    + [("fc", t, t, 8 if t == 3 else None) for t in range(4)]
    + [("yf", c, 4 + c, 10 if c else None) for c in range(2)]
    + [("four", c, 6 + c, None) for c in range(2)]
    + [("pool", c, c, 11 if c else None) for c in range(2)]
)
NU = len(MIX_UNITS)
READY_BEFORE = [sum(u[3] is None for u in MIX_UNITS[:i]) for i in range(NU + 1)]
READY1 = READY_BEFORE[NU]
UNIT_AT = {u[:2]: i for i, u in enumerate(MIX_UNITS)}

UNITS2 = 64


def shape_constants():
    i = np.arange(P)
    consts = np.zeros((P, NC), np.float64)
    consts[:, C_ID * P:(C_ID + 1) * P] = np.eye(P)
    consts[:, C_MEAN * P:(C_MEAN + 1) * P] = 1.0 / D
    consts[:, C_HALF * P:(C_HALF + 1) * P] = (i[:, None] // 64 == i[None] // 64) / 64.0
    consts[:, C_HEAD * P:(C_HEAD + 1) * P] = 1.0 / P
    rot = np.zeros((P, P))
    for m in range(P):
        if m % 64 < 32:
            rot[m + 32, m] = -1.0
        else:
            rot[m - 32, m] = 1.0
    consts[:, C_ROT * P:(C_ROT + 1) * P] = rot
    consts[:, C_ONE * P:(C_ONE + 1) * P] = 1.0
    consts[:, NC - 1] = EPS
    lag = i[:, None] + (T - P) - np.arange(TOE)[None]
    dist = np.abs(lag)
    causal = np.where(lag >= 0, 0.0, MASKED)
    count = ((lag <= 128).astype(int) + (lag % 4 == 0) + (lag % 16 == 0)) * (lag >= 0)
    dilated = np.where(count > 0, np.log(np.maximum(count, 1)), MASKED)
    t = np.arange(T)
    recip = np.zeros((P, 2, T))
    for g, w in enumerate(WINDOWS):
        cnt = np.minimum(t + w - 1 - w // 2 + 1, T) - np.maximum(t - w // 2, 0)
        recip[64 * (g % 2):64 * (g % 2) + 64, g // 2] = 1.0 / cnt
    inv = (10000.0 ** (-np.arange(32, dtype=np.float32) / np.float32(32))).astype(np.float32)
    ang = (t.astype(np.float32)[:, None] * inv[None]).astype(np.float32).astype(np.float64)
    rope = np.stack([np.cos(ang).T[i % 32], np.sin(ang).T[i % 32]], 1)
    c64 = 2 * np.pi * np.outer(np.arange(64), np.arange(64)) / 64
    chan = np.zeros((P, 2, P))
    for g in range(2):
        s = slice(64 * g, 64 * g + 64)
        chan[s, 0, s] = np.cos(c64) / 8
        chan[s, 1, s] = np.sin(c64) / 8
    cs = 2 * np.pi * (np.outer(t, t) % T) / T
    seq = np.stack([np.cos(cs), -np.sin(cs)]) / math.sqrt(T)
    seq = seq.reshape(2, TB, P, T).transpose(0, 2, 1, 3).reshape(2, P, PANEL)
    f = np.float32
    return {
        "consts": consts.astype(f), "dist": dist.astype(f),
        "masks": np.stack([causal, dilated], 1).reshape(P, 2 * TOE).astype(f),
        "recip": recip.reshape(P, 2 * T).astype(f), "rope": rope.reshape(P, 2 * T).astype(f),
        "chan": chan.reshape(P, 2 * P).astype(f), "seq": seq.astype(f),
    }


def build(nc, x, mem, stream, vecs1, vecs2, final_g, lamv, consts, dist, masks, recip, rope, out):
    ctx = ExitStack()
    with ctx:
        def sb(name, shape, dt=F32, stack=ctx):
            return stack.enter_context(nc.sbuf_tensor(name, shape, dt))

        def sem(name):
            return ctx.enter_context(nc.semaphore(name))

        x_sb = sb("x_sb", [P, KB, T])
        h_hi = sb("h_hi", [P, KB, T], F32R)
        h_lo = sb("h_lo", [P, KB, T], F32R)
        raw = sb("raw", [P, 2, PANEL])
        w_hi = sb("w_hi", [P, 2, PANEL], F32R)
        w_lo = sb("w_lo", [P, 2, PANEL], F32R)
        cst = sb("cst", [P, NC])
        v1_all = sb("v1_all", [P, LAYERS * NV1])
        v1 = sb("v1", [P, NV1])
        v2_all = sb("v2_all", [P, LAYERS * NV2])
        v2 = sb("v2", [P, NV2])
        fin_g = sb("fin_g", [P, KB])
        nlam_all = sb("nlam_all", [P, LAYERS])
        nlam = sb("nlam", [P, 1])
        sq = sb("sq", [P, 2, T])
        ms = sb("ms", [P, T])
        guess = sb("guess", [P, T])
        guess2 = sb("guess2", [P, T])
        newt = sb("newt", [P, T])
        rstd = sb("rstd", [P, T])
        hraw = sb("hraw", [P, 2, T])
        mx = sb("mx", [P, 2, 2])
        nmx = sb("nmx", [P, 2, 2])
        ssum = sb("ssum", [P, 2, 2])
        rsum = sb("rsum", [P, 2, 2])
        tick = sb("tick", [P, 1])
        eps = cst[:, NC - 1:NC]

        def const(i):
            return cst[:, i * P:(i + 1) * P]

        ffn = ExitStack()
        hid_hi = sb("hid_hi", [P, FB, T], F32R, ffn)
        hid_lo = sb("hid_lo", [P, FB, T], F32R, ffn)
        ffn.close()
        mix = ExitStack()
        q_hi = sb("q_hi", [P, HEADS1, T], F32R, mix)
        q_lo = sb("q_lo", [P, HEADS1, T], F32R, mix)
        k_hi = sb("k_hi", [P, HEADS1, T], F32R, mix)
        k_lo = sb("k_lo", [P, HEADS1, T], F32R, mix)
        v_hi = sb("v_hi", [P, TB, 512], F32R, mix)
        v_lo = sb("v_lo", [P, TB, 512], F32R, mix)
        bias = sb("bias", [P, 2, TOE], F32, mix)
        dist_sb = sb("dist_sb", [P, TOE], F32, mix)
        four = ExitStack()
        rec_sb = sb("rec_sb", [P, 2, T], F32, four)
        f_hi = sb("f_hi", [P, 2, T], F32R, four)
        f_lo = sb("f_lo", [P, 2, T], F32R, four)
        apad = sb("apad", [P, 2, T + 2 * PAD], F32, four)
        win = sb("win", [P, 2, T + 2 * PAD], F32, four)
        m_hi = sb("m_hi", [P, 2, T], F32R, four)
        m_lo = sb("m_lo", [P, 2, T], F32R, four)
        four.close()
        prob1 = sb("prob1", [P, 2, 2, T], F32, mix)
        att1 = sb("att1", [P, 2, T], F32, mix)
        at_hi = sb("at_hi", [P, TB, T], F32R, mix)
        at_lo = sb("at_lo", [P, TB, T], F32R, mix)
        fc_hi, fc_lo = h_hi[:, 4:8, :], h_lo[:, 4:8, :]
        mix.close()
        two = ExitStack()
        y = sb("y", [P, KB, T], F32, two)
        memn = sb("memn", [P, KB, 256], F32, two)
        qk_hi = sb("qk_hi", [P, 2, T], F32R, two)
        qk_lo = sb("qk_lo", [P, 2, T], F32R, two)
        km_hi = sb("km_hi", [P, 2, 256], F32R, two)
        km_lo = sb("km_lo", [P, 2, 256], F32R, two)
        vp_hi = sb("vp_hi", [P, TB, 2, P], F32R, two)
        vp_lo = sb("vp_lo", [P, TB, 2, P], F32R, two)
        vm_hi = sb("vm_hi", [P, 2, 2, 2, P], F32R, two)
        vm_lo = sb("vm_lo", [P, 2, 2, 2, P], F32R, two)
        pt_hi = sb("pt_hi", [P, TB, T], F32R, two)
        pt_lo = sb("pt_lo", [P, TB, T], F32R, two)
        xs = sb("xs", [P, 2, T], F32, two)
        mask = sb("mask", [P, 2, T], F32, two)
        prob2 = sb("prob2", [P, 2, T], F32, two)
        att2 = sb("att2", [P, 2, T], F32, two)
        rope_sb = sb("rope_sb", [P, 2, T], F32, two)
        two.close()
        mh_hi = pt_hi[:].rearrange("p a (b n) -> p (a b) n", b=2)
        mh_lo = pt_lo[:].rearrange("p a (b n) -> p (a b) n", b=2)

        ps = ctx.enter_context(nc.psum_tensor("ps", [P, 8, 512], F32))

        in_x = sem("in_x")
        in_small = sem("in_small")
        in_mix = sem("in_mix")
        in_two = sem("in_two")
        raw_ready = [sem("raw_ready0"), sem("raw_ready1")]
        hi_split = sem("hi_split")
        lo_split = sem("lo_split")
        panel_done = sem("panel_done")
        x_ready = sem("x_ready")
        square_ready = sem("square_ready")
        sum_step = sem("sum_step")
        guess_ready = sem("guess_ready")
        h_ready = sem("h_ready")
        silu_ready = sem("silu_ready")
        hid_ready = sem("hid_ready")
        out_ready = sem("out_ready")
        lam_mm = sem("lam_mm")
        lam_in = sem("lam_in")
        lam_exp = sem("lam_exp")
        lam_done = sem("lam_done")
        unit_ready = sem("unit_ready")
        unit_hi = sem("unit_hi")
        unit_lo = sem("unit_lo")
        pooled = sem("pooled")
        bias_ready = sem("bias_ready")
        s_scores = sem("s_scores")
        s_max = sem("s_max")
        s_exp = sem("s_exp")
        s_att = sem("s_att")
        s_tr = sem("s_tr")
        s_thi = sem("s_thi")
        s_tlo = sem("s_tlo")
        s_o = sem("s_o")
        s_osq = sem("s_osq")
        s_osum = sem("s_osum")
        s_oguess = sem("s_oguess")
        s_y = sem("s_y")
        mem_sq = sem("mem_sq")
        mem_sum = sem("mem_sum")
        mem_guess = sem("mem_guess")
        mem_normed = sem("mem_normed")
        memh_ready = sem("memh_ready")
        chunk_ready = sem("chunk_ready")
        hn_in = sem("hn_in")
        hn_mm = sem("hn_mm")
        hn_guess = sem("hn_guess")
        hn_out = sem("hn_out")
        v_in = sem("v_in")
        v_tr = sem("v_tr")
        v_thi = sem("v_thi")
        v_tlo = sem("v_tlo")
        g_in = sem("g_in")
        t_scores, t_max, t_exp, t_att, t_tr, t_thi, t_tlo = (
            sem(f"t_{n}") for n in ("scores", "max", "exp", "att", "tr", "thi", "tlo"))
        t_o = sem("t_o")
        t_y = sem("t_y")
        y_ready = sem("y_ready")
        stored = sem("stored")

        block = ctx.enter_context(nc.Block())

        def slot(ap, p):
            return ap[:, p % 2, :]

        units1 = [(h, b) for h in range(HEADS1) for b in range(TB)]

        @block.sync
        def _(sp):
            for s in range(2):
                sp.dma_start(raw[:, s, :], stream[s]).then_inc(raw_ready[s], 16)
            with sp.Fori(1, (ALL_PANELS + SPARE_PANELS) // 2) as i:
                for s in range(2):
                    sp.wait_ge(lo_split, 2 * i + s - 1)
                    sp.dma_start(raw[:, bass.ds(s, 1), :],
                                 stream[bass.ds(2 * i + s, 1)].rearrange("a p n -> p a n")
                                 ).then_inc(raw_ready[s], 16)
            for i in range(KB):
                sp.wait_ge(x_ready, 8 * (3 * LAYERS + 1 + LAYERS) + OUT_ORDER.index(i) + 1)
                sp.dma_start(out[:, i, :], x_sb[:, i, :]).then_inc(stored, 16)
            sp.wait_ge(stored, 16 * KB)

        @block.gpsimd
        def _(gp):
            with gp.Fori(0, (ALL_PANELS + SPARE_PANELS) // 2) as i:
                for s in range(2):
                    gp.wait_ge(hi_split, 2 * i + s + 1)
                    gp.tensor_tensor(w_lo[:, s, :], raw[:, s, :], w_hi[:, s, :].bitcast(F32),
                                     ALU.subtract).then_inc(lo_split, 1)

        @block.tensor
        def _(pe):
            def three(dst, l_hi, l_lo, r_hi, r_lo, first, last):
                pe.matmul(dst, l_hi, r_hi, start=first, stop=False)
                pe.matmul(dst, l_hi, r_lo, start=False, stop=False)
                return pe.matmul(dst, l_lo, r_hi, start=False, stop=last)

            def sum_squares(n):
                for i in range(KB):
                    pe.wait_ge(square_ready, 8 * n + i + 1)
                    pe.matmul(ps[:, SUM_BANK, :], const(C_MEAN), sq[:, i % 2, :],
                              start=(i == 0), stop=(i == KB - 1)).then_inc(sum_step, 1)

            def panel(p):
                pe.wait_ge(lo_split, p + 1)

            def up(n, p, c, s, first=False):
                panel(p)
                w = [t[:, s, :].rearrange("p (k g n) -> p k g n", k=KB, g=2) for t in (w_hi, w_lo)]
                for k in range(KB):
                    if first:
                        pe.wait_ge(h_ready, 8 * n + k + 1)
                    for g in range(2):
                        mm = three(ps[:, 2 * (c % 2) + g, :], w[0][:, k, g, :], w[1][:, k, g, :],
                                   h_hi[:, k, :], h_lo[:, k, :], k == 0, k == KB - 1)
                mm.then_inc(panel_done, 1)

            def down(p, d, s, F, first=False, last=False):
                panel(p)
                w = [t[:, s, :].rearrange("p (f n) -> p f n", f=2) for t in (w_hi, w_lo)]
                for i, m in enumerate(OUT_ORDER):
                    if first and m == 0:
                        pe.wait_ge(hid_ready, FB * F + FB)
                    for f in range(2):
                        if isinstance(d, int):
                            r = hid_hi[:, 2 * d + f, :], hid_lo[:, 2 * d + f, :]
                        else:
                            r = [t[:, bass.ds(2 * d + f, 1), :] for t in (hid_hi, hid_lo)]
                        mm = three(ps[:, m, :], w[0][:, f, P * m:P * m + P], w[1][:, f, P * m:P * m + P],
                                   *r, first and f == 0, last and f == 1)
                    if last and i < KB - 1:
                        mm.then_inc(out_ready, 1)
                mm.then_inc(panel_done, 1)

            def feed_forward(n, F, p0, odd):
                sum_squares(n)
                for c in range(2):
                    up(n, p0 + c, c, (odd + c) % 2, first=(c == 0))
                with pe.Fori(1, FB // 2) as i:
                    for c in range(2):
                        pe.wait_ge(hid_ready, FB * F + 2 * i + c - 1)
                        up(n, p0 + 2 * i + c, c, (odd + c) % 2)
                pd = p0 + UP_PANELS
                pe.wait_ge(hid_ready, FB * F + 2)
                down(pd, 0, odd % 2, F, first=True)
                with pe.Fori(0, (DOWN_PANELS - 3) // 2) as i:
                    for e in range(2):
                        down(pd + 1 + 2 * i + e, 1 + 2 * i + e, (odd + 1 + e) % 2, F)
                for d in (DOWN_PANELS - 2, DOWN_PANELS - 1):
                    down(pd + d, d, (odd + d) % 2, F, last=(d == DOWN_PANELS - 1))

            def project_out(p0, odd, ready):
                for j in range(OUT_PANELS):
                    panel(p0 + j)
                    w = [t[:, (odd + j) % 2, :].rearrange("p (k g n) -> p k g n", k=KB, g=2) for t in (w_hi, w_lo)]
                    for g in range(2):
                        for k in range(KB):
                            if j == 0 and g == 0:
                                ready(k)
                            mm = three(ps[:, OUT_ORDER[2 * j + g], :], w[0][:, k, g, :], w[1][:, k, g, :],
                                       h_hi[:, k, :], h_lo[:, k, :], k == 0, k == KB - 1)
                        if g == 0:
                            mm.then_inc(out_ready, 1)
                    mm.then_inc(panel_done, 1)

            def mixer1(l, n, p0):
                lo0 = NU * l

                def finish(i, mm):
                    mm.then_inc(unit_ready if MIX_UNITS[i][3] is None else panel_done, 1)

                sum_squares(n)
                i = 0
                for j in range(6):
                    panel(p0 + j)
                    w = [t[:, (j + 1) % 2, :].rearrange("p (k g n) -> p k g n", k=KB, g=2) for t in (w_hi, w_lo)]
                    for g in range(2):
                        if i >= 4:
                            pe.wait_ge(unit_lo, lo0 + i - 3)
                        for k in range(KB):
                            if i == 0:
                                pe.wait_ge(h_ready, 8 * n + k + 1)
                            mm = three(ps[:, MIX_UNITS[i][2], :], w[0][:, k, g, :], w[1][:, k, g, :],
                                       h_hi[:, k, :], h_lo[:, k, :], k == 0, k == KB - 1)
                        finish(i, mm)
                        i += 1
                for j in range(6, 8):
                    panel(p0 + j)
                    w = [t[:, (j + 1) % 2, :].rearrange("p (k n) -> p k n", k=KB) for t in (w_hi, w_lo)]
                    for t in range(TB):
                        if j == 6:
                            pe.wait_ge(unit_lo, lo0 + i - 3)
                        s = slice(P * t, P * t + P)
                        for k in range(KB):
                            mm = three(ps[:, MIX_UNITS[i][2], 0:256], h_hi[:, k, s], h_lo[:, k, s],
                                       w[0][:, k, :], w[1][:, k, :], k == 0, k == KB - 1)
                        finish(i, mm)
                        i += 1
                panel(p0 + 8)
                for t in range(TB):
                    pe.wait_ge(unit_lo, lo0 + i - 7)
                    s = slice(P * t, P * t + P)
                    for c in range(2):
                        mm = three(ps[:, MIX_UNITS[i][2], 256 * c:256 * c + 256], f_hi[:, c, s], f_lo[:, c, s],
                                   w_hi[:, 1, 0:256], w_lo[:, 1, 0:256], True, True)
                    finish(i, mm)
                    i += 1
                pe.wait_ge(unit_lo, lo0 + i)
                for e in range(2):
                    panel(p0 + 9 + e)
                    w = [t[:, e, :].rearrange("p (t n) -> p t n", t=TB) for t in (w_hi, w_lo)]
                    for c in range(2):
                        s = slice(256 * c + P * e, 256 * c + P * e + P)
                        for t in range(TB):
                            mm = three(ps[:, 4 + c, :], fc_hi[:, t, s], fc_lo[:, t, s],
                                       w[0][:, t, :], w[1][:, t, :], e == 0 and t == 0, e == 1 and t == TB - 1)
                        if e == 1:
                            finish(i, mm)
                            i += 1
                    if e == 0:
                        mm.then_inc(panel_done, 1)
                panel(p0 + 11)
                pe.wait_ge(unit_lo, lo0 + i)
                for c in range(2):
                    for k in range(2):
                        s = slice(256 * k + P * c, 256 * k + P * c + P)
                        mm = three(ps[:, 6 + c, :], w_hi[:, 0, s], w_lo[:, 0, s],
                                   f_hi[:, k, :], f_lo[:, k, :], k == 0, k == 1)
                    finish(i, mm)
                    i += 1
                for c in range(2):
                    pe.wait_ge(pooled, 2 * l + c + 1)
                    s = slice(512 + P * c, 512 + P * c + P)
                    mm = three(ps[:, c, :], w_hi[:, 0, s], w_lo[:, 0, s],
                               m_hi[:, c, :], m_lo[:, c, :], True, True)
                    finish(i, mm)
                    i += 1
                pe.wait_ge(unit_lo, lo0 + NU)
                u0 = UNITS1 * l
                for s in range(UNITS1 + 4):
                    if s < UNITS1:
                        h, b = units1[s]
                        if s >= 2:
                            pe.wait_ge(s_max, u0 + s - 1)
                        for j in range(2):
                            r, c = slice(64 * j, 64 * j + 64), slice(P * b, P * b + P)
                            mm = three(ps[:, 2 * (s % 2) + j, :], q_hi[r, h, c], q_lo[r, h, c],
                                       k_hi[r, h, :], k_lo[r, h, :], True, True)
                        mm.then_inc(s_scores, 1)
                    if 1 <= s <= UNITS1:
                        u = s - 1
                        pe.wait_ge(s_att, u0 + u + 1)
                        if u >= 2:
                            pe.wait_ge(s_tlo, u0 + u - 1)
                        for kb in range(TB):
                            mm = pe.transpose(ps[:, 4 + u % 2, P * kb:P * kb + P],
                                              att1[:, u % 2, P * kb:P * kb + P], const(C_ID))
                        mm.then_inc(s_tr, 1)
                    if s >= 2 and (s - 2) % TB == TB - 1 and s - 2 < UNITS1:
                        h = (s - 2) // TB
                        pe.wait_ge(s_tlo, u0 + s - 1)
                        if h:
                            pe.wait_ge(s_y, HEADS1 * l + h)
                        for kb in range(TB):
                            c = slice(P * h, P * h + P)
                            mm = three(ps[:, 6, :], v_hi[:, kb, c], v_lo[:, kb, c],
                                       at_hi[:, kb, :], at_lo[:, kb, :], kb == 0, kb == TB - 1)
                        mm.then_inc(s_o, 1)
                    if s >= 3 and (s - 3) % TB == TB - 1 and s - 3 < UNITS1:
                        h = (s - 3) // TB
                        pe.wait_ge(s_osq, HEADS1 * l + h + 1)
                        pe.matmul(ps[:, 7, :], const(C_HEAD), sq[:, 0, :], start=True, stop=True).then_inc(s_osum, 1)
                project_out(p0 + MIX_PANELS, 1,
                            lambda k: pe.wait_ge(s_y, HEADS1 * l + k - 3) if k >= 4 else None)

            def head_norm_sums(i, j, width, rotate):
                pe.wait_ge(hn_in, i + 1)
                if rotate:
                    pe.matmul(ps[:, 4 + 2 * j, 0:width], const(C_ROT), xs[:, j, 0:width], start=True, stop=True)
                pe.matmul(ps[:, 5 + 2 * j, 0:width], const(C_HALF), sq[:, j, 0:width],
                          start=True, stop=True).then_inc(hn_mm, 1)

            def group_products(p, act_hi, act_lo, width, between):
                for e in range(2):
                    panel(p + e)
                    w = [t[:, e, :].rearrange("p (k g n) -> p k g n", k=KB, g=2) for t in (w_hi, w_lo)]
                    for g in range(2):
                        for k in range(KB):
                            mm = three(ps[:, 2 * e + g, 0:width], w[0][:, k, g, :], w[1][:, k, g, :],
                                       act_hi[:, k, :], act_lo[:, k, :], k == 0, k == KB - 1)
                        mm.then_inc(panel_done if g else chunk_ready, 1)
                        between[2 * e + g]()

            def attend(u0, units, widths, scores, outputs):
                n = len(units)
                for s in range(n + 2):
                    if s < n:
                        if s >= 2:
                            pe.wait_ge(t_max, u0 + s - 1)
                        scores(s).then_inc(t_scores, 1)
                    if 1 <= s <= n:
                        u = s - 1
                        pe.wait_ge(t_att, u0 + u + 1)
                        if u >= 2:
                            pe.wait_ge(t_tlo, u0 + u - 1)
                        for kb in range(widths[u] // P):
                            mm = pe.transpose(ps[:, 2 + u % 2, P * kb:P * kb + P],
                                              att2[:, u % 2, P * kb:P * kb + P], const(C_ID))
                        mm.then_inc(t_tr, 1)
                    if s >= 2 and (s - 2) % TB == TB - 1:
                        pe.wait_ge(t_tlo, u0 + s - 1)
                        outputs((s - 2) // TB)

            def stack2(l):
                n = 3 * LAYERS + 1 + l
                p0 = BASE2 + LAYER2_PANELS * l
                sum_squares(n)
                for k in range(KB):
                    pe.wait_ge(memh_ready, 8 * l + k + 1)
                g0 = GROUPS * l

                def v_transposes_mem():
                    pe.wait_ge(v_in, 7 * l + 1)
                    pe.wait_ge(hn_out, 2 * g0 + 1)
                    for c in range(2):
                        for tb in range(2):
                            mm = pe.transpose(ps[:, 4, 256 * tb + P * c:256 * tb + P * c + P],
                                              hraw[:, c, P * tb:P * tb + P], const(C_ID))
                    mm.then_inc(v_tr, 1)

                group_products(p0, mh_hi, mh_lo, 256, [
                    lambda: None,
                    lambda: head_norm_sums(2 * g0, 0, 256, False),
                    lambda: head_norm_sums(2 * g0 + 1, 1, 256, False),
                    v_transposes_mem])
                for branch in range(2):
                    with pe.Fori(0, 3) as j:
                        gi = 1 + 3 * branch + j
                        G = g0 + gi
                        pe.wait_ge(hn_out, 2 * G)
                        pe.wait_ge(v_tlo, 7 * l + gi)

                        def v_transposes():
                            pe.wait_ge(v_in, 7 * l + gi + 1)
                            pe.wait_ge(hn_out, 2 * G + 1)
                            for tb in range(TB):
                                mm = pe.transpose(ps[:, 4, P * tb:P * tb + P],
                                                  hraw[:, 0, P * tb:P * tb + P], const(C_ID))
                            mm.then_inc(v_tr, 1)

                        group_products(p0 + 2 * gi, h_hi, h_lo, T, [
                            lambda: None,
                            lambda: head_norm_sums(2 * G, 0, T, True),
                            lambda: head_norm_sums(2 * G + 1, 1, T, True),
                            v_transposes])
                        pe.wait_ge(hn_out, 2 * G + 2)
                        pe.wait_ge(v_tlo, 7 * l + gi + 1)
                        pe.wait_ge(g_in, 7 * l + gi)
                        u0 = UNITS2 * l + 8 * (gi - 1)
                        units = [(h, b) for h in range(2) for b in range(TB)]
                        widths = [P * (b + 1) for _, b in units]

                        def scores(u):
                            h, b = units[u]
                            r, c, w = slice(64 * h, 64 * h + 64), slice(P * b, P * b + P), slice(0, widths[u])
                            return three(ps[:, u % 2, w], qk_hi[r, 0, c], qk_lo[r, 0, c],
                                         qk_hi[r, 1, w], qk_lo[r, 1, w], True, True)

                        def outputs(h):
                            for kb in range(TB):
                                c = slice(P * kb, T)
                                mm = three(ps[:, 5, c], vp_hi[:, kb, h, :], vp_lo[:, kb, h, :],
                                           pt_hi[:, kb, c], pt_lo[:, kb, c],
                                           h == 0 and kb == 0, h == 1 and kb == TB - 1)
                            mm.then_inc(t_o, 1)

                        attend(u0, units, widths, scores, outputs)
                        pe.wait_ge(t_y, 8 * l + gi)
                gi, G = 7, g0 + 7
                group_products(p0 + 2 * gi, h_hi, h_lo, T, [
                    lambda: None,
                    lambda: head_norm_sums(2 * G, 0, T, False),
                    lambda: head_norm_sums(2 * G + 1, 1, T, False),
                    lambda: None])
                pe.wait_ge(hn_out, 2 * G + 2)
                pe.wait_ge(g_in, 7 * l + gi)
                u0 = UNITS2 * l + 48
                units = [(h, b) for h in range(4) for b in range(TB)]

                def scores_mem(u):
                    h, b = units[u]
                    r, c = slice(64 * (h % 2), 64 * (h % 2) + 64), slice(P * b, P * b + P)
                    return three(ps[:, u % 2, 0:256], qk_hi[r, h // 2, c], qk_lo[r, h // 2, c],
                                 km_hi[r, h // 2, :], km_lo[r, h // 2, :], True, True)

                def outputs_mem(h):
                    for kb in range(2):
                        mm = three(ps[:, 5 + h // 2, :], vm_hi[:, kb, h // 2, h % 2, :], vm_lo[:, kb, h // 2, h % 2, :],
                                   pt_hi[:, kb, :], pt_lo[:, kb, :],
                                   h % 2 == 0 and kb == 0, h % 2 == 1 and kb == 1)
                    mm.then_inc(t_o, 1)

                attend(u0, units, [256] * 16, scores_mem, outputs_mem)
                project_out(p0 + 2 * GROUPS, 0, lambda k: pe.wait_ge(y_ready, 8 * l + k + 1))

            pe.wait_ge(in_small, 16 * 5)
            pe.wait_ge(lam_in, 1)
            pe.matmul(ps[:, 7, 0:4], cst[0:64, C_ONE * P:C_ONE * P + P], hraw[0:64, 0, 0:4],
                      start=True, stop=True).then_inc(lam_mm, 1)
            with pe.Fori(0, LAYERS) as l:
                p0 = LAYER1_PANELS * l
                feed_forward(3 * l, 2 * l, p0, 0)
                mixer_p0 = p0 + FFN_PANELS
                mixer1(l, 3 * l + 1, mixer_p0)
                feed_forward(3 * l + 2, 2 * l + 1, mixer_p0 + MIX_PANELS + OUT_PANELS, 1)
            sum_squares(3 * LAYERS)
            for i in range(KB):
                pe.wait_ge(mem_sq, i + 1)
                pe.matmul(ps[:, 5, 0:256], const(C_MEAN), sq[:, i % 2, 0:256],
                          start=(i == 0), stop=(i == KB - 1)).then_inc(mem_sum, 1)
            with pe.Fori(0, LAYERS) as l:
                stack2(l)

        @block.scalar
        def _(act):
            def split(p, s):
                act.wait_ge(raw_ready[s], 8 * (p - s) + 16)
                act.activation(w_hi[:, s, :], raw[:, s, :], ACT.Copy).then_inc(hi_split, 1)

            def split_after(p, s):
                act.wait_ge(panel_done, p + 1)
                split(p + 2, s)

            def guesses(src, width, done):
                w = slice(0, width)
                act.activation(ms[:, w], src, ACT.Identity, bias=eps)
                act.activation(guess[:, w], src, ACT.Abs_reciprocal_sqrt, bias=eps)
                act.drain()
                act.activation(guess2[:, w], guess[:, w], ACT.Square).then_inc(done, 1)

            def norm(n):
                for i, m in enumerate(OUT_ORDER):
                    act.wait_ge(x_ready, 8 * n + i + 1)
                    if i >= 2:
                        act.wait_ge(sum_step, 8 * n + i - 1)
                    act.activation(sq[:, i % 2, :], x_sb[:, m, :], ACT.Square).then_inc(square_ready, 1)
                act.wait_ge(sum_step, 8 * n + 8)
                guesses(ps[:, SUM_BANK, :], T, guess_ready)

            def feed_forward(p0, odd):
                with act.Fori(0, FB // 2) as i:
                    for e in range(2):
                        act.wait_ge(panel_done, p0 + 2 * i + e + 1)
                        act.activation(hraw[:, e, :], ps[:, 2 * e, :], ACT.Silu).then_inc(silu_ready, 1)
                        split(p0 + 2 * i + e + 2, (odd + e) % 2)
                pd = p0 + UP_PANELS
                with act.Fori(0, (DOWN_PANELS - 1) // 2) as i:
                    for e in range(2):
                        split_after(pd + 2 * i + e, (odd + e) % 2)

            def mixer1(l, p0):
                act.dma_start(dist_sb[:], dist).then_inc(in_mix, 16)
                act.dma_start(rec_sb[:].rearrange("p a n -> p (a n)"), recip).then_inc(in_mix, 16)
                for i, (kind, c, bank, ends) in enumerate(MIX_UNITS):
                    if kind == "yf" and c == 0:
                        split_after(p0 + 9, 0)
                    if ends is None:
                        act.wait_ge(unit_ready, READY1 * l + READY_BEFORE[i + 1])
                    else:
                        act.wait_ge(panel_done, p0 + ends + 1)
                    src, scale = ps[:, bank, :], 1.0
                    if kind == "a":
                        dst = apad[:, c, PAD:PAD + T]
                    elif kind in ("f", "yf"):
                        dst = f_hi[:, c, :]
                    elif kind == "q":
                        dst, scale = q_hi[:, c, :], 0.125
                    elif kind == "k":
                        dst = k_hi[:, c, :]
                    elif kind == "v":
                        dst, src = v_hi[:, c % 4, 256 * (c // 4):256 * (c // 4) + 256], ps[:, bank, 0:256]
                    elif kind == "fc":
                        dst = fc_hi[:, c, :]
                    elif kind == "four":
                        dst = h_hi[:, 2 + c, :]
                    else:
                        dst, scale = h_hi[:, c, :], v1[:, G_POOL + c:G_POOL + c + 1]
                    act.activation(dst, src, ACT.Copy, scale=scale).then_inc(unit_hi, 1)
                    if ends is not None:
                        split(p0 + ends + 2, (ends + 1) % 2)

                def head_bias(h):
                    if h >= 2:
                        act.wait_ge(s_max, UNITS1 * l + TB * (h - 1))
                    act.activation(bias[:, h % 2, :], dist_sb[:], ACT.Copy, scale=-SLOPES[h]).then_inc(bias_ready, 1)

                u0 = UNITS1 * l
                act.wait_ge(in_mix, 32 * l + 32)
                head_bias(0)
                act.wait_ge(unit_lo, NU * l + NU)
                for s in range(UNITS1 + 5):
                    if s < UNITS1:
                        act.wait_ge(s_max, u0 + s + 1)
                        for j in range(2):
                            ins = act.activation(prob1[:, s % 2, j, :], prob1[:, s % 2, j, :], ACT.Exp,
                                                 bias=nmx[:, s % 2, j:j + 1], accum_out=ssum[:, s % 2, j:j + 1])
                        ins.then_inc(s_exp, 1)
                        if s % TB == 0 and s // TB + 1 < HEADS1:
                            head_bias(s // TB + 1)
                    if 1 <= s <= UNITS1:
                        u = s - 1
                        h, b = units1[u]
                        act.wait_ge(s_tr, u0 + u + 1)
                        if b == 0 and h:
                            act.wait_ge(s_o, HEADS1 * l + h)
                        act.activation(at_hi[:, :, P * b:P * b + P],
                                       ps[:, 4 + u % 2, :].rearrange("p (k n) -> p k n", k=TB),
                                       ACT.Copy).then_inc(s_thi, 1)
                    if s >= 3 and (s - 3) % TB == TB - 1 and s - 3 < UNITS1:
                        h = (s - 3) // TB
                        act.wait_ge(s_o, HEADS1 * l + h + 1)
                        act.activation(sq[:, 0, :], ps[:, 6, :], ACT.Square).then_inc(s_osq, 1)
                    if s >= 4 and (s - 4) % TB == TB - 1 and s - 4 < UNITS1:
                        h = (s - 4) // TB
                        act.wait_ge(s_osum, HEADS1 * l + h + 1)
                        guesses(ps[:, 7, :], T, s_oguess)
                for j in range(OUT_PANELS - 1):
                    split_after(p0 + MIX_PANELS + j, (j + 1) % 2)

            def head_norm_in(i, j, bank, width, gain):
                w = slice(0, width)
                act.activation(xs[:, j, w], ps[:, bank, w], ACT.Copy, scale=v2[:, G_QK + gain:G_QK + gain + 1])
                act.activation(sq[:, j, w], ps[:, bank, w], ACT.Square).then_inc(hn_in, 1)

            def head_norm_guess(i, j, width):
                act.wait_ge(hn_mm, i + 1)
                act.wait_ge(hn_out, i)
                guesses(ps[:, 5 + 2 * j, 0:width], width, hn_guess)

            def attend(l, u0, widths, biased, reuse):
                n = len(widths)
                for s in range(n + 1):
                    if s < n:
                        act.wait_ge(t_max, u0 + s + 1)
                        w = slice(0, widths[s])
                        src = prob2[:, s % 2, w] if biased else ps[:, s % 2, w]
                        act.activation(prob2[:, s % 2, w], src, ACT.Exp, bias=nmx[:, s % 2, 0:1],
                                       accum_out=ssum[:, s % 2, 0:1]).then_inc(t_exp, 1)
                    if s >= 1:
                        u = s - 1
                        b, kbs = u % TB, widths[u] // P
                        act.wait_ge(t_tr, u0 + u + 1)
                        if b == 0 and u:
                            act.wait_ge(t_o, reuse + u // TB)
                        act.activation(pt_hi[:, 0:kbs, P * b:P * b + P],
                                       ps[:, 2 + u % 2, 0:P * kbs].rearrange("p (k n) -> p k n", k=kbs),
                                       ACT.Copy).then_inc(t_thi, 1)

            def stack2(l):
                p0 = BASE2 + LAYER2_PANELS * l
                norm(3 * LAYERS + 1 + l)
                g0 = GROUPS * l
                c0 = 2 * g0
                o0 = 16 * l
                p = p0
                act.wait_ge(chunk_ready, c0 + 1)
                head_norm_in(2 * g0, 0, 0, 256, 5)
                act.wait_ge(panel_done, p + 1)
                head_norm_in(2 * g0 + 1, 1, 1, 256, 5)
                split(p + 2, 0)
                act.wait_ge(guess_ready, 3 * LAYERS + 2 + l)
                act.wait_ge(h_ready, 8 * (3 * LAYERS + 1 + l))
                act.wait_ge(hn_mm, 2 * g0 + 1)
                guesses(ps[:, 5, 0:256], 256, hn_guess)
                head_norm_guess(2 * g0 + 1, 1, 256)
                act.wait_ge(chunk_ready, c0 + 2)
                act.activation(hraw[:, 0, 0:256], ps[:, 2, 0:256], ACT.Copy)
                act.wait_ge(panel_done, p + 2)
                act.activation(hraw[:, 1, 0:256], ps[:, 3, 0:256], ACT.Copy).then_inc(v_in, 1)
                split(p + 3, 1)
                act.wait_ge(v_tr, 7 * l + 1)
                for h in range(2):
                    ins = act.activation(
                        vm_hi[:, :, :, h, 64 * h:64 * h + 64],
                        ps[:, 4, :].rearrange("p (t c n) -> p t c n", t=2, c=2)[:, :, :, 64 * h:64 * h + 64], ACT.Copy)
                ins.then_inc(v_thi, 1)
                for branch in range(2):
                    with act.Fori(0, 3) as j:
                        gi = 1 + 3 * branch + j
                        G = g0 + gi
                        p = p0 + 2 * gi
                        act.wait_ge(chunk_ready, c0 + 2 * gi + 1)
                        head_norm_in(2 * G, 0, 0, T, 2 * branch)
                        act.wait_ge(panel_done, p + 1)
                        head_norm_in(2 * G + 1, 1, 1, T, 2 * branch + 1)
                        split(p + 2, 0)
                        head_norm_guess(2 * G, 0, T)
                        act.wait_ge(chunk_ready, c0 + 2 * gi + 2)
                        act.activation(hraw[:, 0, :], ps[:, 2, :], ACT.Copy).then_inc(v_in, 1)
                        head_norm_guess(2 * G + 1, 1, T)
                        act.wait_ge(panel_done, p + 2)
                        act.activation(y[:, bass.ds(gi - 1, 1), :], ps[:, 3, :], ACT.Silu).then_inc(g_in, 1)
                        split(p + 3, 1)
                        act.wait_ge(v_tr, 7 * l + gi + 1)
                        for h in range(2):
                            ins = act.activation(
                                vp_hi[:, :, h, 64 * h:64 * h + 64],
                                ps[:, 4, :].rearrange("p (t n) -> p t n", t=TB)[:, :, 64 * h:64 * h + 64], ACT.Copy)
                        ins.then_inc(v_thi, 1)
                        attend(l, UNITS2 * l + 8 * (gi - 1), [P * (b + 1) for _ in range(2) for b in range(TB)],
                               True, o0 + 2 * (gi - 1))
                gi, G = 7, g0 + 7
                p = p0 + 2 * gi
                act.wait_ge(chunk_ready, c0 + 2 * gi + 1)
                head_norm_in(2 * G, 0, 0, T, 4)
                act.wait_ge(panel_done, p + 1)
                head_norm_in(2 * G + 1, 1, 1, T, 4)
                split(p + 2, 0)
                head_norm_guess(2 * G, 0, T)
                head_norm_guess(2 * G + 1, 1, T)
                act.wait_ge(chunk_ready, c0 + 2 * gi + 2)
                act.activation(y[:, 6, :], ps[:, 2, :], ACT.Silu)
                act.wait_ge(panel_done, p + 2)
                act.activation(y[:, 7, :], ps[:, 3, :], ACT.Silu).then_inc(g_in, 1)
                split(p + 3, 1)
                attend(l, UNITS2 * l + 48, [256] * 16, False, o0 + 12)
                for j in range(OUT_PANELS):
                    split_after(p0 + 2 * GROUPS + j, j % 2)

            act.dma_start(x_sb[:].rearrange("p k n -> p (k n)"), x).then_inc(in_x, 16)
            for dst, src in ((cst, consts), (v1_all, vecs1), (v2_all, vecs2), (fin_g, final_g)):
                act.dma_start(dst[:], src).then_inc(in_small, 16)
            act.dma_start(hraw[0:64, 1, 0:8], lamv).then_inc(in_small, 16)
            for s in range(2):
                split(s, s)
            act.wait_ge(lam_mm, 1)
            act.activation(hraw[:, 1, 8:12], ps[:, 7, 0:4], ACT.Exp).then_inc(lam_exp, 1)
            norm(0)
            with act.Fori(0, LAYERS) as l:
                p0 = LAYER1_PANELS * l
                feed_forward(p0, 0)
                norm(3 * l + 1)
                split_after(p0 + FFN_PANELS - 1, 0)
                mixer1(l, p0 + FFN_PANELS)
                norm(3 * l + 2)
                split_after(p0 + LAYER1_PANELS - FFN_PANELS - 1, 0)
                feed_forward(p0 + LAYER1_PANELS - FFN_PANELS, 1)
                norm(3 * l + 3)
                split_after(p0 + LAYER1_PANELS - 1, 1)
            act.dma_start(mask[:].rearrange("p a n -> p (a n)"), masks).then_inc(in_two, 16)
            act.dma_start(rope_sb[:].rearrange("p a n -> p (a n)"), rope).then_inc(in_two, 16)
            act.dma_start(memn[:].rearrange("p k n -> p (k n)"), mem).then_inc(in_two, 16)
            act.wait_ge(in_two, 48)
            for i in range(KB):
                if i >= 2:
                    act.wait_ge(mem_sum, i - 1)
                act.activation(sq[:, i % 2, 0:256], memn[:, i, :], ACT.Square).then_inc(mem_sq, 1)
            act.wait_ge(mem_sum, KB)
            act.wait_ge(x_ready, 8 * (3 * LAYERS + 2))
            guesses(ps[:, 5, 0:256], 256, mem_guess)
            act.wait_ge(mem_normed, 1)
            with act.Fori(0, LAYERS) as l:
                stack2(l)

        @block.vector
        def _(dve):
            def newton(width):
                w = slice(0, width)
                dve.tensor_tensor(newt[:, w], ms[:, w], guess2[:, w], ALU.mult)
                dve.drain()
                dve.tensor_scalar(newt[:, w], newt[:, w], -0.5, 1.5, ALU.mult, ALU.add)
                dve.drain()
                dve.tensor_tensor(rstd[:, w], newt[:, w], guess[:, w], ALU.mult)
                dve.drain()

            def remainder(dst, src, hi):
                return dve.tensor_tensor(dst, src, hi.bitcast(F32), ALU.subtract)

            def norm(n, gain):
                dve.wait_ge(guess_ready, n + 1)
                newton(T)

                wholes = [hraw[:, 0, :], hraw[:, 1, :], newt[:]]

                def whole(k):
                    dve.scalar_tensor_tensor(out=wholes[k % 3], in0=x_sb[:, k, :], scalar=gain[:, k:k + 1],
                                             in1=rstd[:], op0=ALU.mult, op1=ALU.mult)
                whole(0)
                dve.drain()
                for k in range(KB):
                    dve.tensor_copy(h_hi[:, k, :], wholes[k % 3])
                    if k + 1 < KB:
                        whole(k + 1)
                    dve.drain()
                    remainder(h_lo[:, k, :], wholes[k % 3], h_hi[:, k, :]).then_inc(h_ready, 1)

            def update(o0, last_panel, scale):
                for i, m in enumerate(OUT_ORDER):
                    at = last_panel(i)
                    if at is not None:
                        dve.wait_ge(panel_done, at)
                    else:
                        dve.wait_ge(out_ready, o0(i))
                    dve.scalar_tensor_tensor(out=x_sb[:, m, :], in0=ps[:, m, :], scalar=scale, in1=x_sb[:, m, :],
                                             op0=ALU.mult, op1=ALU.add).then_inc(x_ready, 1)

            def feed_forward(n, F, p0, gain, o0):
                norm(n, gain)
                with dve.Fori(0, FB // 2) as i:
                    for e in range(2):
                        dve.wait_ge(silu_ready, FB * F + 2 * i + e + 1)
                        c = bass.ds(2 * i + e, 1)
                        dve.tensor_tensor(sq[:, e, :], hraw[:, e, :], ps[:, 2 * e + 1, :], ALU.mult)
                        dve.drain()
                        dve.tensor_copy(hid_hi[:, c, :], sq[:, e:e + 1, :])
                        dve.drain()
                        remainder(hid_lo[:, c, :], sq[:, e:e + 1, :], hid_hi[:, c, :]).then_inc(hid_ready, 1)
                update(lambda i: o0 + i + 1, lambda i: p0 + FFN_PANELS if i == KB - 1 else None, 0.5)

            def project_out(p0, o0):
                update(lambda i: o0 + i // 2 + 1, lambda i: p0 + i // 2 + 1 if i % 2 else None, 1.0)

            def pool_block(l, c):
                n = T + 2 * PAD
                up = slice(64, P)
                a = apad[:, c, :]

                def step(dst, src, d, rows=slice(0, P), lo=0):
                    ins = dve.tensor_tensor(dst[rows, lo + d:n - d], src[rows, lo:n - 2 * d], src[rows, lo + 2 * d:n],
                                            ALU.add)
                    dve.drain()
                    return ins
                w0, w1 = win[:, 0, :], win[:, 1, :]
                dve.tensor_tensor(w0[:, 1:n], a[:, 0:n - 1], a[:, 1:n], ALU.add).then_inc(unit_lo, 1)
                dve.drain()
                if c == 0:
                    dve.tensor_tensor(w1[up, 2:n - 1], w0[up, 1:n - 2], w0[up, 3:n], ALU.add)
                else:
                    dve.tensor_tensor(w1[:, 2:n - 1], w0[:, 1:n - 2], w0[:, 3:n], ALU.add)
                    dve.drain()
                    dve.tensor_tensor(w0[:, 4:n - 3], w1[:, 2:n - 5], w1[:, 6:n - 1], ALU.add)
                    dve.drain()
                    dve.tensor_tensor(w1[up, 8:n - 7], w0[up, 4:n - 11], w0[up, 12:n - 3], ALU.add)
                dve.drain()
                t = slice(PAD, PAD + T)
                if c == 0:
                    dve.wait_ge(in_mix, 32 * l + 32)
                for rows, w in ((slice(0, 64), w0), (up, w1)):
                    dve.tensor_tensor(hraw[rows, c, :], w[rows, t], rec_sb[rows, c, :], ALU.mult)
                dve.drain()
                dve.tensor_tensor(hraw[:, c, :], hraw[:, c, :], a[:, t], ALU.subtract)
                dve.drain()
                dve.tensor_copy(m_hi[:, c, :], hraw[:, c, :])
                dve.drain()
                remainder(m_lo[:, c, :], hraw[:, c, :], m_hi[:, c, :]).then_inc(pooled, 1)

            def mixer1(l, n, p0):
                norm(n, v1[:, G_MIX:G_MIX + KB])
                dve.memset(apad[:, :, 0:PAD], 0.0)
                dve.memset(apad[:, :, PAD + T:], 0.0)
                dve.drain()
                for i, (kind, c, bank, _) in enumerate(MIX_UNITS):
                    dve.wait_ge(unit_hi, NU * l + i + 1)
                    src = ps[:, bank, :]
                    if kind == "a":
                        pool_block(l, c)
                        continue
                    if kind in ("f", "yf"):
                        ins = remainder(f_lo[:, c, :], src, f_hi[:, c, :])
                    elif kind == "q":
                        ins = dve.scalar_tensor_tensor(out=q_lo[:, c, :], in0=src, scalar=0.125,
                                                       in1=q_hi[:, c, :].bitcast(F32), op0=ALU.mult, op1=ALU.subtract)
                    elif kind == "k":
                        ins = remainder(k_lo[:, c, :], src, k_hi[:, c, :])
                    elif kind == "v":
                        s = slice(256 * (c // 4), 256 * (c // 4) + 256)
                        ins = remainder(v_lo[:, c % 4, s], ps[:, bank, 0:256], v_hi[:, c % 4, s])
                    elif kind == "fc":
                        ins = remainder(fc_lo[:, c, :], src, fc_hi[:, c, :])
                    elif kind == "four":
                        ins = remainder(h_lo[:, 2 + c, :], src, h_hi[:, 2 + c, :])
                    else:
                        ins = dve.scalar_tensor_tensor(out=h_lo[:, c, :], in0=src,
                                                       scalar=v1[:, G_POOL + c:G_POOL + c + 1],
                                                       in1=h_hi[:, c, :].bitcast(F32), op0=ALU.mult, op1=ALU.subtract)
                    ins.then_inc(unit_lo, 1)
                u0 = UNITS1 * l
                for s in range(UNITS1 + 6):
                    if s < UNITS1:
                        h, b = units1[s]
                        dve.wait_ge(s_scores, u0 + s + 1)
                        if b == 0:
                            dve.wait_ge(bias_ready, HEADS1 * l + h + 1)
                        dve.memset(tick[:], 0.0)
                        for j in range(2):
                            dve.tensor_tensor_reduce(prob1[:, s % 2, j, :], ps[:, 2 * (s % 2) + j, :],
                                                     bias[:, h % 2, T - P - P * b:2 * T - P - P * b],
                                                     1.0, -3e38, ALU.add, ALU.max, mx[:, s % 2, j:j + 1])
                        dve.drain()
                        dve.tensor_scalar(nmx[:, s % 2, :], mx[:, s % 2, :], -1.0, None, ALU.mult).then_inc(s_max, 1)
                    if 1 <= s <= UNITS1:
                        u = s - 1
                        dve.wait_ge(s_exp, u0 + u + 1)
                        dve.reciprocal(rsum[:, u % 2, :], ssum[:, u % 2, :])
                        dve.drain()
                        dve.tensor_scalar(att1[:, u % 2, :], prob1[:, u % 2, 0, :], rsum[:, u % 2, 0:1], None, ALU.mult)
                        dve.tensor_tensor(rsum[:, u % 2, 1:2], rsum[:, u % 2, 1:2], nlam[:], ALU.mult)
                        dve.drain()
                        dve.scalar_tensor_tensor(out=att1[:, u % 2, :], in0=prob1[:, u % 2, 1, :],
                                                 scalar=rsum[:, u % 2, 1:2], in1=att1[:, u % 2, :],
                                                 op0=ALU.mult, op1=ALU.add).then_inc(s_att, 1)
                    if 2 <= s <= UNITS1 + 1:
                        u = s - 2
                        q = slice(P * units1[u][1], P * units1[u][1] + P)
                        dve.wait_ge(s_thi, u0 + u + 1)
                        remainder(at_lo[:, :, q], ps[:, 4 + u % 2, :].rearrange("p (k n) -> p k n", k=TB),
                                  at_hi[:, :, q]).then_inc(s_tlo, 1)
                    if s >= 5 and (s - 5) % TB == TB - 1 and s - 5 < UNITS1:
                        h = (s - 5) // TB
                        dve.wait_ge(s_oguess, HEADS1 * l + h + 1)
                        newton(T)
                        dve.scalar_tensor_tensor(out=hraw[:, 0, :], in0=ps[:, 6, :], scalar=v1[:, G_HEAD + h:G_HEAD + h + 1],
                                                 in1=rstd[:], op0=ALU.mult, op1=ALU.mult)
                        dve.drain()
                        dve.tensor_copy(h_hi[:, 4 + h, :], hraw[:, 0, :])
                        dve.drain()
                        remainder(h_lo[:, 4 + h, :], hraw[:, 0, :], h_hi[:, 4 + h, :]).then_inc(s_y, 1)
                project_out(p0 + MIX_PANELS, 18 * l + KB - 1)

            def head_norm(i, j, width, rotate, scale, dst_hi, dst_lo):
                w = slice(0, width)
                dve.wait_ge(hn_guess, i + 1)
                newton(width)
                if rotate:
                    dve.tensor_tensor(xs[:, j, w], xs[:, j, w], rope_sb[:, 0, w], ALU.mult)
                    dve.tensor_tensor(newt[:, w], ps[:, 4 + 2 * j, w], rope_sb[:, 1, w], ALU.mult)
                    dve.drain()
                    dve.tensor_tensor(xs[:, j, w], xs[:, j, w], newt[:, w], ALU.add)
                    dve.drain()
                dve.scalar_tensor_tensor(out=xs[:, j, w], in0=xs[:, j, w], scalar=scale, in1=rstd[:, w],
                                         op0=ALU.mult, op1=ALU.mult)
                dve.drain()
                dve.tensor_copy(dst_hi, xs[:, j, w])
                dve.drain()
                remainder(dst_lo, xs[:, j, w], dst_hi).then_inc(hn_out, 1)

            def attend(u0, widths, branch, outputs):
                n = len(widths)
                for s in range(n + 2):
                    if s < n:
                        w, b = slice(0, widths[s]), s % TB
                        dve.wait_ge(t_scores, u0 + s + 1)
                        if branch is None:
                            dve.tensor_reduce(mx[:, s % 2, 0:1], ps[:, s % 2, w], AX_X, ALU.max)
                        else:
                            dve.memset(tick[:], 0.0)
                            dve.tensor_tensor_reduce(prob2[:, s % 2, w], ps[:, s % 2, w],
                                                     mask[:, branch, T - P - P * b:T],
                                                     1.0, -3e38, ALU.add, ALU.max, mx[:, s % 2, 0:1])
                        dve.drain()
                        dve.tensor_scalar(nmx[:, s % 2, 0:1], mx[:, s % 2, 0:1], -1.0, None, ALU.mult).then_inc(t_max, 1)
                    if 1 <= s <= n:
                        u = s - 1
                        w = slice(0, widths[u])
                        dve.wait_ge(t_exp, u0 + u + 1)
                        dve.reciprocal(rsum[:, u % 2, 0:1], ssum[:, u % 2, 0:1])
                        dve.drain()
                        dve.tensor_scalar(att2[:, u % 2, w], prob2[:, u % 2, w], rsum[:, u % 2, 0:1], None,
                                          ALU.mult).then_inc(t_att, 1)
                    if s >= 2:
                        u = s - 2
                        q, kbs = slice(P * (u % TB), P * (u % TB) + P), widths[u] // P
                        dve.wait_ge(t_thi, u0 + u + 1)
                        remainder(pt_lo[:, 0:kbs, q], ps[:, 2 + u % 2, 0:P * kbs].rearrange("p (k n) -> p k n", k=kbs),
                                  pt_hi[:, 0:kbs, q]).then_inc(t_tlo, 1)
                        outputs(u)

            def stack2(l):
                n = 3 * LAYERS + 1 + l
                p0 = BASE2 + LAYER2_PANELS * l
                g0 = GROUPS * l
                dve.tensor_copy(v2[:], v2_all[:, bass.ds(NV2 * l, NV2)])
                dve.drain()
                for k in range(KB):
                    g = v2[:, G_MEM + k:G_MEM + k + 1]
                    dve.tensor_scalar(mh_hi[:, k, :], memn[:, k, :], g, None, ALU.mult)
                    dve.drain()
                    dve.scalar_tensor_tensor(out=mh_lo[:, k, :], in0=memn[:, k, :], scalar=g,
                                             in1=mh_hi[:, k, :].bitcast(F32), op0=ALU.mult,
                                             op1=ALU.subtract).then_inc(memh_ready, 1)
                norm(n, v2[:, G_NORM:G_NORM + KB])
                for c in range(2):
                    head_norm(2 * g0 + c, c, 256, False, 1.0, km_hi[:, c, :], km_lo[:, c, :])
                dve.wait_ge(v_thi, 7 * l + 1)
                for h in range(2):
                    s = slice(64 * h, 64 * h + 64)
                    ins = remainder(vm_lo[:, :, :, h, s],
                                    ps[:, 4, :].rearrange("p (t c n) -> p t c n", t=2, c=2)[:, :, :, s],
                                    vm_hi[:, :, :, h, s])
                ins.then_inc(v_tlo, 1)
                for branch in range(2):
                    with dve.Fori(0, 3) as j:
                        gi = 1 + 3 * branch + j
                        G = g0 + gi
                        for c in range(2):
                            head_norm(2 * G + c, c, T, True, 1.0 if c else 0.125, qk_hi[:, c, :], qk_lo[:, c, :])
                        dve.wait_ge(v_thi, 7 * l + gi + 1)
                        for h in range(2):
                            s = slice(64 * h, 64 * h + 64)
                            ins = remainder(vp_lo[:, :, h, s], ps[:, 4, :].rearrange("p (t n) -> p t n", t=TB)[:, :, s],
                                            vp_hi[:, :, h, s])
                        ins.then_inc(v_tlo, 1)
                        attend(UNITS2 * l + 8 * (gi - 1), [P * (b + 1) for _ in range(2) for b in range(TB)],
                               branch, lambda u: None)
                        dve.wait_ge(t_o, 16 * l + 2 * gi)
                        c = bass.ds(gi - 1, 1)
                        dve.tensor_tensor(y[:, c, :], y[:, c, :], ps[:, 5:6, :], ALU.mult).then_inc(t_y, 1)
                G = g0 + 7
                for c in range(2):
                    head_norm(2 * G + c, c, T, False, 0.125, qk_hi[:, c, :], qk_lo[:, c, :])

                def outputs_mem(u):
                    pass
                attend(UNITS2 * l + 48, [256] * 16, None, outputs_mem)
                for c in range(2):
                    dve.wait_ge(t_o, 16 * l + 12 + 2 * c + 2)
                    dve.tensor_tensor(y[:, 6 + c, :], y[:, 6 + c, :], ps[:, 5 + c, :], ALU.mult).then_inc(t_y, 1)
                dve.drain()
                dve.tensor_copy(h_hi[:, 0, :], y[:, 0, :])
                for k in range(KB):
                    dve.drain()
                    if k + 1 < KB:
                        dve.tensor_copy(h_hi[:, k + 1, :], y[:, k + 1, :])
                    remainder(h_lo[:, k, :], y[:, k, :], h_hi[:, k, :]).then_inc(y_ready, 1)
                project_out(p0 + 2 * GROUPS, 18 * LAYERS + OUT_PANELS * l)

            dve.wait_ge(in_small, 16 * 5)
            dve.tensor_tensor(hraw[0:64, 0, 0:4], hraw[0:64, 1, 0:4], hraw[0:64, 1, 4:8], ALU.mult).then_inc(lam_in, 1)
            dve.wait_ge(lam_exp, 1)
            e = hraw[:, 1, 8:12].rearrange("p (l n) -> p l n", l=LAYERS)
            dve.tensor_tensor(nlam_all[:], e[:, :, 1], e[:, :, 0], ALU.subtract)
            dve.drain()
            dve.tensor_tensor(nlam_all[:], nlam_all[:],
                              v1_all[:].rearrange("p (l n) -> p l n", l=LAYERS)[:, :, G_LAM], ALU.subtract)
            dve.wait_ge(in_x, 16)
            for i in range(KB):
                dve.engine_nop().then_inc(x_ready, 1)
            with dve.Fori(0, LAYERS) as l:
                p0 = LAYER1_PANELS * l
                dve.drain()
                dve.tensor_copy(v1[:], v1_all[:, bass.ds(NV1 * l, NV1)])
                dve.tensor_copy(nlam[:], nlam_all[:, bass.ds(l, 1)])
                dve.drain()
                dve.tensor_scalar(v1[:, G_HEAD:G_HEAD + HEADS1], v1[:, G_HEAD:G_HEAD + HEADS1],
                                  v1[:, G_KEEP:G_KEEP + 1], None, ALU.mult)
                feed_forward(3 * l, 2 * l, p0, v1[:, G_FFN1:G_FFN1 + KB], 18 * l)
                mixer1(l, 3 * l + 1, p0 + FFN_PANELS)
                feed_forward(3 * l + 2, 2 * l + 1, p0 + LAYER1_PANELS - FFN_PANELS,
                             v1[:, G_FFN2:G_FFN2 + KB], 18 * l + KB - 1 + OUT_PANELS)
            dve.wait_ge(guess_ready, 3 * LAYERS + 1)
            newton(T)
            for m in OUT_ORDER:
                dve.scalar_tensor_tensor(out=x_sb[:, m, :], in0=x_sb[:, m, :], scalar=fin_g[:, m:m + 1], in1=rstd[:],
                                         op0=ALU.mult, op1=ALU.mult).then_inc(x_ready, 1)
            for z in (vp_hi, vp_lo, vm_hi, vm_lo):
                dve.memset(z[:].bitcast(F32), 0.0)
            dve.drain()
            dve.wait_ge(mem_guess, 1)
            newton(256)
            for k in range(KB):
                ins = dve.tensor_tensor(memn[:, k, :], memn[:, k, :], rstd[:, 0:256], ALU.mult)
            ins.then_inc(mem_normed, 1)
            dve.drain()
            with dve.Fori(0, LAYERS) as l:
                stack2(l)


def blocks(w, cols):
    r, n = w.shape
    return w.reshape(r // P, P, n // cols, cols).transpose(2, 1, 0, 3).reshape(n // cols, P, -1)


def weight_stream(inp, const):
    out = np.zeros((ALL_PANELS + SPARE_PANELS, P, PANEL), np.float32)
    at = 0

    def put(panels):
        nonlocal at
        out[at:at + len(panels), :, :panels.shape[2]] = panels
        at += len(panels)

    def feed_forward(gate, up, down):
        both = np.stack([gate.reshape(D, FB, P), up.reshape(D, FB, P)], 2).reshape(D, 2 * FF)
        put(blocks(both, 2 * P))
        put(down.reshape(DOWN_PANELS, 2, P, D).transpose(0, 2, 1, 3).reshape(DOWN_PANELS, P, PANEL))

    def out_blocks(w):
        put(blocks(w.reshape(D, KB, P)[:, OUT_ORDER].reshape(D, D), 2 * P))

    for l in range(LAYERS):
        feed_forward(inp["ffn1_w_gate"][l], inp["ffn1_w_up"][l], inp["ffn1_w_down"][l])
        put(blocks(inp["w_in"][l], 2 * P))
        put(const["chan"][None])
        put(const["seq"])
        four = inp["fourier_w"][l].reshape(2, P, 2 * P).transpose(1, 0, 2).reshape(P, 4 * P)
        pool = np.zeros((P, 2, P), np.float32)
        for g in range(4):
            s = slice(64 * (g % 2), 64 * (g % 2) + 64)
            pool[s, g // 2, s] = inp["pool_w"][l][g]
        put(np.concatenate([four, pool.reshape(P, 2 * P)], 1)[None])
        out_blocks(inp["w_out"][l])
        feed_forward(inp["ffn2_w_gate"][l], inp["ffn2_w_up"][l], inp["ffn2_w_down"][l])
    for l in range(LAYERS):
        w = inp["w_in_2"][l]
        put(blocks(inp["w_mem_kv_2"][l], 2 * P))
        for branch in range(2):
            for j in range(3):
                q, k, v, g = (w[:, 1536 * branch + 384 * i + P * j:][:, :P] for i in range(4))
                put(blocks(np.concatenate([q, k, v, g], 1), 2 * P))
        put(blocks(w[:, 3072:3584], 2 * P))
        out_blocks(inp["w_out_2"][l])
    assert at == ALL_PANELS
    return out


def columns(v):
    return v.reshape(-1, P).T


def kernel(**inputs):
    import concourse.bacc as bacc
    from concourse.bass_utils import run_bass_kernel_spmd as run

    inp = {k: np.asarray(v) for k, v in inputs.items()}
    const = shape_constants()
    start = [0.8 - 0.6 * math.exp(-0.3 * l) for l in range(LAYERS)]
    f = np.float32
    vecs1 = [np.concatenate([
        columns(inp["ffn1_norm"][l]), columns(inp["mix_norm"][l]), columns(inp["ffn2_norm"][l]),
        columns(inp["pool_scale"][l]), columns(inp["attn_head_norm"][l]),
        np.full((P, 1), 1.0 - start[l], f), np.full((P, 1), start[l], f)], 1) for l in range(LAYERS)]
    vecs2 = [np.concatenate([
        columns(inp["norm_g_2"][l]), columns(inp["mem_norm_g_2"][l]),
        np.concatenate([inp["qk_g_2"][l].T] * 2, 0)], 1) for l in range(LAYERS)]
    lamv = np.stack([inp[n][l] for a in "qk" for l in range(LAYERS) for n in (f"lam_{a}1", f"lam_{a}2")], 1)
    feature_major = lambda a: a[0].T.reshape(KB, P, -1).transpose(1, 0, 2).reshape(P, -1)
    arrays = {
        "x": feature_major(inp["x"]), "mem": feature_major(inp["mem_2"]),
        "stream": weight_stream(inp, const),
        "vecs1": np.concatenate(vecs1, 1), "vecs2": np.concatenate(vecs2, 1),
        "final_g": columns(inp["final_norm"]), "lamv": lamv, "consts": const["consts"],
        "dist": const["dist"], "masks": const["masks"].reshape(P, 2, TOE)[:, :, :T].reshape(P, 2 * T),
        "recip": const["recip"], "rope": const["rope"],
    }
    arrays = {k: np.ascontiguousarray(v) for k, v in arrays.items()}
    nc = bacc.Bacc("TRN2", target_bir_lowering=False, num_devices=1)
    args = [nc.dram_tensor(f"in_{k}", a.shape, mybir.dt.from_np(a.dtype), kind="ExternalInput").ap()
            for k, a in arrays.items()]
    args.append(nc.dram_tensor("out_x", (P, KB, T), F32, kind="ExternalOutput").ap())
    names = dict(zip(arrays, args))
    build(nc, **names, out=args[-1])
    r = run(nc, [{f"in_{k}": a for k, a in arrays.items()}], core_ids=[0])
    got = np.asarray(r.results[0]["out_x"])
    return np.ascontiguousarray(got.transpose(1, 0, 2).reshape(D, T).T)[None]
```

```python
from contextlib import ExitStack
import math

import numpy as np
import concourse.bass as bass
from concourse import mybir

F32 = mybir.dt.float32
F32R = mybir.dt.float32r
ALU = mybir.AluOpType
ACT = mybir.ActivationFunctionType
AX_X = mybir.AxisListType.X

P = 128
D = 1024
T = 512
KB = D // P
TB = T // P
LAYERS = 2
FF = 2816
FB = FF // P
PANEL = 2048
EPS = 1e-6
MASKED = -1e30

UP_PANELS = FB
DOWN_PANELS = FB // 2
FFN_PANELS = UP_PANELS + DOWN_PANELS
MIX_PANELS = 12
OUT_PANELS = 4
LAYER1_PANELS = 2 * FFN_PANELS + MIX_PANELS + OUT_PANELS
GROUPS = 8
LAYER2_PANELS = 2 * GROUPS + OUT_PANELS
BASE2 = LAYERS * LAYER1_PANELS
ALL_PANELS = BASE2 + LAYERS * LAYER2_PANELS
SPARE_PANELS = 2

OUT_ORDER = [4, 5, 6, 7, 0, 1, 2, 3]
SUM_BANK = 4

HEADS1 = 4
UNITS1 = HEADS1 * TB
SLOPES = [2.0 ** (-8.0 * (i + 1) / HEADS1) for i in range(HEADS1)]
PAD = 8
WINDOWS = (2, 4, 8, 16)
TOE = 2 * T - P

G_FFN1, G_MIX, G_FFN2, G_POOL, G_HEAD, G_KEEP, G_LAM, NV1 = 0, 8, 16, 24, 26, 30, 31, 32
G_NORM, G_MEM, G_QK, NV2 = 0, 8, 16, 32
C_ID, C_MEAN, C_HALF, C_HEAD, C_ROT = range(5)
NC = 5 * P + 1

MIX_UNITS = (
    [("a", c, c, 0 if c else None) for c in range(2)]
    + [("f", c, 2 + c, 1 if c else None) for c in range(2)]
    + [("q", c, c, 2 + c // 2 if c % 2 else None) for c in range(4)]
    + [("k", c, c, 4 + c // 2 if c % 2 else None) for c in range(4)]
    + [("v", 4 * h + t, 4 * h + t, 6 + h if t == 3 else None) for h in range(2) for t in range(4)]
    + [("fc", t, t, 8 if t == 3 else None) for t in range(4)]
    + [("yf", c, 4 + c, 10 if c else None) for c in range(2)]
    + [("four", c, 6 + c, None) for c in range(2)]
    + [("pool", c, c, 11 if c else None) for c in range(2)]
)
NU = len(MIX_UNITS)
READY_BEFORE = [sum(u[3] is None for u in MIX_UNITS[:i]) for i in range(NU + 1)]
READY1 = READY_BEFORE[NU]
UNIT_AT = {u[:2]: i for i, u in enumerate(MIX_UNITS)}

UNITS2 = 64
PAIR_UNITS = 2 * TB


def shape_constants():
    i = np.arange(P)
    consts = np.zeros((P, NC), np.float64)
    consts[:, C_ID * P:(C_ID + 1) * P] = np.eye(P)
    consts[:, C_MEAN * P:(C_MEAN + 1) * P] = 1.0 / D
    consts[:, C_HALF * P:(C_HALF + 1) * P] = (i[:, None] // 64 == i[None] // 64) / 64.0
    consts[:, C_HEAD * P:(C_HEAD + 1) * P] = 1.0 / P
    rot = np.zeros((P, P))
    for m in range(P):
        if m % 64 < 32:
            rot[m + 32, m] = -1.0
        else:
            rot[m - 32, m] = 1.0
    consts[:, C_ROT * P:(C_ROT + 1) * P] = rot
    consts[:, NC - 1] = EPS
    lag = i[:, None] + (T - P) - np.arange(TOE)[None]
    dist = np.abs(lag)
    causal = np.where(lag >= 0, 0.0, MASKED)
    count = ((lag <= 128).astype(int) + (lag % 4 == 0) + (lag % 16 == 0)) * (lag >= 0)
    dilated = np.where(count > 0, np.log(np.maximum(count, 1)), MASKED)
    t = np.arange(T)
    recip = np.zeros((P, 2, T))
    for g, w in enumerate(WINDOWS):
        cnt = np.minimum(t + w - 1 - w // 2 + 1, T) - np.maximum(t - w // 2, 0)
        recip[64 * (g % 2):64 * (g % 2) + 64, g // 2] = 1.0 / cnt
    inv = (10000.0 ** (-np.arange(32, dtype=np.float32) / np.float32(32))).astype(np.float32)
    ang = (t.astype(np.float32)[:, None] * inv[None]).astype(np.float32).astype(np.float64)
    rope = np.stack([np.cos(ang).T[i % 32], np.sin(ang).T[i % 32]], 1)
    c64 = 2 * np.pi * np.outer(np.arange(64), np.arange(64)) / 64
    chan = np.zeros((P, 2, P))
    for g in range(2):
        s = slice(64 * g, 64 * g + 64)
        chan[s, 0, s] = np.cos(c64) / 8
        chan[s, 1, s] = np.sin(c64) / 8
    cs = 2 * np.pi * (np.outer(t, t) % T) / T
    seq = np.stack([np.cos(cs), -np.sin(cs)]) / math.sqrt(T)
    seq = seq.reshape(2, TB, P, T).transpose(0, 2, 1, 3).reshape(2, P, PANEL)
    f = np.float32
    return {
        "consts": consts.astype(f), "dist": dist.astype(f),
        "masks": np.stack([causal, dilated], 1).reshape(P, 2 * TOE).astype(f),
        "recip": recip.reshape(P, 2 * T).astype(f), "rope": rope.reshape(P, 2 * T).astype(f),
        "chan": chan.reshape(P, 2 * P).astype(f), "seq": seq.astype(f),
    }


def build(nc, x, mem, stream, vecs1, vecs2, final_g, lamv, consts, dist, masks, recip, rope, out):
    ctx = ExitStack()
    with ctx:
        def sb(name, shape, dt=F32, stack=ctx):
            return stack.enter_context(nc.sbuf_tensor(name, shape, dt))

        def sem(name):
            return ctx.enter_context(nc.semaphore(name))

        x_sb = sb("x_sb", [P, KB, T])
        h_hi = sb("h_hi", [P, KB, T], F32R)
        h_lo = sb("h_lo", [P, KB, T], F32R)
        raw = sb("raw", [P, 2, PANEL])
        w_hi = sb("w_hi", [P, 2, PANEL], F32R)
        w_lo = sb("w_lo", [P, 2, PANEL], F32R)
        cst = sb("cst", [P, NC])
        v1_all = sb("v1_all", [P, LAYERS * NV1])
        v1 = sb("v1", [P, NV1])
        v2_all = sb("v2_all", [P, LAYERS * NV2])
        v2 = sb("v2", [P, NV2])
        fin_g = sb("fin_g", [P, KB])
        nlam_all = sb("nlam_all", [P, LAYERS])
        nlam = sb("nlam", [P, 1])
        sq = sb("sq", [P, 2, T])
        ms = sb("ms", [P, 2, T])
        guess = sb("guess", [P, 2, T])
        newt = sb("newt", [P, 2, T])
        hraw = sb("hraw", [P, 2, T])
        mx = sb("mx", [P, 2, 2])
        nmx = sb("nmx", [P, 2, 2])
        ssum = sb("ssum", [P, 2, 2])
        rsum = sb("rsum", [P, 2, 2])
        tick = sb("tick", [P, 1])
        eps = cst[:, NC - 1:NC]

        def const(i):
            return cst[:, i * P:(i + 1) * P]

        ffn = ExitStack()
        hid_hi = sb("hid_hi", [P, FB, T], F32R, ffn)
        hid_lo = sb("hid_lo", [P, FB, T], F32R, ffn)
        ffn.close()
        mix = ExitStack()
        q_hi = sb("q_hi", [P, HEADS1, T], F32R, mix)
        q_lo = sb("q_lo", [P, HEADS1, T], F32R, mix)
        k_hi = sb("k_hi", [P, HEADS1, T], F32R, mix)
        k_lo = sb("k_lo", [P, HEADS1, T], F32R, mix)
        v_hi = sb("v_hi", [P, TB, 512], F32R, mix)
        v_lo = sb("v_lo", [P, TB, 512], F32R, mix)
        bias = sb("bias", [P, 2, TOE], F32, mix)
        dist_sb = sb("dist_sb", [P, TOE], F32, mix)
        four = ExitStack()
        rec_sb = sb("rec_sb", [P, 2, T], F32, four)
        f_hi = sb("f_hi", [P, 2, T], F32R, four)
        f_lo = sb("f_lo", [P, 2, T], F32R, four)
        apad = sb("apad", [P, 2, T + 2 * PAD], F32, four)
        win = sb("win", [P, 2, T + 2 * PAD], F32, four)
        m_hi = sb("m_hi", [P, 2, T], F32R, four)
        m_lo = sb("m_lo", [P, 2, T], F32R, four)
        four.close()
        prob1 = sb("prob1", [P, 2, 2, T], F32, mix)
        att1 = sb("att1", [P, 2, T], F32, mix)
        at_hi = sb("at_hi", [P, TB, T], F32R, mix)
        at_lo = sb("at_lo", [P, TB, T], F32R, mix)
        fc_hi, fc_lo = h_hi[:, 4:8, :], h_lo[:, 4:8, :]
        mix.close()
        two = ExitStack()
        y = sb("y", [P, KB, T], F32, two)
        memn = sb("memn", [P, KB, 256], F32, two)
        qk_hi = sb("qk_hi", [P, 2, T], F32R, two)
        qk_lo = sb("qk_lo", [P, 2, T], F32R, two)
        km_hi = sb("km_hi", [P, 2, 256], F32R, two)
        km_lo = sb("km_lo", [P, 2, 256], F32R, two)
        vp_hi = sb("vp_hi", [P, TB, 2, P], F32R, two)
        vp_lo = sb("vp_lo", [P, TB, 2, P], F32R, two)
        vm_hi = sb("vm_hi", [P, 2, 2, 2, P], F32R, two)
        vm_lo = sb("vm_lo", [P, 2, 2, 2, P], F32R, two)
        pt_hi = sb("pt_hi", [P, TB, T], F32R, two)
        pt_lo = sb("pt_lo", [P, TB, T], F32R, two)
        xs = sb("xs", [P, 2, T], F32, two)
        mask = sb("mask", [P, 2, T], F32, two)
        prob2 = sb("prob2", [P, 2, T], F32, two)
        att2 = sb("att2", [P, 2, T], F32, two)
        rope_sb = sb("rope_sb", [P, 2, T], F32, two)
        two.close()
        mh_hi = pt_hi[:].rearrange("p a (b n) -> p (a b) n", b=2)
        mh_lo = pt_lo[:].rearrange("p a (b n) -> p (a b) n", b=2)

        ps = ctx.enter_context(nc.psum_tensor("ps", [P, 8, 512], F32))

        in_x = sem("in_x")
        in_small = sem("in_small")
        in_mix = sem("in_mix")
        in_two = sem("in_two")
        raw_ready = [sem("raw_ready0"), sem("raw_ready1")]
        hi_split = sem("hi_split")
        lo_split = sem("lo_split")
        panel_done = sem("panel_done")
        x_ready = sem("x_ready")
        square_ready = sem("square_ready")
        sum_step = sem("sum_step")
        guess_ready = sem("guess_ready")
        h_ready = sem("h_ready")
        silu_ready = sem("silu_ready")
        hid_ready = sem("hid_ready")
        out_ready = sem("out_ready")
        lam_mm = sem("lam_mm")
        lam_in = sem("lam_in")
        lam_exp = sem("lam_exp")
        lam_done = sem("lam_done")
        unit_ready = sem("unit_ready")
        unit_hi = sem("unit_hi")
        unit_lo = sem("unit_lo")
        pooled = sem("pooled")
        bias_ready = sem("bias_ready")
        s_scores = sem("s_scores")
        s_max = sem("s_max")
        s_exp = sem("s_exp")
        s_att = sem("s_att")
        s_tr = sem("s_tr")
        s_thi = sem("s_thi")
        s_tlo = sem("s_tlo")
        s_o = sem("s_o")
        s_osq = sem("s_osq")
        s_osum = sem("s_osum")
        s_oguess = sem("s_oguess")
        s_y = sem("s_y")
        mem_sq = sem("mem_sq")
        mem_sum = sem("mem_sum")
        mem_guess = sem("mem_guess")
        mem_normed = sem("mem_normed")
        memh_ready = sem("memh_ready")
        chunk_ready = sem("chunk_ready")
        hn_in = sem("hn_in")
        hn_mm = sem("hn_mm")
        hn_ms = sem("hn_ms")
        hn_rot = sem("hn_rot")
        hn_guess = sem("hn_guess")
        hn_out = sem("hn_out")
        v_in = sem("v_in")
        v_tr = sem("v_tr")
        v_thi = sem("v_thi")
        v_tlo = sem("v_tlo")
        g_in = sem("g_in")
        t_scores, t_max, t_exp, t_att, t_tr, t_thi, t_tlo = (
            sem(f"t_{n}") for n in ("scores", "max", "exp", "att", "tr", "thi", "tlo"))
        t_o = sem("t_o")
        t_y = sem("t_y")
        y_ready = sem("y_ready")
        stored = sem("stored")

        block = ctx.enter_context(nc.Block())

        def slot(ap, p):
            return ap[:, p % 2, :]

        units1 = [(h, b) for h in range(HEADS1) for b in range(TB)]

        @block.sync
        def _(sp):
            for s in range(2):
                sp.dma_start(raw[:, s, :], stream[s]).then_inc(raw_ready[s], 16)
            with sp.Fori(1, (ALL_PANELS + SPARE_PANELS) // 2) as i:
                for s in range(2):
                    sp.wait_ge(lo_split, 2 * i + s - 1)
                    sp.dma_start(raw[:, bass.ds(s, 1), :],
                                 stream[bass.ds(2 * i + s, 1)].rearrange("a p n -> p a n")
                                 ).then_inc(raw_ready[s], 16)
            for i in range(KB):
                sp.wait_ge(x_ready, 8 * (3 * LAYERS + 1 + LAYERS) + OUT_ORDER.index(i) + 1)
                sp.dma_start(out[:, i, :], x_sb[:, i, :]).then_inc(stored, 16)
            sp.wait_ge(stored, 16 * KB)

        @block.gpsimd
        def _(gp):
            with gp.Fori(0, (ALL_PANELS + SPARE_PANELS) // 2) as i:
                for s in range(2):
                    gp.wait_ge(hi_split, 2 * i + s + 1)
                    gp.tensor_tensor(w_lo[:, s, :], raw[:, s, :], w_hi[:, s, :].bitcast(F32),
                                     ALU.subtract).then_inc(lo_split, 1)

        @block.tensor
        def _(pe):
            def three(dst, l_hi, l_lo, r_hi, r_lo, first, last):
                pe.matmul(dst, l_hi, r_hi, start=first, stop=False)
                pe.matmul(dst, l_hi, r_lo, start=False, stop=False)
                return pe.matmul(dst, l_lo, r_hi, start=False, stop=last)

            def sum_squares(n):
                for i in range(KB):
                    pe.wait_ge(square_ready, 8 * n + i + 1)
                    pe.matmul(ps[:, SUM_BANK, :], const(C_MEAN), sq[:, i % 2, :],
                              start=(i == 0), stop=(i == KB - 1)).then_inc(sum_step, 1)

            def panel(p):
                pe.wait_ge(lo_split, p + 1)

            def up(n, p, c, s, first=False):
                panel(p)
                w = [t[:, s, :].rearrange("p (k g n) -> p k g n", k=KB, g=2) for t in (w_hi, w_lo)]
                for k in range(KB):
                    if first:
                        pe.wait_ge(h_ready, 8 * n + k + 1)
                    for g in range(2):
                        mm = three(ps[:, 2 * (c % 2) + g, :], w[0][:, k, g, :], w[1][:, k, g, :],
                                   h_hi[:, k, :], h_lo[:, k, :], k == 0, k == KB - 1)
                mm.then_inc(panel_done, 1)

            def down(p, d, s, F, first=False, last=False):
                panel(p)
                w = [t[:, s, :].rearrange("p (f n) -> p f n", f=2) for t in (w_hi, w_lo)]
                for i, m in enumerate(OUT_ORDER):
                    if first and m == 0:
                        pe.wait_ge(hid_ready, FB * F + FB)
                    for f in range(2):
                        if isinstance(d, int):
                            r = hid_hi[:, 2 * d + f, :], hid_lo[:, 2 * d + f, :]
                        else:
                            r = [t[:, bass.ds(2 * d + f, 1), :] for t in (hid_hi, hid_lo)]
                        mm = three(ps[:, m, :], w[0][:, f, P * m:P * m + P], w[1][:, f, P * m:P * m + P],
                                   *r, first and f == 0, last and f == 1)
                    if last and i < KB - 1:
                        mm.then_inc(out_ready, 1)
                mm.then_inc(panel_done, 1)

            def feed_forward(n, F, p0, odd):
                sum_squares(n)
                for c in range(2):
                    up(n, p0 + c, c, (odd + c) % 2, first=(c == 0))
                with pe.Fori(1, FB // 2) as i:
                    for c in range(2):
                        pe.wait_ge(hid_ready, FB * F + 2 * i + c - 1)
                        up(n, p0 + 2 * i + c, c, (odd + c) % 2)
                pd = p0 + UP_PANELS
                pe.wait_ge(hid_ready, FB * F + 2)
                down(pd, 0, odd % 2, F, first=True)
                with pe.Fori(0, (DOWN_PANELS - 3) // 2) as i:
                    for e in range(2):
                        down(pd + 1 + 2 * i + e, 1 + 2 * i + e, (odd + 1 + e) % 2, F)
                for d in (DOWN_PANELS - 2, DOWN_PANELS - 1):
                    down(pd + d, d, (odd + d) % 2, F, last=(d == DOWN_PANELS - 1))

            def project_out(p0, odd, ready):
                for j in range(OUT_PANELS):
                    panel(p0 + j)
                    w = [t[:, (odd + j) % 2, :].rearrange("p (k g n) -> p k g n", k=KB, g=2) for t in (w_hi, w_lo)]
                    for g in range(2):
                        for k in range(KB):
                            if j == 0 and g == 0:
                                ready(k)
                            mm = three(ps[:, OUT_ORDER[2 * j + g], :], w[0][:, k, g, :], w[1][:, k, g, :],
                                       h_hi[:, k, :], h_lo[:, k, :], k == 0, k == KB - 1)
                        if g == 0:
                            mm.then_inc(out_ready, 1)
                    mm.then_inc(panel_done, 1)

            def mixer1(l, n, p0):
                lo0 = NU * l

                def finish(i, mm):
                    mm.then_inc(unit_ready if MIX_UNITS[i][3] is None else panel_done, 1)

                sum_squares(n)
                i = 0
                for j in range(6):
                    panel(p0 + j)
                    w = [t[:, (j + 1) % 2, :].rearrange("p (k g n) -> p k g n", k=KB, g=2) for t in (w_hi, w_lo)]
                    for g in range(2):
                        if i >= 4:
                            pe.wait_ge(unit_lo, lo0 + i - 3)
                        for k in range(KB):
                            if i == 0:
                                pe.wait_ge(h_ready, 8 * n + k + 1)
                            mm = three(ps[:, MIX_UNITS[i][2], :], w[0][:, k, g, :], w[1][:, k, g, :],
                                       h_hi[:, k, :], h_lo[:, k, :], k == 0, k == KB - 1)
                        finish(i, mm)
                        i += 1
                for j in range(6, 8):
                    panel(p0 + j)
                    w = [t[:, (j + 1) % 2, :].rearrange("p (k n) -> p k n", k=KB) for t in (w_hi, w_lo)]
                    for t in range(TB):
                        if j == 6:
                            pe.wait_ge(unit_lo, lo0 + i - 3)
                        s = slice(P * t, P * t + P)
                        for k in range(KB):
                            mm = three(ps[:, MIX_UNITS[i][2], 0:256], h_hi[:, k, s], h_lo[:, k, s],
                                       w[0][:, k, :], w[1][:, k, :], k == 0, k == KB - 1)
                        finish(i, mm)
                        i += 1
                panel(p0 + 8)
                for t in range(TB):
                    pe.wait_ge(unit_lo, lo0 + i - 7)
                    s = slice(P * t, P * t + P)
                    for c in range(2):
                        mm = three(ps[:, MIX_UNITS[i][2], 256 * c:256 * c + 256], f_hi[:, c, s], f_lo[:, c, s],
                                   w_hi[:, 1, 0:256], w_lo[:, 1, 0:256], True, True)
                    finish(i, mm)
                    i += 1
                pe.wait_ge(unit_lo, lo0 + i)
                for e in range(2):
                    panel(p0 + 9 + e)
                    w = [t[:, e, :].rearrange("p (t n) -> p t n", t=TB) for t in (w_hi, w_lo)]
                    for c in range(2):
                        s = slice(256 * c + P * e, 256 * c + P * e + P)
                        for t in range(TB):
                            mm = three(ps[:, 4 + c, :], fc_hi[:, t, s], fc_lo[:, t, s],
                                       w[0][:, t, :], w[1][:, t, :], e == 0 and t == 0, e == 1 and t == TB - 1)
                        if e == 1:
                            finish(i, mm)
                            i += 1
                    if e == 0:
                        mm.then_inc(panel_done, 1)
                panel(p0 + 11)
                pe.wait_ge(unit_lo, lo0 + i)
                for c in range(2):
                    for k in range(2):
                        s = slice(256 * k + P * c, 256 * k + P * c + P)
                        mm = three(ps[:, 6 + c, :], w_hi[:, 0, s], w_lo[:, 0, s],
                                   f_hi[:, k, :], f_lo[:, k, :], k == 0, k == 1)
                    finish(i, mm)
                    i += 1
                for c in range(2):
                    pe.wait_ge(pooled, 2 * l + c + 1)
                    s = slice(512 + P * c, 512 + P * c + P)
                    mm = three(ps[:, c, :], w_hi[:, 0, s], w_lo[:, 0, s],
                               m_hi[:, c, :], m_lo[:, c, :], True, True)
                    finish(i, mm)
                    i += 1
                pe.wait_ge(unit_lo, lo0 + NU)
                u0 = UNITS1 * l
                for s in range(UNITS1 + 5):
                    if s < UNITS1:
                        h, b = units1[s]
                        if s >= 2:
                            pe.wait_ge(s_max, u0 + s - 1)
                        for j in range(2):
                            r, c = slice(64 * j, 64 * j + 64), slice(P * b, P * b + P)
                            mm = three(ps[:, 2 * (s % 2) + j, :], q_hi[r, h, c], q_lo[r, h, c],
                                       k_hi[r, h, :], k_lo[r, h, :], True, True)
                        mm.then_inc(s_scores, 1)
                    if 2 <= s <= UNITS1 + 1:
                        u = s - 2
                        pe.wait_ge(s_att, u0 + u + 1)
                        if u >= 2:
                            pe.wait_ge(s_tlo, u0 + u - 1)
                        for kb in range(TB):
                            mm = pe.transpose(ps[:, 4 + u % 2, P * kb:P * kb + P],
                                              att1[:, u % 2, P * kb:P * kb + P], const(C_ID))
                        mm.then_inc(s_tr, 1)
                    if s >= 3 and (s - 3) % TB == TB - 1 and s - 3 < UNITS1:
                        h = (s - 3) // TB
                        pe.wait_ge(s_tlo, u0 + s - 2)
                        if h:
                            pe.wait_ge(s_y, HEADS1 * l + h)
                        for kb in range(TB):
                            c = slice(P * h, P * h + P)
                            mm = three(ps[:, 6, :], v_hi[:, kb, c], v_lo[:, kb, c],
                                       at_hi[:, kb, :], at_lo[:, kb, :], kb == 0, kb == TB - 1)
                        mm.then_inc(s_o, 1)
                    if s >= 4 and (s - 4) % TB == TB - 1 and s - 4 < UNITS1:
                        h = (s - 4) // TB
                        pe.wait_ge(s_osq, HEADS1 * l + h + 1)
                        pe.matmul(ps[:, 7, :], const(C_HEAD), sq[:, 0, :], start=True, stop=True).then_inc(s_osum, 1)
                project_out(p0 + MIX_PANELS, 1,
                            lambda k: pe.wait_ge(s_y, HEADS1 * l + k - 3) if k >= 4 else None)

            def chunk_slices(s):
                return [t[:, s, :].rearrange("p (k g n) -> p k g n", k=KB, g=2) for t in (w_hi, w_lo)]

            def mem_group(G, p, act_hi, act_lo, width, busy):
                w_ = slice(0, width)
                for c in range(4):
                    busy[c]()
                    if c % 2 == 0:
                        panel(p + c // 2)
                    w = chunk_slices(c // 2)
                    for k in range(KB):
                        mm = three(ps[:, c, w_], w[0][:, k, c % 2, :], w[1][:, k, c % 2, :],
                                   act_hi[:, k, :], act_lo[:, k, :], k == 0, k == KB - 1)
                    mm.then_inc(panel_done if c % 2 else chunk_ready, 1)
                    if 1 <= c <= 2:
                        j = c - 1
                        pe.wait_ge(hn_in, 2 * G + j + 1)
                        pe.matmul(ps[:, 5 + 2 * j, w_], const(C_HALF), sq[:, j, w_],
                                  start=True, stop=True).then_inc(hn_mm, 1)

            def attend(u0, units, widths, scores, scores_read, outputs, produce):
                n = len(units)
                for s in range(n + 3):
                    if s < n:
                        if s >= 2:
                            pe.wait_ge(scores_read, u0 + s - 1)
                        scores(s).then_inc(t_scores, 1)
                    if 2 <= s <= n + 1:
                        u = s - 2
                        pe.wait_ge(t_att, u0 + u + 1)
                        if u >= 2:
                            pe.wait_ge(t_tlo, u0 + u - 1)
                        for kb in range(widths[u] // P):
                            mm = pe.transpose(ps[:, 2 + u % 2, P * kb:P * kb + P],
                                              att2[:, u % 2, P * kb:P * kb + P], const(C_ID))
                        mm.then_inc(t_tr, 1)
                    if s >= 3 and (s - 3) % TB == TB - 1:
                        pe.wait_ge(t_tlo, u0 + s - 2)
                        outputs((s - 3) // TB)
                    produce(s)

            def producer(l, gi, p):
                G = GROUPS * l + gi
                rot0 = 12 * l + 2 * (gi - 2)

                def rotate(j):
                    pe.matmul(ps[:, 6, :], const(C_ROT), xs[:, j, :], start=True, stop=True)
                    pe.matmul(ps[:, 7, :], const(C_HALF), sq[:, j, :], start=True, stop=True).then_inc(hn_mm, 1)

                def step(s):
                    if s > 7:
                        return
                    c = s // 2
                    if s == 0:
                        pe.wait_ge(g_in, 7 * l + gi - 1)
                    if s == 2:
                        pe.wait_ge(hn_in, 2 * G + 1)
                    if s == 4:
                        pe.wait_ge(hn_in, 2 * G + 2)
                    if s == 6:
                        pe.wait_ge(v_in, 7 * l + gi)
                    if s % 4 == 0:
                        panel(p + s // 4)
                    w = chunk_slices(c // 2)
                    for k in range(4 * (s % 2), 4 * (s % 2) + 4):
                        mm = three(ps[:, 4, :], w[0][:, k, c % 2, :], w[1][:, k, c % 2, :],
                                   h_hi[:, k, :], h_lo[:, k, :], k == 0, k == KB - 1)
                    if s % 2:
                        mm.then_inc(panel_done if c % 2 else chunk_ready, 1)
                    if s == 2:
                        pe.wait_ge(v_tlo, 7 * l + gi - 1)
                        rotate(0)
                    if s == 4:
                        pe.wait_ge(hn_ms, 2 * G + 1)
                        pe.wait_ge(hn_rot, rot0 + 1)
                        rotate(1)
                    if s == 7:
                        pe.wait_ge(hn_rot, rot0 + 2)
                        for tb in range(TB):
                            mm = pe.transpose(ps[:, 6, P * tb:P * tb + P],
                                              hraw[:, 0, P * tb:P * tb + P], const(C_ID))
                        mm.then_inc(v_tr, 1)
                return step

            def pair_attention(l, gi, produce):
                pe.wait_ge(hn_out, GROUPS * l + gi + 1)
                units = [(h, b) for h in range(2) for b in range(TB)]
                widths = [P * (b + 1) for _, b in units]

                def scores(u):
                    h, b = units[u]
                    r, c, w = slice(64 * h, 64 * h + 64), slice(P * b, P * b + P), slice(0, widths[u])
                    return three(ps[:, u % 2, w], qk_hi[r, 0, c], qk_lo[r, 0, c],
                                 qk_hi[r, 1, w], qk_lo[r, 1, w], True, True)

                def outputs(h):
                    if h == 0:
                        pe.wait_ge(v_tlo, 7 * l + gi)
                        pe.wait_ge(t_y, 8 * l + gi)
                    for kb in range(TB):
                        c = slice(P * kb, T)
                        mm = three(ps[:, 5, c], vp_hi[:, kb, h, :], vp_lo[:, kb, h, :],
                                   pt_hi[:, kb, c], pt_lo[:, kb, c],
                                   h == 0 and kb == 0, h == 1 and kb == TB - 1)
                    mm.then_inc(t_o, 1)

                attend(UNITS2 * l + 16 + PAIR_UNITS * (gi - 2), units, widths, scores, t_max, outputs, produce)

            def stack2(l):
                n = 3 * LAYERS + 1 + l
                p0 = BASE2 + LAYER2_PANELS * l
                g0 = GROUPS * l
                sum_squares(n)
                for k in range(KB):
                    pe.wait_ge(memh_ready, 8 * l + k + 1)
                mem_group(g0, p0, mh_hi, mh_lo, 256, [lambda: None] * 4)
                pe.wait_ge(v_in, 7 * l + 1)
                for c in range(2):
                    for tb in range(2):
                        mm = pe.transpose(ps[:, 4, 256 * tb + P * c:256 * tb + P * c + P],
                                          hraw[:, c, P * tb:P * tb + P], const(C_ID))
                mm.then_inc(v_tr, 1)
                mem_group(g0 + 1, p0 + 2, h_hi, h_lo, T, [
                    lambda: pe.wait_ge(hn_in, 2 * g0 + 1), lambda: pe.wait_ge(hn_in, 2 * g0 + 2),
                    lambda: pe.wait_ge(hn_ms, 2 * g0 + 2), lambda: None])
                pe.wait_ge(hn_out, g0 + 2)
                pe.wait_ge(v_tlo, 7 * l + 1)
                pe.wait_ge(g_in, 7 * l + 1)
                units = [(h, b) for h in range(4) for b in range(TB)]

                def scores_mem(u):
                    h, b = units[u]
                    r, c = slice(64 * (h % 2), 64 * (h % 2) + 64), slice(P * b, P * b + P)
                    return three(ps[:, u % 2, 0:256], qk_hi[r, h // 2, c], qk_lo[r, h // 2, c],
                                 km_hi[r, h // 2, :], km_lo[r, h // 2, :], True, True)

                def outputs_mem(h):
                    if h == 2:
                        pe.wait_ge(t_y, 8 * l + 1)
                    for kb in range(2):
                        mm = three(ps[:, 5, :], vm_hi[:, kb, h // 2, h % 2, :], vm_lo[:, kb, h // 2, h % 2, :],
                                   pt_hi[:, kb, :], pt_lo[:, kb, :],
                                   h % 2 == 0 and kb == 0, h % 2 == 1 and kb == 1)
                    mm.then_inc(t_o, 1)

                attend(UNITS2 * l, units, [256] * 16, scores_mem, t_exp, outputs_mem, producer(l, 2, p0 + 4))
                for first, count in ((2, 3), (5, 2)):
                    with pe.Fori(0, count) as j:
                        gi = first + j
                        pair_attention(l, gi, producer(l, gi + 1, p0 + 2 * (gi + 1)))
                pair_attention(l, 7, lambda s: None)
                project_out(p0 + 2 * GROUPS, 0, lambda k: pe.wait_ge(y_ready, 8 * l + k + 1))

            pe.wait_ge(in_small, 16 * 5)
            pe.wait_ge(lam_in, 1)
            pe.matmul(ps[:, 7, 0:4], newt[0:64, 0, 0:P], hraw[0:64, 0, 0:4],
                      start=True, stop=True).then_inc(lam_mm, 1)
            with pe.Fori(0, LAYERS) as l:
                p0 = LAYER1_PANELS * l
                feed_forward(3 * l, 2 * l, p0, 0)
                mixer_p0 = p0 + FFN_PANELS
                mixer1(l, 3 * l + 1, mixer_p0)
                feed_forward(3 * l + 2, 2 * l + 1, mixer_p0 + MIX_PANELS + OUT_PANELS, 1)
            sum_squares(3 * LAYERS)
            for i in range(KB):
                pe.wait_ge(mem_sq, i + 1)
                pe.matmul(ps[:, 5, 0:256], const(C_MEAN), sq[:, i % 2, 0:256],
                          start=(i == 0), stop=(i == KB - 1)).then_inc(mem_sum, 1)
            with pe.Fori(0, LAYERS) as l:
                stack2(l)

        @block.scalar
        def _(act):
            def split(p, s):
                act.wait_ge(raw_ready[s], 8 * (p - s) + 16)
                act.activation(w_hi[:, s, :], raw[:, s, :], ACT.Copy).then_inc(hi_split, 1)

            def split_after(p, s):
                act.wait_ge(panel_done, p + 1)
                split(p + 2, s)

            def guesses(src, width, done):
                w = slice(0, width)
                act.activation(guess[:, 0, w], src, ACT.Abs_reciprocal_sqrt, bias=eps)
                act.activation(ms[:, 0, w], src, ACT.Identity, bias=eps)
                act.drain()
                act.activation(newt[:, 0, w], guess[:, 0, w], ACT.Square).then_inc(done, 1)

            def pair_guesses(width):
                w = slice(0, width)
                act.activation(guess[:, :, w], ms[:, :, w], ACT.Abs_reciprocal_sqrt)
                act.drain()
                act.activation(newt[:, :, w], guess[:, :, w], ACT.Square).then_inc(hn_guess, 1)

            def norm(n):
                for i, m in enumerate(OUT_ORDER):
                    act.wait_ge(x_ready, 8 * n + i + 1)
                    if i >= 2:
                        act.wait_ge(sum_step, 8 * n + i - 1)
                    act.activation(sq[:, i % 2, :], x_sb[:, m, :], ACT.Square).then_inc(square_ready, 1)
                act.wait_ge(sum_step, 8 * n + 8)
                guesses(ps[:, SUM_BANK, :], T, guess_ready)

            def feed_forward(p0, odd):
                with act.Fori(0, FB // 2) as i:
                    for e in range(2):
                        act.wait_ge(panel_done, p0 + 2 * i + e + 1)
                        act.activation(hraw[:, e, :], ps[:, 2 * e, :], ACT.Silu).then_inc(silu_ready, 1)
                        split(p0 + 2 * i + e + 2, (odd + e) % 2)
                pd = p0 + UP_PANELS
                with act.Fori(0, (DOWN_PANELS - 1) // 2) as i:
                    for e in range(2):
                        split_after(pd + 2 * i + e, (odd + e) % 2)

            def mixer1(l, p0):
                act.dma_start(dist_sb[:], dist).then_inc(in_mix, 16)
                act.dma_start(rec_sb[:].rearrange("p a n -> p (a n)"), recip).then_inc(in_mix, 16)
                for i, (kind, c, bank, ends) in enumerate(MIX_UNITS):
                    if kind == "yf" and c == 0:
                        split_after(p0 + 9, 0)
                    if ends is None:
                        act.wait_ge(unit_ready, READY1 * l + READY_BEFORE[i + 1])
                    else:
                        act.wait_ge(panel_done, p0 + ends + 1)
                    src, scale = ps[:, bank, :], 1.0
                    if kind == "a":
                        dst = apad[:, c, PAD:PAD + T]
                    elif kind in ("f", "yf"):
                        dst = f_hi[:, c, :]
                    elif kind == "q":
                        dst, scale = q_hi[:, c, :], 0.125
                    elif kind == "k":
                        dst = k_hi[:, c, :]
                    elif kind == "v":
                        dst, src = v_hi[:, c % 4, 256 * (c // 4):256 * (c // 4) + 256], ps[:, bank, 0:256]
                    elif kind == "fc":
                        dst = fc_hi[:, c, :]
                    elif kind == "four":
                        dst = h_hi[:, 2 + c, :]
                    else:
                        dst, scale = h_hi[:, c, :], v1[:, G_POOL + c:G_POOL + c + 1]
                    act.activation(dst, src, ACT.Copy, scale=scale).then_inc(unit_hi, 1)
                    if ends is not None:
                        split(p0 + ends + 2, (ends + 1) % 2)

                def head_bias(h):
                    if h >= 2:
                        act.wait_ge(s_max, UNITS1 * l + TB * (h - 1))
                    act.activation(bias[:, h % 2, :], dist_sb[:], ACT.Copy, scale=-SLOPES[h]).then_inc(bias_ready, 1)

                u0 = UNITS1 * l
                act.wait_ge(in_mix, 32 * l + 32)
                head_bias(0)
                act.wait_ge(unit_lo, NU * l + NU)
                for s in range(UNITS1 + 6):
                    if s < UNITS1:
                        act.wait_ge(s_max, u0 + s + 1)
                        for j in range(2):
                            ins = act.activation(prob1[:, s % 2, j, :], prob1[:, s % 2, j, :], ACT.Exp,
                                                 bias=nmx[:, s % 2, j:j + 1], accum_out=ssum[:, s % 2, j:j + 1])
                        ins.then_inc(s_exp, 1)
                        if s % TB == 0 and s // TB + 1 < HEADS1:
                            head_bias(s // TB + 1)
                    if 2 <= s <= UNITS1 + 1:
                        u = s - 2
                        h, b = units1[u]
                        act.wait_ge(s_tr, u0 + u + 1)
                        if b == 0 and h:
                            act.wait_ge(s_o, HEADS1 * l + h)
                        act.activation(at_hi[:, :, P * b:P * b + P],
                                       ps[:, 4 + u % 2, :].rearrange("p (k n) -> p k n", k=TB),
                                       ACT.Copy).then_inc(s_thi, 1)
                    if s >= 4 and (s - 4) % TB == TB - 1 and s - 4 < UNITS1:
                        h = (s - 4) // TB
                        act.wait_ge(s_o, HEADS1 * l + h + 1)
                        act.activation(sq[:, 0, :], ps[:, 6, :], ACT.Square).then_inc(s_osq, 1)
                    if s >= 5 and (s - 5) % TB == TB - 1 and s - 5 < UNITS1:
                        h = (s - 5) // TB
                        act.wait_ge(s_osum, HEADS1 * l + h + 1)
                        guesses(ps[:, 7, :], T, s_oguess)
                for j in range(OUT_PANELS - 1):
                    split_after(p0 + MIX_PANELS + j, (j + 1) % 2)

            def head_norm_in(j, bank, width, gain):
                w = slice(0, width)
                if isinstance(gain, int):
                    g = v2[:, gain:gain + 1]
                else:
                    g = v2[:, bass.ds(gain, 1)]
                act.activation(xs[:, j, w], ps[:, bank, w], ACT.Copy, scale=g)
                act.activation(sq[:, j, w], ps[:, bank, w], ACT.Square).then_inc(hn_in, 1)

            def mean_square(i, j, bank, width):
                w = slice(0, width)
                act.wait_ge(hn_mm, i + 1)
                act.activation(ms[:, j, w], ps[:, bank, w], ACT.Identity, bias=eps).then_inc(hn_ms, 1)

            def attend(u0, widths, biased, o0, produce):
                n = len(widths)
                for s in range(n + 2):
                    produce(s)
                    if s < n:
                        act.wait_ge(t_max, u0 + s + 1)
                        w = slice(0, widths[s])
                        src = prob2[:, s % 2, w] if biased else ps[:, s % 2, w]
                        act.activation(prob2[:, s % 2, w], src, ACT.Exp, bias=nmx[:, s % 2, 0:1],
                                       accum_out=ssum[:, s % 2, 0:1]).then_inc(t_exp, 1)
                    if s >= 2:
                        u = s - 2
                        b, kbs = u % TB, widths[u] // P
                        act.wait_ge(t_tr, u0 + u + 1)
                        if b == 0 and u:
                            act.wait_ge(t_o, o0 + u // TB)
                        act.activation(pt_hi[:, 0:kbs, P * b:P * b + P],
                                       ps[:, 2 + u % 2, 0:P * kbs].rearrange("p (k n) -> p k n", k=kbs),
                                       ACT.Copy).then_inc(t_thi, 1)

            def producer(l, gi, p):
                G = GROUPS * l + gi

                def step(s):
                    if s == 2:
                        act.wait_ge(chunk_ready, 2 * G + 1)
                        act.wait_ge(hn_out, G)
                        head_norm_in(0, 4, T, G_QK + 2 * gi)
                    if s == 3:
                        mean_square(2 * G, 0, 7, T)
                    if s == 4:
                        act.wait_ge(panel_done, p + 1)
                        head_norm_in(1, 4, T, G_QK + 2 * gi + 1)
                        split(p + 2, 0)
                    if s == 5:
                        mean_square(2 * G + 1, 1, 7, T)
                        act.drain()
                        pair_guesses(T)
                    if s == 6:
                        act.wait_ge(chunk_ready, 2 * G + 2)
                        act.activation(hraw[:, 0, :], ps[:, 4, :], ACT.Copy).then_inc(v_in, 1)
                    if s == 8:
                        act.wait_ge(panel_done, p + 2)
                        if isinstance(gi, int):
                            dst = y[:, gi - 2, :]
                        else:
                            dst = y[:, bass.ds(gi - 2, 1), :]
                        act.activation(dst, ps[:, 4, :], ACT.Silu).then_inc(g_in, 1)
                        split(p + 3, 1)
                return step

            def pair_attention(l, gi, produce):
                o0 = 16 * l + 4 + 2 * (gi - 2)

                def step(s):
                    produce(s)
                    if s == 1:
                        act.wait_ge(t_o, o0)
                        act.wait_ge(v_tr, 7 * l + gi)
                        for h in range(2):
                            ins = act.activation(
                                vp_hi[:, :, h, 64 * h:64 * h + 64],
                                ps[:, 6, :].rearrange("p (t n) -> p t n", t=TB)[:, :, 64 * h:64 * h + 64], ACT.Copy)
                        ins.then_inc(v_thi, 1)
                attend(UNITS2 * l + 16 + PAIR_UNITS * (gi - 2), [P * (b + 1) for _ in range(2) for b in range(TB)],
                       True, o0, step)

            def stack2(l):
                p0 = BASE2 + LAYER2_PANELS * l
                g0 = GROUPS * l
                norm(3 * LAYERS + 1 + l)
                act.wait_ge(chunk_ready, 2 * g0 + 1)
                head_norm_in(0, 0, 256, G_QK)
                act.wait_ge(panel_done, p0 + 1)
                head_norm_in(1, 1, 256, G_QK + 1)
                split(p0 + 2, 0)
                act.wait_ge(h_ready, 8 * (3 * LAYERS + 1 + l))
                mean_square(2 * g0, 0, 5, 256)
                mean_square(2 * g0 + 1, 1, 7, 256)
                act.drain()
                pair_guesses(256)
                act.wait_ge(chunk_ready, 2 * g0 + 2)
                act.activation(hraw[:, 0, 0:256], ps[:, 2, 0:256], ACT.Copy)
                act.wait_ge(panel_done, p0 + 2)
                act.activation(hraw[:, 1, 0:256], ps[:, 3, 0:256], ACT.Copy).then_inc(v_in, 1)
                split(p0 + 3, 1)
                act.wait_ge(v_tr, 7 * l + 1)
                for h in range(2):
                    ins = act.activation(
                        vm_hi[:, :, :, h, 64 * h:64 * h + 64],
                        ps[:, 4, :].rearrange("p (t c n) -> p t c n", t=2, c=2)[:, :, :, 64 * h:64 * h + 64], ACT.Copy)
                ins.then_inc(v_thi, 1)
                act.wait_ge(chunk_ready, 2 * g0 + 3)
                act.wait_ge(hn_out, g0 + 1)
                head_norm_in(0, 0, T, G_QK + 2)
                act.wait_ge(panel_done, p0 + 3)
                head_norm_in(1, 1, T, G_QK + 3)
                split(p0 + 4, 0)
                mean_square(2 * g0 + 2, 0, 5, T)
                mean_square(2 * g0 + 3, 1, 7, T)
                act.drain()
                pair_guesses(T)
                act.wait_ge(chunk_ready, 2 * g0 + 4)
                act.activation(y[:, 6, :], ps[:, 2, :], ACT.Silu)
                act.wait_ge(panel_done, p0 + 4)
                act.activation(y[:, 7, :], ps[:, 3, :], ACT.Silu).then_inc(g_in, 1)
                split(p0 + 5, 1)
                attend(UNITS2 * l, [256] * 16, False, 16 * l, producer(l, 2, p0 + 4))
                for first, count in ((2, 3), (5, 2)):
                    with act.Fori(0, count) as j:
                        gi = first + j
                        pair_attention(l, gi, producer(l, gi + 1, p0 + 2 * (gi + 1)))
                pair_attention(l, 7, lambda s: None)
                for j in range(OUT_PANELS):
                    split_after(p0 + 2 * GROUPS + j, j % 2)

            act.dma_start(x_sb[:].rearrange("p k n -> p (k n)"), x).then_inc(in_x, 16)
            for dst, src in ((cst, consts), (v1_all, vecs1), (v2_all, vecs2), (fin_g, final_g)):
                act.dma_start(dst[:], src).then_inc(in_small, 16)
            act.dma_start(hraw[0:64, 1, 0:8], lamv).then_inc(in_small, 16)
            for s in range(2):
                split(s, s)
            act.wait_ge(lam_mm, 1)
            act.activation(hraw[:, 1, 8:12], ps[:, 7, 0:4], ACT.Exp).then_inc(lam_exp, 1)
            norm(0)
            with act.Fori(0, LAYERS) as l:
                p0 = LAYER1_PANELS * l
                feed_forward(p0, 0)
                norm(3 * l + 1)
                split_after(p0 + FFN_PANELS - 1, 0)
                mixer1(l, p0 + FFN_PANELS)
                norm(3 * l + 2)
                split_after(p0 + LAYER1_PANELS - FFN_PANELS - 1, 0)
                feed_forward(p0 + LAYER1_PANELS - FFN_PANELS, 1)
                norm(3 * l + 3)
                split_after(p0 + LAYER1_PANELS - 1, 1)
            act.dma_start(mask[:].rearrange("p a n -> p (a n)"), masks).then_inc(in_two, 16)
            act.dma_start(rope_sb[:].rearrange("p a n -> p (a n)"), rope).then_inc(in_two, 16)
            act.dma_start(memn[:].rearrange("p k n -> p (k n)"), mem).then_inc(in_two, 16)
            act.wait_ge(in_two, 48)
            for i in range(KB):
                if i >= 2:
                    act.wait_ge(mem_sum, i - 1)
                act.activation(sq[:, i % 2, 0:256], memn[:, i, :], ACT.Square).then_inc(mem_sq, 1)
            act.wait_ge(mem_sum, KB)
            act.wait_ge(x_ready, 8 * (3 * LAYERS + 2))
            guesses(ps[:, 5, 0:256], 256, mem_guess)
            act.wait_ge(mem_normed, 1)
            with act.Fori(0, LAYERS) as l:
                stack2(l)

        @block.vector
        def _(dve):
            rstd = guess[:, 0, :]

            def newton(width, slots=1):
                at = (slice(None), slice(0, slots), slice(0, width))
                dve.tensor_tensor(newt[at], ms[at], newt[at], ALU.mult)
                dve.drain()
                dve.tensor_scalar(newt[at], newt[at], -0.5, 1.5, ALU.mult, ALU.add)
                dve.drain()
                dve.tensor_tensor(guess[at], newt[at], guess[at], ALU.mult)
                dve.drain()

            def remainder(dst, src, hi):
                return dve.tensor_tensor(dst, src, hi.bitcast(F32), ALU.subtract)

            def norm(n, gain):
                dve.wait_ge(guess_ready, n + 1)
                newton(T)

                wholes = [hraw[:, 0, :], hraw[:, 1, :], newt[:, 1, :]]

                def whole(k):
                    dve.scalar_tensor_tensor(out=wholes[k % 3], in0=x_sb[:, k, :], scalar=gain[:, k:k + 1],
                                             in1=rstd, op0=ALU.mult, op1=ALU.mult)
                whole(0)
                dve.drain()
                for k in range(KB):
                    dve.tensor_copy(h_hi[:, k, :], wholes[k % 3])
                    if k + 1 < KB:
                        whole(k + 1)
                    dve.drain()
                    remainder(h_lo[:, k, :], wholes[k % 3], h_hi[:, k, :]).then_inc(h_ready, 1)

            def update(o0, last_panel, scale):
                for i, m in enumerate(OUT_ORDER):
                    at = last_panel(i)
                    if at is not None:
                        dve.wait_ge(panel_done, at)
                    else:
                        dve.wait_ge(out_ready, o0(i))
                    dve.scalar_tensor_tensor(out=x_sb[:, m, :], in0=ps[:, m, :], scalar=scale, in1=x_sb[:, m, :],
                                             op0=ALU.mult, op1=ALU.add).then_inc(x_ready, 1)

            def feed_forward(n, F, p0, gain, o0):
                norm(n, gain)
                with dve.Fori(0, FB // 2) as i:
                    for e in range(2):
                        dve.wait_ge(silu_ready, FB * F + 2 * i + e + 1)
                        c = bass.ds(2 * i + e, 1)
                        dve.tensor_tensor(sq[:, e, :], hraw[:, e, :], ps[:, 2 * e + 1, :], ALU.mult)
                        dve.drain()
                        dve.tensor_copy(hid_hi[:, c, :], sq[:, e:e + 1, :])
                        dve.drain()
                        remainder(hid_lo[:, c, :], sq[:, e:e + 1, :], hid_hi[:, c, :]).then_inc(hid_ready, 1)
                update(lambda i: o0 + i + 1, lambda i: p0 + FFN_PANELS if i == KB - 1 else None, 0.5)

            def project_out(p0, o0):
                update(lambda i: o0 + i // 2 + 1, lambda i: p0 + i // 2 + 1 if i % 2 else None, 1.0)

            def pool_block(l, c):
                n = T + 2 * PAD
                up = slice(64, P)
                a = apad[:, c, :]

                def step(dst, src, d, rows=slice(0, P), lo=0):
                    ins = dve.tensor_tensor(dst[rows, lo + d:n - d], src[rows, lo:n - 2 * d], src[rows, lo + 2 * d:n],
                                            ALU.add)
                    dve.drain()
                    return ins
                w0, w1 = win[:, 0, :], win[:, 1, :]
                dve.tensor_tensor(w0[:, 1:n], a[:, 0:n - 1], a[:, 1:n], ALU.add).then_inc(unit_lo, 1)
                dve.drain()
                if c == 0:
                    dve.tensor_tensor(w1[up, 2:n - 1], w0[up, 1:n - 2], w0[up, 3:n], ALU.add)
                else:
                    dve.tensor_tensor(w1[:, 2:n - 1], w0[:, 1:n - 2], w0[:, 3:n], ALU.add)
                    dve.drain()
                    dve.tensor_tensor(w0[:, 4:n - 3], w1[:, 2:n - 5], w1[:, 6:n - 1], ALU.add)
                    dve.drain()
                    dve.tensor_tensor(w1[up, 8:n - 7], w0[up, 4:n - 11], w0[up, 12:n - 3], ALU.add)
                dve.drain()
                t = slice(PAD, PAD + T)
                if c == 0:
                    dve.wait_ge(in_mix, 32 * l + 32)
                for rows, w in ((slice(0, 64), w0), (up, w1)):
                    dve.tensor_tensor(hraw[rows, c, :], w[rows, t], rec_sb[rows, c, :], ALU.mult)
                dve.drain()
                dve.tensor_tensor(hraw[:, c, :], hraw[:, c, :], a[:, t], ALU.subtract)
                dve.drain()
                dve.tensor_copy(m_hi[:, c, :], hraw[:, c, :])
                dve.drain()
                remainder(m_lo[:, c, :], hraw[:, c, :], m_hi[:, c, :]).then_inc(pooled, 1)

            def mixer1(l, n, p0):
                norm(n, v1[:, G_MIX:G_MIX + KB])
                dve.memset(apad[:, :, 0:PAD], 0.0)
                dve.memset(apad[:, :, PAD + T:], 0.0)
                dve.drain()
                for i, (kind, c, bank, _) in enumerate(MIX_UNITS):
                    dve.wait_ge(unit_hi, NU * l + i + 1)
                    src = ps[:, bank, :]
                    if kind == "a":
                        pool_block(l, c)
                        continue
                    if kind in ("f", "yf"):
                        ins = remainder(f_lo[:, c, :], src, f_hi[:, c, :])
                    elif kind == "q":
                        ins = dve.scalar_tensor_tensor(out=q_lo[:, c, :], in0=src, scalar=0.125,
                                                       in1=q_hi[:, c, :].bitcast(F32), op0=ALU.mult, op1=ALU.subtract)
                    elif kind == "k":
                        ins = remainder(k_lo[:, c, :], src, k_hi[:, c, :])
                    elif kind == "v":
                        s = slice(256 * (c // 4), 256 * (c // 4) + 256)
                        ins = remainder(v_lo[:, c % 4, s], ps[:, bank, 0:256], v_hi[:, c % 4, s])
                    elif kind == "fc":
                        ins = remainder(fc_lo[:, c, :], src, fc_hi[:, c, :])
                    elif kind == "four":
                        ins = remainder(h_lo[:, 2 + c, :], src, h_hi[:, 2 + c, :])
                    else:
                        ins = dve.scalar_tensor_tensor(out=h_lo[:, c, :], in0=src,
                                                       scalar=v1[:, G_POOL + c:G_POOL + c + 1],
                                                       in1=h_hi[:, c, :].bitcast(F32), op0=ALU.mult, op1=ALU.subtract)
                    ins.then_inc(unit_lo, 1)
                u0 = UNITS1 * l
                for s in range(UNITS1 + 7):
                    if s < UNITS1:
                        h, b = units1[s]
                        dve.wait_ge(s_scores, u0 + s + 1)
                        if b == 0:
                            dve.wait_ge(bias_ready, HEADS1 * l + h + 1)
                        if s >= 2:
                            dve.wait_ge(s_att, u0 + s - 1)
                        dve.memset(tick[:], 0.0)
                        for j in range(2):
                            dve.tensor_tensor_reduce(prob1[:, s % 2, j, :], ps[:, 2 * (s % 2) + j, :],
                                                     bias[:, h % 2, T - P - P * b:2 * T - P - P * b],
                                                     1.0, -3e38, ALU.add, ALU.max, mx[:, s % 2, j:j + 1])
                        dve.drain()
                        dve.tensor_scalar(nmx[:, s % 2, :], mx[:, s % 2, :], -1.0, None, ALU.mult).then_inc(s_max, 1)
                    if 1 <= s <= UNITS1:
                        u = s - 1
                        dve.wait_ge(s_exp, u0 + u + 1)
                        if u >= 2:
                            dve.wait_ge(s_tr, u0 + u - 1)
                        dve.reciprocal(rsum[:, u % 2, :], ssum[:, u % 2, :])
                        dve.drain()
                        dve.tensor_scalar(att1[:, u % 2, :], prob1[:, u % 2, 0, :], rsum[:, u % 2, 0:1], None, ALU.mult)
                        dve.tensor_tensor(rsum[:, u % 2, 1:2], rsum[:, u % 2, 1:2], nlam[:], ALU.mult)
                        dve.drain()
                        dve.scalar_tensor_tensor(out=att1[:, u % 2, :], in0=prob1[:, u % 2, 1, :],
                                                 scalar=rsum[:, u % 2, 1:2], in1=att1[:, u % 2, :],
                                                 op0=ALU.mult, op1=ALU.add).then_inc(s_att, 1)
                    if 3 <= s <= UNITS1 + 2:
                        u = s - 3
                        q = slice(P * units1[u][1], P * units1[u][1] + P)
                        dve.wait_ge(s_thi, u0 + u + 1)
                        remainder(at_lo[:, :, q], ps[:, 4 + u % 2, :].rearrange("p (k n) -> p k n", k=TB),
                                  at_hi[:, :, q]).then_inc(s_tlo, 1)
                    if s >= 6 and (s - 6) % TB == TB - 1 and s - 6 < UNITS1:
                        h = (s - 6) // TB
                        dve.wait_ge(s_oguess, HEADS1 * l + h + 1)
                        newton(T)
                        dve.scalar_tensor_tensor(out=hraw[:, 0, :], in0=ps[:, 6, :], scalar=v1[:, G_HEAD + h:G_HEAD + h + 1],
                                                 in1=rstd, op0=ALU.mult, op1=ALU.mult)
                        dve.drain()
                        dve.tensor_copy(h_hi[:, 4 + h, :], hraw[:, 0, :])
                        dve.drain()
                        remainder(h_lo[:, 4 + h, :], hraw[:, 0, :], h_hi[:, 4 + h, :]).then_inc(s_y, 1)
                project_out(p0 + MIX_PANELS, 18 * l + KB - 1)

            def head_norm(G, width, scales):
                dve.wait_ge(hn_guess, G + 1)
                newton(width, 2)
                w = slice(0, width)
                for j in range(2):
                    dve.scalar_tensor_tensor(out=xs[:, j, w], in0=xs[:, j, w], scalar=scales[j], in1=guess[:, j, w],
                                             op0=ALU.mult, op1=ALU.mult)
                dve.drain()

            def head_split(width, dst_hi, dst_lo):
                w = slice(0, width)
                dve.tensor_copy(dst_hi[:, :, w], xs[:, :, w])
                dve.drain()
                remainder(dst_lo[:, :, w], xs[:, :, w], dst_hi[:, :, w]).then_inc(hn_out, 1)

            def attend(u0, widths, branch, produce, gated):
                n = len(widths)
                for s in range(n + 4):
                    if s < n:
                        w, b = slice(0, widths[s]), s % TB
                        dve.wait_ge(t_scores, u0 + s + 1)
                        if s >= 2:
                            dve.wait_ge(t_att, u0 + s - 1)
                        if branch is None:
                            dve.tensor_reduce(mx[:, s % 2, 0:1], ps[:, s % 2, w], AX_X, ALU.max)
                        else:
                            dve.memset(tick[:], 0.0)
                            dve.tensor_tensor_reduce(prob2[:, s % 2, w], ps[:, s % 2, w],
                                                     mask[:, branch, T - P - P * b:T],
                                                     1.0, -3e38, ALU.add, ALU.max, mx[:, s % 2, 0:1])
                        dve.drain()
                        dve.tensor_scalar(nmx[:, s % 2, 0:1], mx[:, s % 2, 0:1], -1.0, None, ALU.mult).then_inc(t_max, 1)
                    if 1 <= s <= n:
                        u = s - 1
                        w = slice(0, widths[u])
                        dve.wait_ge(t_exp, u0 + u + 1)
                        if u >= 2:
                            dve.wait_ge(t_tr, u0 + u - 1)
                        dve.reciprocal(rsum[:, u % 2, 0:1], ssum[:, u % 2, 0:1])
                        dve.drain()
                        dve.tensor_scalar(att2[:, u % 2, w], prob2[:, u % 2, w], rsum[:, u % 2, 0:1], None,
                                          ALU.mult).then_inc(t_att, 1)
                    if 3 <= s <= n + 2:
                        u = s - 3
                        q, kbs = slice(P * (u % TB), P * (u % TB) + P), widths[u] // P
                        dve.wait_ge(t_thi, u0 + u + 1)
                        remainder(pt_lo[:, 0:kbs, q], ps[:, 2 + u % 2, 0:P * kbs].rearrange("p (k n) -> p k n", k=kbs),
                                  pt_hi[:, 0:kbs, q]).then_inc(t_tlo, 1)
                    produce(s)
                    if s >= 4 and (s - 4) % PAIR_UNITS == PAIR_UNITS - 1:
                        gated((s - 4) // PAIR_UNITS)

            def producer(l, gi, n, u0):
                G = GROUPS * l + gi

                def step(s):
                    if s in (4, 6):
                        j = (s - 4) // 2
                        dve.wait_ge(hn_mm, 2 * G + j + 1)
                        dve.tensor_tensor(xs[:, j, :], xs[:, j, :], rope_sb[:, 0, :], ALU.mult)
                        dve.tensor_tensor(hraw[:, 1, :], ps[:, 6, :], rope_sb[:, 1, :], ALU.mult)
                        dve.drain()
                        dve.tensor_tensor(xs[:, j, :], xs[:, j, :], hraw[:, 1, :], ALU.add).then_inc(hn_rot, 1)
                    if s == 7:
                        head_norm(G, T, (0.125, 1.0))
                    if s == n:
                        dve.wait_ge(t_scores, u0 + n)
                        head_split(T, qk_hi, qk_lo)
                return step

            def pair_attention(l, gi, branch, produce):
                def step(s):
                    if s == 1:
                        dve.wait_ge(v_thi, 7 * l + gi)
                        for h in range(2):
                            c = slice(64 * h, 64 * h + 64)
                            ins = remainder(vp_lo[:, :, h, c], ps[:, 6, :].rearrange("p (t n) -> p t n", t=TB)[:, :, c],
                                            vp_hi[:, :, h, c])
                        ins.then_inc(v_tlo, 1)
                    produce(s)

                def gated(_):
                    dve.wait_ge(t_o, 16 * l + 4 + 2 * (gi - 1))
                    c = slice(gi - 2, gi - 1) if isinstance(gi, int) else bass.ds(gi - 2, 1)
                    dve.tensor_tensor(y[:, c, :], y[:, c, :], ps[:, 5:6, :], ALU.mult).then_inc(t_y, 1)

                attend(UNITS2 * l + 16 + PAIR_UNITS * (gi - 2), [P * (b + 1) for _ in range(2) for b in range(TB)],
                       branch, step, gated)

            def stack2(l):
                n = 3 * LAYERS + 1 + l
                p0 = BASE2 + LAYER2_PANELS * l
                g0 = GROUPS * l
                dve.tensor_copy(v2[:], v2_all[:, bass.ds(NV2 * l, NV2)])
                dve.drain()
                for k in range(KB):
                    g = v2[:, G_MEM + k:G_MEM + k + 1]
                    dve.tensor_scalar(mh_hi[:, k, :], memn[:, k, :], g, None, ALU.mult)
                    dve.drain()
                    dve.scalar_tensor_tensor(out=mh_lo[:, k, :], in0=memn[:, k, :], scalar=g,
                                             in1=mh_hi[:, k, :].bitcast(F32), op0=ALU.mult,
                                             op1=ALU.subtract).then_inc(memh_ready, 1)
                norm(n, v2[:, G_NORM:G_NORM + KB])
                head_norm(g0, 256, (1.0, 1.0))
                head_split(256, km_hi, km_lo)
                dve.wait_ge(v_thi, 7 * l + 1)
                for h in range(2):
                    s = slice(64 * h, 64 * h + 64)
                    ins = remainder(vm_lo[:, :, :, h, s],
                                    ps[:, 4, :].rearrange("p (t c n) -> p t c n", t=2, c=2)[:, :, :, s],
                                    vm_hi[:, :, :, h, s])
                ins.then_inc(v_tlo, 1)
                head_norm(g0 + 1, T, (0.125, 0.125))
                head_split(T, qk_hi, qk_lo)

                def gated_mem(c):
                    dve.wait_ge(t_o, 16 * l + 2 * c + 2)
                    dve.tensor_tensor(y[:, 6 + c, :], y[:, 6 + c, :], ps[:, 5, :], ALU.mult).then_inc(t_y, 1)

                u0 = UNITS2 * l
                attend(u0, [256] * 16, None, producer(l, 2, 16, u0), gated_mem)
                for branch, first, count in ((0, 2, 3), (1, 5, 2)):
                    with dve.Fori(0, count) as j:
                        gi = first + j
                        pair_attention(l, gi, branch,
                                       producer(l, gi + 1, PAIR_UNITS, u0 + 16 + PAIR_UNITS * (gi - 2)))
                pair_attention(l, 7, 1, lambda s: None)
                dve.drain()
                dve.tensor_copy(h_hi[:, 0, :], y[:, 0, :])
                for k in range(KB):
                    dve.drain()
                    if k + 1 < KB:
                        dve.tensor_copy(h_hi[:, k + 1, :], y[:, k + 1, :])
                    remainder(h_lo[:, k, :], y[:, k, :], h_hi[:, k, :]).then_inc(y_ready, 1)
                project_out(p0 + 2 * GROUPS, 18 * LAYERS + OUT_PANELS * l)

            dve.wait_ge(in_small, 16 * 5)
            dve.memset(newt[0:64, 0, 0:P], 1.0)
            dve.drain()
            dve.tensor_tensor(hraw[0:64, 0, 0:4], hraw[0:64, 1, 0:4], hraw[0:64, 1, 4:8], ALU.mult).then_inc(lam_in, 1)
            dve.wait_ge(lam_exp, 1)
            e = hraw[:, 1, 8:12].rearrange("p (l n) -> p l n", l=LAYERS)
            dve.tensor_tensor(nlam_all[:], e[:, :, 1], e[:, :, 0], ALU.subtract)
            dve.drain()
            dve.tensor_tensor(nlam_all[:], nlam_all[:],
                              v1_all[:].rearrange("p (l n) -> p l n", l=LAYERS)[:, :, G_LAM], ALU.subtract)
            dve.wait_ge(in_x, 16)
            for i in range(KB):
                dve.engine_nop().then_inc(x_ready, 1)
            with dve.Fori(0, LAYERS) as l:
                p0 = LAYER1_PANELS * l
                dve.drain()
                dve.tensor_copy(v1[:], v1_all[:, bass.ds(NV1 * l, NV1)])
                dve.tensor_copy(nlam[:], nlam_all[:, bass.ds(l, 1)])
                dve.drain()
                dve.tensor_scalar(v1[:, G_HEAD:G_HEAD + HEADS1], v1[:, G_HEAD:G_HEAD + HEADS1],
                                  v1[:, G_KEEP:G_KEEP + 1], None, ALU.mult)
                feed_forward(3 * l, 2 * l, p0, v1[:, G_FFN1:G_FFN1 + KB], 18 * l)
                mixer1(l, 3 * l + 1, p0 + FFN_PANELS)
                feed_forward(3 * l + 2, 2 * l + 1, p0 + LAYER1_PANELS - FFN_PANELS,
                             v1[:, G_FFN2:G_FFN2 + KB], 18 * l + KB - 1 + OUT_PANELS)
            dve.wait_ge(guess_ready, 3 * LAYERS + 1)
            newton(T)
            for m in OUT_ORDER:
                dve.scalar_tensor_tensor(out=x_sb[:, m, :], in0=x_sb[:, m, :], scalar=fin_g[:, m:m + 1], in1=rstd,
                                         op0=ALU.mult, op1=ALU.mult).then_inc(x_ready, 1)
            for z in (vp_hi, vp_lo, vm_hi, vm_lo):
                dve.memset(z[:].bitcast(F32), 0.0)
            dve.drain()
            dve.wait_ge(mem_guess, 1)
            newton(256)
            for k in range(KB):
                ins = dve.tensor_tensor(memn[:, k, :], memn[:, k, :], guess[:, 0, 0:256], ALU.mult)
            ins.then_inc(mem_normed, 1)
            dve.drain()
            with dve.Fori(0, LAYERS) as l:
                stack2(l)


def blocks(w, cols):
    r, n = w.shape
    return w.reshape(r // P, P, n // cols, cols).transpose(2, 1, 0, 3).reshape(n // cols, P, -1)


def weight_stream(inp, const):
    out = np.zeros((ALL_PANELS + SPARE_PANELS, P, PANEL), np.float32)
    at = 0

    def put(panels):
        nonlocal at
        out[at:at + len(panels), :, :panels.shape[2]] = panels
        at += len(panels)

    def feed_forward(gate, up, down):
        both = np.stack([gate.reshape(D, FB, P), up.reshape(D, FB, P)], 2).reshape(D, 2 * FF)
        put(blocks(both, 2 * P))
        put(down.reshape(DOWN_PANELS, 2, P, D).transpose(0, 2, 1, 3).reshape(DOWN_PANELS, P, PANEL))

    def out_blocks(w):
        put(blocks(w.reshape(D, KB, P)[:, OUT_ORDER].reshape(D, D), 2 * P))

    for l in range(LAYERS):
        feed_forward(inp["ffn1_w_gate"][l], inp["ffn1_w_up"][l], inp["ffn1_w_down"][l])
        put(blocks(inp["w_in"][l], 2 * P))
        put(const["chan"][None])
        put(const["seq"])
        four = inp["fourier_w"][l].reshape(2, P, 2 * P).transpose(1, 0, 2).reshape(P, 4 * P)
        pool = np.zeros((P, 2, P), np.float32)
        for g in range(4):
            s = slice(64 * (g % 2), 64 * (g % 2) + 64)
            pool[s, g // 2, s] = inp["pool_w"][l][g]
        put(np.concatenate([four, pool.reshape(P, 2 * P)], 1)[None])
        out_blocks(inp["w_out"][l])
        feed_forward(inp["ffn2_w_gate"][l], inp["ffn2_w_up"][l], inp["ffn2_w_down"][l])
    for l in range(LAYERS):
        w = inp["w_in_2"][l]
        put(blocks(inp["w_mem_kv_2"][l], 2 * P))
        put(blocks(w[:, 3072:3584], 2 * P))
        for branch in range(2):
            for j in range(3):
                q, k, v, g = (w[:, 1536 * branch + 384 * i + P * j:][:, :P] for i in range(4))
                put(blocks(np.concatenate([q, k, v, g], 1), 2 * P))
        out_blocks(inp["w_out_2"][l])
    assert at == ALL_PANELS
    return out


def columns(v):
    return v.reshape(-1, P).T


def kernel(**inputs):
    import concourse.bacc as bacc
    from concourse.bass_utils import run_bass_kernel_spmd as run

    inp = {k: np.asarray(v) for k, v in inputs.items()}
    const = shape_constants()
    start = [0.8 - 0.6 * math.exp(-0.3 * l) for l in range(LAYERS)]
    f = np.float32
    vecs1 = [np.concatenate([
        columns(inp["ffn1_norm"][l]), columns(inp["mix_norm"][l]), columns(inp["ffn2_norm"][l]),
        columns(inp["pool_scale"][l]), columns(inp["attn_head_norm"][l]),
        np.full((P, 1), 1.0 - start[l], f), np.full((P, 1), start[l], f)], 1) for l in range(LAYERS)]
    vecs2 = [np.concatenate([
        columns(inp["norm_g_2"][l]), columns(inp["mem_norm_g_2"][l]),
        np.concatenate([inp["qk_g_2"][l][[5, 5, 4, 4] + 3 * [0, 1] + 3 * [2, 3]].T] * 2, 0)], 1) for l in range(LAYERS)]
    lamv = np.stack([inp[n][l] for a in "qk" for l in range(LAYERS) for n in (f"lam_{a}1", f"lam_{a}2")], 1)
    feature_major = lambda a: a[0].T.reshape(KB, P, -1).transpose(1, 0, 2).reshape(P, -1)
    arrays = {
        "x": feature_major(inp["x"]), "mem": feature_major(inp["mem_2"]),
        "stream": weight_stream(inp, const),
        "vecs1": np.concatenate(vecs1, 1), "vecs2": np.concatenate(vecs2, 1),
        "final_g": columns(inp["final_norm"]), "lamv": lamv, "consts": const["consts"],
        "dist": const["dist"], "masks": const["masks"].reshape(P, 2, TOE)[:, :, :T].reshape(P, 2 * T),
        "recip": const["recip"], "rope": const["rope"],
    }
    arrays = {k: np.ascontiguousarray(v) for k, v in arrays.items()}
    nc = bacc.Bacc("TRN2", target_bir_lowering=False, num_devices=1)
    args = [nc.dram_tensor(f"in_{k}", a.shape, mybir.dt.from_np(a.dtype), kind="ExternalInput").ap()
            for k, a in arrays.items()]
    args.append(nc.dram_tensor("out_x", (P, KB, T), F32, kind="ExternalOutput").ap())
    names = dict(zip(arrays, args))
    build(nc, **names, out=args[-1])
    r = run(nc, [{f"in_{k}": a for k, a in arrays.items()}], core_ids=[0])
    got = np.asarray(r.results[0]["out_x"])
    return np.ascontiguousarray(got.transpose(1, 0, 2).reshape(D, T).T)[None]
```

```python
from contextlib import ExitStack
import math

import numpy as np
import concourse.bass as bass
from concourse import mybir

F32 = mybir.dt.float32
F32R = mybir.dt.float32r
ALU = mybir.AluOpType
ACT = mybir.ActivationFunctionType
AX_X = mybir.AxisListType.X

P = 128
D = 1024
T = 512
KB = D // P
TB = T // P
LAYERS = 2
FF = 2816
FB = FF // P
PANEL = 2048
EPS = 1e-6
MASKED = -1e30

UP_PANELS = FB
DOWN_PANELS = FB // 2
FFN_PANELS = UP_PANELS + DOWN_PANELS
MIX_PANELS = 12
OUT_PANELS = 4
LAYER1_PANELS = 2 * FFN_PANELS + MIX_PANELS + OUT_PANELS
GROUPS = 8
LAYER2_PANELS = 2 * GROUPS + OUT_PANELS
BASE2 = LAYERS * LAYER1_PANELS
ALL_PANELS = BASE2 + LAYERS * LAYER2_PANELS
SPARE_PANELS = 2

DOWN_ORDER = [4, 5, 6, 7, 0, 1, 2, 3]
DONE_ORDER = [0, 1, 4, 6, 7, 5, 2, 3]
SUM_BANK = 4

HEADS1 = 4
UNITS1 = HEADS1 * TB
SLOPES = [2.0 ** (-8.0 * (i + 1) / HEADS1) for i in range(HEADS1)]
PAD = 8
WINDOWS = (2, 4, 8, 16)
TOE = 2 * T - P

G_FFN1, G_MIX, G_FFN2, G_POOL, G_HEAD, G_KEEP, G_LAM, NV1 = 0, 8, 16, 24, 26, 30, 31, 32
G_NORM, G_MEM, G_QK, NV2 = 0, 8, 16, 32
C_ID, C_MEAN, C_HALF, C_HEAD, C_ROT = range(5)
NC = 5 * P + 1

MIX_ORDER = (
    [("a", c, 0) for c in range(2)]
    + [("f", c, 1 if c else None) for c in range(2)]
    + [("q", c, 2 + c // 2 if c % 2 else None) for c in range(4)]
    + [("fc", t, 4 if t == 3 else None) for t in range(4)]
    + [("k", c, 5 + c // 2 if c % 2 else None) for c in range(4)]
    + [("yf", c, 8 if c else None) for c in range(2)]
    + [("v", 4 * h + t, 9 + h if t == 3 else None) for h in range(2) for t in range(4)]
    + [("four", c, None) for c in range(2)]
    + [("pool", c, 11 if c else None) for c in range(2)]
)
MIX_UNITS = [(kind, c, i % 4, ends) for i, (kind, c, ends) in enumerate(MIX_ORDER)]
NORMED = "afqkv"
NU = len(MIX_UNITS)
NORMED_BEFORE = [sum(u[0] in NORMED for u in MIX_UNITS[:i]) for i in range(NU + 1)]
READY_BEFORE = [sum(u[3] is None for u in MIX_UNITS[:i]) for i in range(NU + 1)]
READY1 = READY_BEFORE[NU]

UNITS2 = 64
PAIR_UNITS = 2 * TB


class Stage:

    def __init__(self, l, gi, branch):
        self.l, self.gi, self.branch = l, gi, branch
        self.memory = branch is None
        self.last = isinstance(gi, int) and gi == GROUPS - 1
        if self.memory:
            self.n, self.widths = 4 * TB, [256] * (4 * TB)
            self.u0, self.heads0 = UNITS2 * l, 16 * l
        else:
            self.n, self.widths = PAIR_UNITS, [P * (b + 1) for _ in range(2) for b in range(TB)]
            self.u0 = UNITS2 * l + 4 * TB + PAIR_UNITS * (gi - 2)
            self.heads0 = 16 * l + 4 + 2 * (gi - 2)


LAG_TR = 3
LAG_OUT = 4
LAG_GATE = 5

Y_ORDER = [6, 7, 0, 1, 2, 3, 4, 5]


def lagged(here, before, s, lag):
    i = s - lag
    if i < 0:
        return (before, before.n + i) if before else None
    return (here, i) if here and i < here.n else None


def run_stages(l, fori, step, producer, last=None, tail=None):
    def stage(here, before, produce):
        steps = here.n if here else LAG_GATE + 1
        for s in range(steps):
            if here and here.memory:
                step(here, before, s, produce, s // 2 if s % 2 == 0 else None)
            else:
                step(here, before, s, produce, s)
    memory = Stage(l, 1, None)
    stage(memory, None, producer(l, 2, memory))
    pair = Stage(l, 2, 0)
    stage(pair, memory, producer(l, 3, pair))
    for first, branch in ((3, 0), (5, 1)):
        with fori(0, 2) as j:
            pair = Stage(l, first + j, branch)
            stage(pair, Stage(l, first - 1 + j, branch), producer(l, first + 1 + j, pair))
    pair = Stage(l, 7, 1)
    stage(pair, Stage(l, 6, 1), last)
    stage(None, pair, tail)


def shape_constants():
    i = np.arange(P)
    consts = np.zeros((P, NC), np.float64)
    consts[:, C_ID * P:(C_ID + 1) * P] = np.eye(P)
    consts[:, C_MEAN * P:(C_MEAN + 1) * P] = 1.0 / D
    consts[:, C_HALF * P:(C_HALF + 1) * P] = (i[:, None] // 64 == i[None] // 64) / 64.0
    consts[:, C_HEAD * P:(C_HEAD + 1) * P] = 1.0 / P
    rot = np.zeros((P, P))
    for m in range(P):
        if m % 64 < 32:
            rot[m + 32, m] = -1.0
        else:
            rot[m - 32, m] = 1.0
    consts[:, C_ROT * P:(C_ROT + 1) * P] = rot
    consts[:, NC - 1] = EPS
    lag = i[:, None] + (T - P) - np.arange(TOE)[None]
    dist = np.abs(lag)
    causal = np.where(lag >= 0, 0.0, MASKED)
    count = ((lag <= 128).astype(int) + (lag % 4 == 0) + (lag % 16 == 0)) * (lag >= 0)
    dilated = np.where(count > 0, np.log(np.maximum(count, 1)), MASKED)
    t = np.arange(T)
    recip = np.zeros((P, 2, T))
    for g, w in enumerate(WINDOWS):
        cnt = np.minimum(t + w - 1 - w // 2 + 1, T) - np.maximum(t - w // 2, 0)
        recip[64 * (g % 2):64 * (g % 2) + 64, g // 2] = 1.0 / cnt
    inv = (10000.0 ** (-np.arange(32, dtype=np.float32) / np.float32(32))).astype(np.float32)
    ang = (t.astype(np.float32)[:, None] * inv[None]).astype(np.float32).astype(np.float64)
    rope = np.stack([np.cos(ang).T[i % 32], np.sin(ang).T[i % 32]], 1)
    c64 = 2 * np.pi * np.outer(np.arange(64), np.arange(64)) / 64
    chan = np.zeros((P, 2, P))
    for g in range(2):
        s = slice(64 * g, 64 * g + 64)
        chan[s, 0, s] = np.cos(c64) / 8
        chan[s, 1, s] = np.sin(c64) / 8
    cs = 2 * np.pi * (np.outer(t, t) % T) / T
    seq = np.stack([np.cos(cs), -np.sin(cs)]) / math.sqrt(T)
    seq = seq.reshape(2, TB, P, T).transpose(0, 2, 1, 3).reshape(2, P, PANEL)
    f = np.float32
    return {
        "consts": consts.astype(f), "dist": dist.astype(f),
        "masks": np.stack([causal, dilated], 1).reshape(P, 2 * TOE).astype(f),
        "recip": recip.reshape(P, 2 * T).astype(f), "rope": rope.reshape(P, 2 * T).astype(f),
        "chan": chan.reshape(P, 2 * P).astype(f), "seq": seq.astype(f),
    }


def build(nc, x, mem, stream, vecs1, vecs2, final_g, lamv, consts, dist, masks, recip, rope, out):
    ctx = ExitStack()
    with ctx:
        def sb(name, shape, dt=F32, stack=ctx):
            return stack.enter_context(nc.sbuf_tensor(name, shape, dt))

        def sem(name):
            return ctx.enter_context(nc.semaphore(name))

        x_sb = sb("x_sb", [P, KB, T])
        h_hi = sb("h_hi", [P, KB, T], F32R)
        h_lo = sb("h_lo", [P, KB, T], F32R)
        raw = sb("raw", [P, 2, PANEL])
        w_hi = sb("w_hi", [P, 2, PANEL], F32R)
        w_lo = sb("w_lo", [P, 2, PANEL], F32R)
        cst = sb("cst", [P, NC])
        v1_all = sb("v1_all", [P, LAYERS * NV1])
        v1 = sb("v1", [P, NV1])
        v2_all = sb("v2_all", [P, (LAYERS + 1) * NV2])
        v2 = sb("v2", [P, NV2])
        fin_g = sb("fin_g", [P, KB])
        nlam_all = sb("nlam_all", [P, LAYERS])
        nlam = sb("nlam", [P, 1])
        sq = sb("sq", [P, 2, T])
        ms = sb("ms", [P, 2, T])
        guess = sb("guess", [P, 2, T])
        newt = sb("newt", [P, 2, T])
        hraw = sb("hraw", [P, 2, T])
        mx = sb("mx", [P, 2, 2])
        nmx = sb("nmx", [P, 2, 2])
        ssum = sb("ssum", [P, 2, 2])
        rsum = sb("rsum", [P, 2, 2])
        tok_rstd = sb("tok_rstd", [P, TB])
        tick = sb("tick", [P, 1])
        eps = cst[:, NC - 1:NC]

        def const(i):
            return cst[:, i * P:(i + 1) * P]

        ffn = ExitStack()
        hid_hi = sb("hid_hi", [P, FB, T], F32R, ffn)
        hid_lo = sb("hid_lo", [P, FB, T], F32R, ffn)
        ffn.close()
        mix = ExitStack()
        q_hi = sb("q_hi", [P, HEADS1, T], F32R, mix)
        q_lo = sb("q_lo", [P, HEADS1, T], F32R, mix)
        k_hi = sb("k_hi", [P, HEADS1, T], F32R, mix)
        k_lo = sb("k_lo", [P, HEADS1, T], F32R, mix)
        v_hi = sb("v_hi", [P, TB, 512], F32R, mix)
        v_lo = sb("v_lo", [P, TB, 512], F32R, mix)
        bias = sb("bias", [P, 2, TOE], F32, mix)
        dist_sb = sb("dist_sb", [P, TOE], F32, mix)
        four = ExitStack()
        rec_sb = sb("rec_sb", [P, 2, T], F32, four)
        f_hi = sb("f_hi", [P, 2, T], F32R, four)
        f_lo = sb("f_lo", [P, 2, T], F32R, four)
        apad = sb("apad", [P, 2, T + 2 * PAD], F32, four)
        win = sb("win", [P, 2, T + 2 * PAD], F32, four)
        m_hi = sb("m_hi", [P, 2, T], F32R, four)
        m_lo = sb("m_lo", [P, 2, T], F32R, four)
        four.close()
        prob1 = sb("prob1", [P, 2, 2, T], F32, mix)
        att1 = sb("att1", [P, 2, T], F32, mix)
        at_hi = sb("at_hi", [P, TB, T], F32R, mix)
        at_lo = sb("at_lo", [P, TB, T], F32R, mix)
        fc_hi, fc_lo = v_hi, v_lo
        mix.close()
        two = ExitStack()
        y = sb("y", [P, KB, T], F32, two)
        memn = sb("memn", [P, KB, 256], F32, two)
        qk_hi = sb("qk_hi", [P, 2, T], F32R, two)
        qk_lo = sb("qk_lo", [P, 2, T], F32R, two)
        km_hi = sb("km_hi", [P, 2, 256], F32R, two)
        km_lo = sb("km_lo", [P, 2, 256], F32R, two)
        vp_hi = sb("vp_hi", [P, TB, 2, P], F32R, two)
        vp_lo = sb("vp_lo", [P, TB, 2, P], F32R, two)
        vm_hi = sb("vm_hi", [P, 2, 2, 2, P], F32R, two)
        vm_lo = sb("vm_lo", [P, 2, 2, 2, P], F32R, two)
        pt_hi = sb("pt_hi", [P, TB, T], F32R, two)
        pt_lo = sb("pt_lo", [P, TB, T], F32R, two)
        xs = sb("xs", [P, 2, T], F32, two)
        mask = sb("mask", [P, 2, T], F32, two)
        prob2 = sb("prob2", [P, 2, T], F32, two)
        att2 = sb("att2", [P, 2, T], F32, two)
        rope_sb = sb("rope_sb", [P, 2, T], F32, two)
        two.close()
        mh_hi = pt_hi[:].rearrange("p a (b n) -> p (a b) n", b=2)
        mh_lo = pt_lo[:].rearrange("p a (b n) -> p (a b) n", b=2)

        ps = ctx.enter_context(nc.psum_tensor("ps", [P, 8, 512], F32))

        in_x = sem("in_x")
        in_small = sem("in_small")
        in_mix = sem("in_mix")
        in_two = sem("in_two")
        raw_ready = [sem("raw_ready0"), sem("raw_ready1")]
        hi_split = sem("hi_split")
        lo_split = sem("lo_split")
        panel_done = sem("panel_done")
        x_ready = sem("x_ready")
        square_ready = sem("square_ready")
        sum_step = sem("sum_step")
        guess_ready = sem("guess_ready")
        h_ready = sem("h_ready")
        h_hi_ready = sem("h_hi_ready")
        rstd_ready = sem("rstd_ready")
        rstd_turned = sem("rstd_turned")
        gate_in = sem("gate_in")
        gate_up_out = sem("gate_up_out")
        v1_ready = sem("v1_ready")
        v2_ready = sem("v2_ready")
        unit_in = sem("unit_in")
        silu_ready = sem("silu_ready")
        hid_ready = sem("hid_ready")
        out_ready = sem("out_ready")
        lam_mm = sem("lam_mm")
        lam_in = sem("lam_in")
        lam_exp = sem("lam_exp")
        lam_done = sem("lam_done")
        unit_ready = sem("unit_ready")
        unit_hi = sem("unit_hi")
        unit_lo = sem("unit_lo")
        pooled = sem("pooled")
        bias_ready = sem("bias_ready")
        s_scores = sem("s_scores")
        s_max = sem("s_max")
        s_exp = sem("s_exp")
        s_att = sem("s_att")
        s_tr = sem("s_tr")
        s_thi = sem("s_thi")
        s_tlo = sem("s_tlo")
        s_o = sem("s_o")
        s_osq = sem("s_osq")
        s_osum = sem("s_osum")
        s_oguess = sem("s_oguess")
        s_y = sem("s_y")
        mem_sq = sem("mem_sq")
        mem_sum = sem("mem_sum")
        mem_guess = sem("mem_guess")
        mem_normed = sem("mem_normed")
        memh_ready = sem("memh_ready")
        chunk_ready = sem("chunk_ready")
        hn_in = sem("hn_in")
        hn_mm = sem("hn_mm")
        hn_ms = sem("hn_ms")
        hn_rot = sem("hn_rot")
        hn_guess = sem("hn_guess")
        hn_out = sem("hn_out")
        v_in = sem("v_in")
        v_tr = sem("v_tr")
        v_thi = sem("v_thi")
        v_tlo = sem("v_tlo")
        g_in = sem("g_in")
        t_scores, t_max, t_exp, t_att, t_tr, t_thi, t_tlo = (
            sem(f"t_{n}") for n in ("scores", "max", "exp", "att", "tr", "thi", "tlo"))
        t_o = sem("t_o")
        t_y = sem("t_y")
        y_ready = sem("y_ready")
        stored = sem("stored")

        block = ctx.enter_context(nc.Block())

        def slot(ap, p):
            return ap[:, p % 2, :]

        units1 = [(h, b) for h in range(HEADS1) for b in range(TB)]

        @block.sync
        def _(sp):
            for s in range(2):
                sp.dma_start(raw[:, s, :], stream[s]).then_inc(raw_ready[s], 16)
            with sp.Fori(1, (ALL_PANELS + SPARE_PANELS) // 2) as i:
                for s in range(2):
                    sp.wait_ge(lo_split, 2 * i + s - 1)
                    sp.dma_start(raw[:, bass.ds(s, 1), :],
                                 stream[bass.ds(2 * i + s, 1)].rearrange("a p n -> p a n")
                                 ).then_inc(raw_ready[s], 16)
            for i in range(KB):
                sp.wait_ge(x_ready, 8 * (3 * LAYERS + 1 + LAYERS) + DONE_ORDER.index(i) + 1)
                sp.dma_start(out[:, i, :], x_sb[:, i, :]).then_inc(stored, 16)
            sp.wait_ge(stored, 16 * KB)

        @block.gpsimd
        def _(gp):
            with gp.Fori(0, (ALL_PANELS + SPARE_PANELS) // 2) as i:
                for s in range(2):
                    gp.wait_ge(hi_split, 2 * i + s + 1)
                    gp.tensor_tensor(w_lo[:, s, :], raw[:, s, :], w_hi[:, s, :].bitcast(F32),
                                     ALU.subtract).then_inc(lo_split, 1)

        @block.tensor
        def _(pe):
            def three(dst, l_hi, l_lo, r_hi, r_lo, first, last):
                pe.matmul(dst, l_hi, r_hi, start=first, stop=False)
                pe.matmul(dst, l_hi, r_lo, start=False, stop=False)
                return pe.matmul(dst, l_lo, r_hi, start=False, stop=last)

            def sum_squares(n):
                pe.wait_ge(x_ready, 8 * n + DONE_ORDER.index(SUM_BANK) + 1)
                for i in range(KB):
                    add_square(n, i)

            def panel(p):
                pe.wait_ge(lo_split, p + 1)

            def add_square(n, i):
                pe.wait_ge(square_ready, 8 * n + i + 1)
                pe.matmul(ps[:, SUM_BANK, :], const(C_MEAN), sq[:, i % 2, :],
                          start=(i == 0), stop=(i == KB - 1)).then_inc(sum_step, 1)

            def first_panel(n, p, s):
                panel(p)
                pe.wait_ge(x_ready, 8 * n + 2)
                w = [t[:, s, :].rearrange("p (k g n) -> p k g n", k=KB, g=2) for t in (w_hi, w_lo)]
                for i, k in enumerate(DONE_ORDER):
                    pe.wait_ge(h_ready, 8 * n + i + 1)
                    for g in range(2):
                        mm = three(ps[:, g, :], w[0][:, k, g, :], w[1][:, k, g, :],
                                   h_hi[:, k, :], h_lo[:, k, :], i == 0, i == KB - 1)
                    if i == KB - 1:
                        mm.then_inc(panel_done, 1)
                    if i == 2:
                        pe.wait_ge(x_ready, 8 * n + DONE_ORDER.index(SUM_BANK) + 1)
                    if i >= 2:
                        add_square(n, i - 2)
                for i in range(KB - 2, KB):
                    add_square(n, i)

            def up(p, c, s):
                panel(p)
                w = [t[:, s, :].rearrange("p (k g n) -> p k g n", k=KB, g=2) for t in (w_hi, w_lo)]
                for k in range(KB):
                    for g in range(2):
                        mm = three(ps[:, 2 * (c % 2) + g, :], w[0][:, k, g, :], w[1][:, k, g, :],
                                   h_hi[:, k, :], h_lo[:, k, :], k == 0, k == KB - 1)
                mm.then_inc(panel_done, 1)

            def down(p, d, s, F, first=False, last=False):
                panel(p)
                w = [t[:, s, :].rearrange("p (f n) -> p f n", f=2) for t in (w_hi, w_lo)]
                for i, m in enumerate(DONE_ORDER if last else DOWN_ORDER):
                    if first and m == 0:
                        pe.wait_ge(hid_ready, FB * F + FB)
                    for f in range(2):
                        if isinstance(d, int):
                            r = hid_hi[:, 2 * d + f, :], hid_lo[:, 2 * d + f, :]
                        else:
                            r = [t[:, bass.ds(2 * d + f, 1), :] for t in (hid_hi, hid_lo)]
                        mm = three(ps[:, m, :], w[0][:, f, P * m:P * m + P], w[1][:, f, P * m:P * m + P],
                                   *r, first and f == 0, last and f == 1)
                    if last and i < KB - 1:
                        mm.then_inc(out_ready, 1)
                mm.then_inc(panel_done, 1)

            def feed_forward(n, F, p0, odd):
                first_panel(n, p0, odd)
                up(p0 + 1, 1, 1 - odd)
                with pe.Fori(1, FB // 2) as i:
                    for c in range(2):
                        pe.wait_ge(gate_up_out, FB * F + 2 * i + c - 1)
                        up(p0 + 2 * i + c, c, (odd + c) % 2)
                pd = p0 + UP_PANELS
                pe.wait_ge(hid_ready, FB * F + 2)
                down(pd, 0, odd % 2, F, first=True)
                with pe.Fori(0, (DOWN_PANELS - 3) // 2) as i:
                    for e in range(2):
                        down(pd + 1 + 2 * i + e, 1 + 2 * i + e, (odd + 1 + e) % 2, F)
                for d in (DOWN_PANELS - 2, DOWN_PANELS - 1):
                    down(pd + d, d, (odd + d) % 2, F, last=(d == DOWN_PANELS - 1))

            def project_out(p0, odd, ready, order=range(KB), begun=(0, 0, 0, 0)):
                for j in range(OUT_PANELS):
                    panel(p0 + j)
                    for g in range(2):
                        for i in range(begun[j], KB):
                            if j == 0 and g == 0:
                                ready(i)
                            mm = project(j, g, (odd + j) % 2, order[i], i)
                        if g == 0:
                            mm.then_inc(out_ready, 1)
                    mm.then_inc(panel_done, 1)

            def project(j, g, s, k, i):
                w = [t[:, s, :].rearrange("p (k g n) -> p k g n", k=KB, g=2) for t in (w_hi, w_lo)]
                return three(ps[:, DONE_ORDER[2 * j + g], :], w[0][:, k, g, :], w[1][:, k, g, :],
                             h_hi[:, k, :], h_lo[:, k, :], i == 0, i == KB - 1)

            def mixer1(l, n, p0):
                lo0 = NU * l

                def finish(i, mm):
                    mm.then_inc(unit_ready if MIX_UNITS[i][3] is None else panel_done, 1)

                def free_bank(i):
                    pe.wait_ge(unit_lo, lo0 + i - 3)

                def feature_major(i, j):
                    panel(p0 + j)
                    w = [t[:, (j + 1) % 2, :].rearrange("p (k g n) -> p k g n", k=KB, g=2) for t in (w_hi, w_lo)]
                    for g in range(2):
                        if i + g >= 4:
                            free_bank(i + g)
                        for k in range(KB):
                            mm = three(ps[:, MIX_UNITS[i + g][2], :], w[0][:, k, g, :], w[1][:, k, g, :],
                                       h_hi[:, k, :], h_lo[:, k, :], k == 0, k == KB - 1)
                        finish(i + g, mm)
                    return i + 2

                first_panel(n, p0, 1)
                i = feature_major(2, 1)
                pe.wait_ge(rstd_ready, l + 1)
                for tb in range(TB):
                    mm = pe.transpose(ps[:, SUM_BANK, P * tb:P * tb + P], guess[:, 0, P * tb:P * tb + P],
                                      const(C_ID))
                mm.then_inc(rstd_turned, 1)
                for j in (2, 3):
                    i = feature_major(i, j)
                panel(p0 + 4)
                for t in range(TB):
                    free_bank(i)
                    s = slice(P * t, P * t + P)
                    for c in range(2):
                        mm = three(ps[:, MIX_UNITS[i][2], 256 * c:256 * c + 256], f_hi[:, c, s], f_lo[:, c, s],
                                   w_hi[:, 1, 0:256], w_lo[:, 1, 0:256], True, True)
                    finish(i, mm)
                    i += 1
                for j in (5, 6):
                    i = feature_major(i, j)
                free_bank(i + 1)
                for e in range(2):
                    panel(p0 + 7 + e)
                    w = [t[:, e, :].rearrange("p (t n) -> p t n", t=TB) for t in (w_hi, w_lo)]
                    for c in range(2):
                        s = slice(256 * c + P * e, 256 * c + P * e + P)
                        for t in range(TB):
                            mm = three(ps[:, MIX_UNITS[i + c][2], :], fc_hi[:, t, s], fc_lo[:, t, s],
                                       w[0][:, t, :], w[1][:, t, :], e == 0 and t == 0, e == 1 and t == TB - 1)
                        if e == 1:
                            finish(i + c, mm)
                    if e == 0:
                        mm.then_inc(panel_done, 1)
                i += 2
                for j in (9, 10):
                    panel(p0 + j)
                    w = [t[:, (j + 1) % 2, :].rearrange("p (k n) -> p k n", k=KB) for t in (w_hi, w_lo)]
                    for t in range(TB):
                        free_bank(i)
                        s = slice(P * t, P * t + P)
                        for k in range(KB):
                            mm = three(ps[:, MIX_UNITS[i][2], 0:256], h_hi[:, k, s], h_lo[:, k, s],
                                       w[0][:, k, :], w[1][:, k, :], k == 0, k == KB - 1)
                        finish(i, mm)
                        i += 1
                panel(p0 + 11)
                for c in range(2):
                    free_bank(i)
                    for k in range(2):
                        s = slice(256 * k + P * c, 256 * k + P * c + P)
                        mm = three(ps[:, MIX_UNITS[i][2], :], w_hi[:, 0, s], w_lo[:, 0, s],
                                   f_hi[:, k, :], f_lo[:, k, :], k == 0, k == 1)
                    finish(i, mm)
                    i += 1
                for c in range(2):
                    free_bank(i)
                    pe.wait_ge(pooled, 2 * l + c + 1)
                    s = slice(512 + P * c, 512 + P * c + P)
                    mm = three(ps[:, MIX_UNITS[i][2], :], w_hi[:, 0, s], w_lo[:, 0, s],
                               m_hi[:, c, :], m_lo[:, c, :], True, True)
                    finish(i, mm)
                    i += 1
                pe.wait_ge(unit_lo, lo0 + NU)
                u0 = UNITS1 * l
                for s in range(UNITS1 + 6):
                    if s < UNITS1:
                        h, b = units1[s]
                        if s >= 2:
                            pe.wait_ge(s_max, u0 + s - 1)
                        for j in range(2):
                            r, c = slice(64 * j, 64 * j + 64), slice(P * b, P * b + P)
                            mm = three(ps[:, 2 * (s % 2) + j, :], q_hi[r, h, c], q_lo[r, h, c],
                                       k_hi[r, h, :], k_lo[r, h, :], True, True)
                        mm.then_inc(s_scores, 1)
                    if 3 <= s <= UNITS1 + 2:
                        u = s - 3
                        pe.wait_ge(s_att, u0 + u + 1)
                        if u >= 2:
                            pe.wait_ge(s_tlo, u0 + u - 1)
                        for kb in range(TB):
                            mm = pe.transpose(ps[:, 4 + u % 2, P * kb:P * kb + P],
                                              att1[:, u % 2, P * kb:P * kb + P], const(C_ID))
                        mm.then_inc(s_tr, 1)
                    if s >= 4 and (s - 4) % TB == TB - 1 and s - 4 < UNITS1:
                        h = (s - 4) // TB
                        pe.wait_ge(s_tlo, u0 + s - 3)
                        if h:
                            pe.wait_ge(s_oguess, HEADS1 * l + h)
                        for kb in range(TB):
                            c = slice(P * h, P * h + P)
                            mm = three(ps[:, 6 + h % 2, :], v_hi[:, kb, c], v_lo[:, kb, c],
                                       at_hi[:, kb, :], at_lo[:, kb, :], kb == 0, kb == TB - 1)
                        mm.then_inc(s_o, 1)
                    if s >= 5 and (s - 5) % TB == TB - 1 and s - 5 < UNITS1:
                        h = (s - 5) // TB
                        pe.wait_ge(s_osq, HEADS1 * l + h + 1)
                        if h:
                            pe.wait_ge(s_y, HEADS1 * l + h)
                        pe.matmul(ps[:, 7 - h % 2, :], const(C_HEAD), sq[:, 0, :],
                                  start=True, stop=True).then_inc(s_osum, 1)
                project_out(p0 + MIX_PANELS, 1,
                            lambda k: pe.wait_ge(s_y, HEADS1 * l + k - 3) if k >= 4 else None)

            def chunk_slices(s):
                return [t[:, s, :].rearrange("p (k g n) -> p k g n", k=KB, g=2) for t in (w_hi, w_lo)]

            def mem_group(G, p, act_hi, act_lo, width, busy):
                w_ = slice(0, width)
                for c in range(4):
                    busy[c]()
                    if c % 2 == 0:
                        panel(p + c // 2)
                    w = chunk_slices(c // 2)
                    for k in range(KB):
                        mm = three(ps[:, c, w_], w[0][:, k, c % 2, :], w[1][:, k, c % 2, :],
                                   act_hi[:, k, :], act_lo[:, k, :], k == 0, k == KB - 1)
                    mm.then_inc(panel_done if c % 2 else chunk_ready, 1)
                    if 1 <= c <= 2:
                        j = c - 1
                        pe.wait_ge(hn_in, 2 * G + j + 1)
                        pe.matmul(ps[:, 5 + 2 * j, w_], const(C_HALF), sq[:, j, w_],
                                  start=True, stop=True).then_inc(hn_mm, 1)

            def scores(stage, u):
                h, b = u // TB, u % TB
                r, c, w = slice(64 * (h % 2), 64 * (h % 2) + 64), slice(P * b, P * b + P), slice(0, stage.widths[u])
                if stage.memory:
                    k_split = km_hi[r, h // 2, w], km_lo[r, h // 2, w]
                else:
                    k_split = qk_hi[r, 1, w], qk_lo[r, 1, w]
                return three(ps[:, u % 2, w], qk_hi[r, h // 2, c], qk_lo[r, h // 2, c], *k_split, True, True)

            def outputs(stage, h):
                l, gi = stage.l, stage.gi
                if stage.memory:
                    if h == 2:
                        pe.wait_ge(t_y, 8 * l + 1)
                    for kb in range(2):
                        mm = three(ps[:, 5, :], vm_hi[:, kb, h // 2, h % 2, :], vm_lo[:, kb, h // 2, h % 2, :],
                                   pt_hi[:, kb, :], pt_lo[:, kb, :],
                                   h % 2 == 0 and kb == 0, h % 2 == 1 and kb == 1)
                else:
                    if h == 0:
                        pe.wait_ge(v_tlo, 7 * l + gi)
                    for kb in range(TB):
                        c = slice(P * kb, T)
                        mm = three(ps[:, 5, c], vp_hi[:, kb, h, :], vp_lo[:, kb, h, :],
                                   pt_hi[:, kb, c], pt_lo[:, kb, c],
                                   h == 0 and kb == 0, h == 1 and kb == TB - 1)
                mm.then_inc(t_o, 1)

            def attention_step(here, before, s, produce, part):
                if here:
                    if s == 0 and not here.memory:
                        pe.wait_ge(hn_out, GROUPS * here.l + here.gi + 1)
                    unit2 = lagged(here, before, s, 2)
                    if unit2:
                        pe.wait_ge(t_exp if unit2[0].memory else t_max, here.u0 + s - 1)
                    scores(here, s).then_inc(t_scores, 1)
                unit = lagged(here, before, s, LAG_TR)
                if unit:
                    stage, u = unit
                    pe.wait_ge(t_att, stage.u0 + u + 1)
                    if u >= 2 or not stage.memory:
                        pe.wait_ge(t_tlo, stage.u0 + u - 1)
                    for kb in range(stage.widths[u] // P):
                        mm = pe.transpose(ps[:, 2 + u % 2, P * kb:P * kb + P],
                                          att2[:, u % 2, P * kb:P * kb + P], const(C_ID))
                    mm.then_inc(t_tr, 1)
                unit = lagged(here, before, s, LAG_OUT)
                if unit and unit[1] % TB == TB - 1:
                    stage, u = unit
                    pe.wait_ge(t_tlo, stage.u0 + u + 1)
                    outputs(stage, u // TB)
                if here and not here.memory and s == 5:
                    pe.wait_ge(v_in, 7 * here.l + here.gi)
                    pe.wait_ge(t_y, 8 * here.l + here.gi)
                    for tb in range(TB):
                        mm = pe.transpose(ps[:, 5, P * tb:P * tb + P],
                                          hraw[:, 0, P * tb:P * tb + P], const(C_ID))
                    mm.then_inc(v_tr, 1)
                if produce and part is not None:
                    produce(part)

            def producer(l, gi, beside):
                G = GROUPS * l + gi
                p = BASE2 + LAYER2_PANELS * l + 2 * gi
                rot0 = 12 * l + 2 * (gi - 2)

                def rotate(j):
                    pe.matmul(ps[:, 6, :], const(C_ROT), xs[:, j, :], start=True, stop=True)
                    pe.matmul(ps[:, 7, :], const(C_HALF), sq[:, j, :], start=True, stop=True).then_inc(hn_mm, 1)

                def step(s):
                    if s > 7:
                        return
                    c = s // 2
                    if s == 0:
                        pe.wait_ge(v_in, 7 * l + gi - 1)
                    if s == 2:
                        pe.wait_ge(hn_in, 2 * G + 1)
                        pe.wait_ge(g_in, 7 * l + gi - 1)
                        rotate(0)
                    if s == 4:
                        pe.wait_ge(hn_in, 2 * G + 2)
                        pe.wait_ge(hn_ms, 2 * G + 1)
                        pe.wait_ge(hn_rot, rot0 + 1)
                        rotate(1)
                    if s == 6:
                        pe.wait_ge(hn_ms, 2 * G + 2)
                    if s % 4 == 0:
                        panel(p + s // 4)
                    w = chunk_slices(c // 2)
                    for k in range(4 * (s % 2), 4 * (s % 2) + 4):
                        mm = three(ps[:, 4 if c < 3 else 7, :], w[0][:, k, c % 2, :], w[1][:, k, c % 2, :],
                                   h_hi[:, k, :], h_lo[:, k, :], k == 0, k == KB - 1)
                    if s % 2:
                        mm.then_inc(panel_done if c % 2 else chunk_ready, 1)
                return step

            def stack2(l):
                n = 3 * LAYERS + 1 + l
                p0 = BASE2 + LAYER2_PANELS * l
                g0 = GROUPS * l
                sum_squares(n)
                for k in range(KB):
                    pe.wait_ge(memh_ready, 8 * l + k + 1)
                mem_group(g0, p0, mh_hi, mh_lo, 256, [lambda: None] * 4)
                pe.wait_ge(v_in, 7 * l + 1)
                for c in range(2):
                    for tb in range(2):
                        mm = pe.transpose(ps[:, 4, 256 * tb + P * c:256 * tb + P * c + P],
                                          hraw[:, c, P * tb:P * tb + P], const(C_ID))
                mm.then_inc(v_tr, 1)
                mem_group(g0 + 1, p0 + 2, h_hi, h_lo, T, [
                    lambda: pe.wait_ge(hn_in, 2 * g0 + 1), lambda: pe.wait_ge(hn_in, 2 * g0 + 2),
                    lambda: pe.wait_ge(hn_ms, 2 * g0 + 2), lambda: None])
                pe.wait_ge(hn_out, g0 + 2)
                pe.wait_ge(v_tlo, 7 * l + 1)
                pe.wait_ge(g_in, 7 * l + 1)
                def tail(s):
                    if s > 3:
                        return
                    g = s // 2
                    if s == 0:
                        panel(p0 + 2 * GROUPS)
                        pe.wait_ge(t_max, UNITS2 * (l + 1))
                    for i in range(4) if s % 2 == 0 else range(4, KB - 1):
                        pe.wait_ge(y_ready, 8 * l + i + 1)
                        project(0, g, 0, Y_ORDER[i], i)

                def beside_last(s):
                    if s == 2:
                        panel(p0 + 2 * GROUPS + 1)
                    if s >= 2:
                        pe.wait_ge(y_ready, 8 * l + s - 1)
                        for g in range(2):
                            project(1, g, 1, Y_ORDER[s - 2], s - 2)

                run_stages(l, pe.Fori, attention_step, producer, beside_last, tail)
                project_out(p0 + 2 * GROUPS, 0, lambda i: pe.wait_ge(y_ready, 8 * l + i + 1), Y_ORDER,
                            (KB - 1, PAIR_UNITS - 2, 0, 0))

            pe.wait_ge(in_small, 16 * 5)
            pe.wait_ge(lam_in, 1)
            pe.matmul(ps[:, 7, 0:4], newt[0:64, 0, 0:P], hraw[0:64, 0, 0:4],
                      start=True, stop=True).then_inc(lam_mm, 1)
            with pe.Fori(0, LAYERS) as l:
                p0 = LAYER1_PANELS * l
                feed_forward(3 * l, 2 * l, p0, 0)
                mixer_p0 = p0 + FFN_PANELS
                mixer1(l, 3 * l + 1, mixer_p0)
                feed_forward(3 * l + 2, 2 * l + 1, mixer_p0 + MIX_PANELS + OUT_PANELS, 1)
            sum_squares(3 * LAYERS)
            for i in range(KB):
                pe.wait_ge(mem_sq, i + 1)
                pe.matmul(ps[:, 5, 0:256], const(C_MEAN), sq[:, i % 2, 0:256],
                          start=(i == 0), stop=(i == KB - 1)).then_inc(mem_sum, 1)
            with pe.Fori(0, LAYERS) as l:
                stack2(l)

        @block.scalar
        def _(act):
            def split(p, s):
                act.wait_ge(raw_ready[s], 8 * (p - s) + 16)
                act.activation(w_hi[:, s, :], raw[:, s, :], ACT.Copy).then_inc(hi_split, 1)

            def split_after(p, s):
                act.wait_ge(panel_done, p + 1)
                split(p + 2, s)

            def guesses(src, width, done):
                w = slice(0, width)
                act.activation(guess[:, 0, w], src, ACT.Abs_reciprocal_sqrt, bias=eps)
                act.activation(ms[:, 0, w], src, ACT.Identity, bias=eps)
                act.drain()
                act.activation(newt[:, 0, w], guess[:, 0, w], ACT.Square).then_inc(done, 1)

            def pair_guesses(width):
                w = slice(0, width)
                act.activation(guess[:, :, w], ms[:, :, w], ACT.Abs_reciprocal_sqrt)
                act.drain()
                act.activation(newt[:, :, w], guess[:, :, w], ACT.Square).then_inc(hn_guess, 1)

            def norm(n):
                for i, m in enumerate(DONE_ORDER):
                    act.wait_ge(x_ready, 8 * n + i + 1)
                    if i >= 2:
                        act.wait_ge(sum_step, 8 * n + i - 1)
                    act.activation(sq[:, i % 2, :], x_sb[:, m, :], ACT.Square).then_inc(square_ready, 1)
                act.wait_ge(sum_step, 8 * n + 8)
                guesses(ps[:, SUM_BANK, :], T, guess_ready)

            def gained(n, last_panel, odd, h_free):
                gain = G_FFN1 if n[1] == 0 else G_MIX if n[1] == 1 else G_FFN2
                n = n[0]

                def square(i):
                    if i >= 2:
                        act.wait_ge(sum_step, 8 * n + i - 1)
                    act.activation(sq[:, i % 2, :], x_sb[:, DONE_ORDER[i], :], ACT.Square).then_inc(square_ready, 1)

                for i, m in enumerate(DONE_ORDER):
                    act.wait_ge(x_ready, 8 * n + i + 1)
                    if h_free and i < 2:
                        square(i)
                    if h_free and i == 2:
                        act.wait_ge(panel_done, last_panel + 1)
                    if h_free and i == 2:
                        for m2 in DONE_ORDER[:2]:
                            act.activation(h_hi[:, m2, :], x_sb[:, m2, :], ACT.Copy,
                                           scale=v1[:, gain + m2:gain + m2 + 1]).then_inc(h_hi_ready, 1)
                    if i >= 2 or not h_free:
                        act.activation(h_hi[:, m, :], x_sb[:, m, :], ACT.Copy,
                                       scale=v1[:, gain + m:gain + m + 1]).then_inc(h_hi_ready, 1)
                    if not h_free and i < 2:
                        square(i)
                if last_panel is not None:
                    split_after(last_panel, odd)
                for i in range(2, KB):
                    square(i)
                act.wait_ge(sum_step, 8 * n + KB)
                guesses(ps[:, SUM_BANK, :], T, guess_ready)

            def feed_forward(F, p0, odd):
                with act.Fori(0, FB // 2) as i:
                    for e in range(2):
                        split_after(p0 + 2 * i + e, (odd + e) % 2)
                        act.wait_ge(gate_in, FB * F + 2 * i + e + 1)
                        act.activation(hraw[:, e, :], hraw[:, e, :], ACT.Silu).then_inc(silu_ready, 1)
                pd = p0 + UP_PANELS
                with act.Fori(0, (DOWN_PANELS - 1) // 2) as i:
                    for e in range(2):
                        split_after(pd + 2 * i + e, (odd + e) % 2)

            def mixer1(l, p0):
                act.dma_start(dist_sb[:], dist).then_inc(in_mix, 16)
                act.dma_start(rec_sb[:].rearrange("p a n -> p (a n)"), recip).then_inc(in_mix, 16)
                for i, (kind, c, bank, ends) in enumerate(MIX_UNITS):
                    if kind == "yf" and c == 0:
                        split_after(p0 + 7, 0)
                    if ends is not None and (kind, c) not in (("a", 1), ("pool", 1)):
                        split_after(p0 + ends, (ends + 1) % 2)
                    if kind in NORMED:
                        act.wait_ge(unit_in, NORMED_BEFORE[NU] * l + NORMED_BEFORE[i + 1])
                    elif ends is None:
                        act.wait_ge(unit_ready, READY1 * l + READY_BEFORE[i + 1])
                    else:
                        act.wait_ge(panel_done, p0 + ends + 1)
                    src, scale = hraw[:, i % 2, :] if kind in NORMED else ps[:, bank, :], 1.0
                    if kind == "a":
                        dst = apad[:, c, PAD:PAD + T]
                    elif kind in ("f", "yf"):
                        dst = f_hi[:, c, :]
                    elif kind == "q":
                        dst = q_hi[:, c, :]
                    elif kind == "k":
                        dst = k_hi[:, c, :]
                    elif kind == "v":
                        dst, src = v_hi[:, c % 4, 256 * (c // 4):256 * (c // 4) + 256], src[:, 0:256]
                    elif kind == "fc":
                        dst = fc_hi[:, c, :]
                    elif kind == "four":
                        dst = h_hi[:, 2 + c, :]
                    else:
                        dst, scale = h_hi[:, c, :], v1[:, G_POOL + c:G_POOL + c + 1]
                    act.activation(dst, src, ACT.Copy, scale=scale).then_inc(unit_hi, 1)
                    if (kind, c) == ("pool", 1):
                        split_after(p0 + ends, (ends + 1) % 2)

                def head_bias(h):
                    if h >= 2:
                        act.wait_ge(s_max, UNITS1 * l + TB * (h - 1))
                    act.activation(bias[:, h % 2, :], dist_sb[:], ACT.Copy, scale=-SLOPES[h]).then_inc(bias_ready, 1)

                u0 = UNITS1 * l
                act.wait_ge(in_mix, 32 * l + 32)
                head_bias(0)
                act.wait_ge(unit_lo, NU * l + NU)
                for s in range(UNITS1 + 7):
                    if s < UNITS1:
                        act.wait_ge(s_max, u0 + s + 1)
                        for j in range(2):
                            ins = act.activation(prob1[:, s % 2, j, :], prob1[:, s % 2, j, :], ACT.Exp,
                                                 bias=nmx[:, s % 2, j:j + 1], accum_out=ssum[:, s % 2, j:j + 1])
                        ins.then_inc(s_exp, 1)
                        if s % TB == 0 and s // TB + 1 < HEADS1:
                            head_bias(s // TB + 1)
                    if 3 <= s <= UNITS1 + 2:
                        u = s - 3
                        h, b = units1[u]
                        act.wait_ge(s_tr, u0 + u + 1)
                        if b == 0 and h:
                            act.wait_ge(s_o, HEADS1 * l + h)
                        act.activation(at_hi[:, :, P * b:P * b + P],
                                       ps[:, 4 + u % 2, :].rearrange("p (k n) -> p k n", k=TB),
                                       ACT.Copy).then_inc(s_thi, 1)
                    if s >= 5 and (s - 5) % TB == TB - 1 and s - 5 < UNITS1:
                        h = (s - 5) // TB
                        act.wait_ge(s_o, HEADS1 * l + h + 1)
                        act.activation(sq[:, 0, :], ps[:, 6 + h % 2, :], ACT.Square).then_inc(s_osq, 1)
                    if s >= 6 and (s - 6) % TB == TB - 1 and s - 6 < UNITS1:
                        h = (s - 6) // TB
                        act.wait_ge(s_osum, HEADS1 * l + h + 1)
                        guesses(ps[:, 7 - h % 2, :], T, s_oguess)
                for j in range(OUT_PANELS - 1):
                    split_after(p0 + MIX_PANELS + j, (j + 1) % 2)

            def head_norm_in(j, bank, width, gain):
                w = slice(0, width)
                if isinstance(gain, int):
                    g = v2[:, gain:gain + 1]
                else:
                    g = v2[:, bass.ds(gain, 1)]
                act.activation(xs[:, j, w], ps[:, bank, w], ACT.Copy, scale=g)
                act.activation(sq[:, j, w], ps[:, bank, w], ACT.Square).then_inc(hn_in, 1)

            def mean_square(i, j, bank, width):
                w = slice(0, width)
                act.wait_ge(hn_mm, i + 1)
                act.activation(ms[:, j, w], ps[:, bank, w], ACT.Identity, bias=eps).then_inc(hn_ms, 1)

            def attention_step(here, before, s, produce, part):
                if produce and part is not None:
                    produce(part)
                if here:
                    w = slice(0, here.widths[s])
                    act.wait_ge(t_max, here.u0 + s + 1)
                    act.activation(prob2[:, s % 2, w], ps[:, s % 2, w] if here.memory else prob2[:, s % 2, w],
                                   ACT.Exp, bias=nmx[:, s % 2, 0:1], accum_out=ssum[:, s % 2, 0:1]).then_inc(t_exp, 1)
                unit = lagged(here, before, s, LAG_TR)
                if unit:
                    stage, u = unit
                    b, kbs = u % TB, stage.widths[u] // P
                    act.wait_ge(t_tr, stage.u0 + u + 1)
                    if b == 0 and (u or not stage.memory):
                        act.wait_ge(t_o, stage.heads0 + u // TB)
                    act.activation(pt_hi[:, 0:kbs, P * b:P * b + P],
                                   ps[:, 2 + u % 2, 0:P * kbs].rearrange("p (k n) -> p k n", k=kbs),
                                   ACT.Copy).then_inc(t_thi, 1)
                if here and not here.memory and s == 5:
                    act.wait_ge(v_tr, 7 * here.l + here.gi)
                    for h in range(2):
                        ins = act.activation(
                            vp_hi[:, :, h, 64 * h:64 * h + 64],
                            ps[:, 5, :].rearrange("p (t n) -> p t n", t=TB)[:, :, 64 * h:64 * h + 64], ACT.Copy)
                    ins.then_inc(v_thi, 1)
                if produce and s == here.n - 1:
                    produce.gates()

            def producer(l, gi, beside):
                G = GROUPS * l + gi
                p = BASE2 + LAYER2_PANELS * l + 2 * gi

                def step(s):
                    if s == 2:
                        act.wait_ge(chunk_ready, 2 * G + 1)
                        act.wait_ge(hn_out, G)
                        head_norm_in(0, 4, T, G_QK + 2 * gi)
                    if s == 3:
                        mean_square(2 * G, 0, 7, T)
                    if s == 4:
                        act.wait_ge(panel_done, p + 1)
                        head_norm_in(1, 4, T, G_QK + 2 * gi + 1)
                        split(p + 2, 0)
                    if s == 5:
                        mean_square(2 * G + 1, 1, 7, T)
                        act.drain()
                        pair_guesses(T)
                    if s == 6:
                        act.wait_ge(chunk_ready, 2 * G + 2)
                        act.activation(hraw[:, 0, :], ps[:, 4, :], ACT.Copy).then_inc(v_in, 1)

                def gates():
                    act.wait_ge(panel_done, p + 2)
                    if isinstance(gi, int):
                        dst = y[:, gi - 2, :]
                    else:
                        dst = y[:, bass.ds(gi - 2, 1), :]
                    act.activation(dst, ps[:, 7, :], ACT.Silu).then_inc(g_in, 1)
                    split(p + 3, 1)
                step.gates = gates
                return step

            def stack2(l):
                p0 = BASE2 + LAYER2_PANELS * l
                g0 = GROUPS * l
                norm(3 * LAYERS + 1 + l)
                act.wait_ge(v2_ready, l + 1)
                act.wait_ge(chunk_ready, 2 * g0 + 1)
                head_norm_in(0, 0, 256, G_QK)
                act.wait_ge(panel_done, p0 + 1)
                head_norm_in(1, 1, 256, G_QK + 1)
                split(p0 + 2, 0)
                act.wait_ge(h_ready, 8 * (3 * LAYERS + 1 + l))
                mean_square(2 * g0, 0, 5, 256)
                mean_square(2 * g0 + 1, 1, 7, 256)
                act.drain()
                pair_guesses(256)
                act.wait_ge(chunk_ready, 2 * g0 + 2)
                act.activation(hraw[:, 0, 0:256], ps[:, 2, 0:256], ACT.Copy)
                act.wait_ge(panel_done, p0 + 2)
                act.activation(hraw[:, 1, 0:256], ps[:, 3, 0:256], ACT.Copy).then_inc(v_in, 1)
                split(p0 + 3, 1)
                act.wait_ge(v_tr, 7 * l + 1)
                for h in range(2):
                    ins = act.activation(
                        vm_hi[:, :, :, h, 64 * h:64 * h + 64],
                        ps[:, 4, :].rearrange("p (t c n) -> p t c n", t=2, c=2)[:, :, :, 64 * h:64 * h + 64], ACT.Copy)
                ins.then_inc(v_thi, 1)
                act.wait_ge(chunk_ready, 2 * g0 + 3)
                act.wait_ge(hn_out, g0 + 1)
                head_norm_in(0, 0, T, G_QK + 2)
                act.wait_ge(panel_done, p0 + 3)
                head_norm_in(1, 1, T, G_QK + 3)
                split(p0 + 4, 0)
                mean_square(2 * g0 + 2, 0, 5, T)
                mean_square(2 * g0 + 3, 1, 7, T)
                act.drain()
                pair_guesses(T)
                act.wait_ge(chunk_ready, 2 * g0 + 4)
                act.activation(y[:, 6, :], ps[:, 2, :], ACT.Silu)
                act.wait_ge(panel_done, p0 + 4)
                act.activation(y[:, 7, :], ps[:, 3, :], ACT.Silu).then_inc(g_in, 1)
                split(p0 + 5, 1)
                run_stages(l, act.Fori, attention_step, producer)
                for j in range(OUT_PANELS):
                    split_after(p0 + 2 * GROUPS + j, j % 2)

            act.dma_start(x_sb[:].rearrange("p k n -> p (k n)"), x).then_inc(in_x, 16)
            for dst, src in ((cst, consts), (v1_all, vecs1), (v2_all, vecs2), (fin_g, final_g)):
                act.dma_start(dst[:], src).then_inc(in_small, 16)
            act.dma_start(hraw[0:64, 1, 0:8], lamv).then_inc(in_small, 16)
            for s in range(2):
                split(s, s)
            act.wait_ge(lam_mm, 1)
            act.activation(hraw[:, 1, 8:12], ps[:, 7, 0:4], ACT.Exp).then_inc(lam_exp, 1)
            with act.Fori(0, LAYERS) as l:
                p0 = LAYER1_PANELS * l
                act.wait_ge(v1_ready, l + 1)
                gained((3 * l, 0), None, 0, False)
                feed_forward(2 * l, p0, 0)
                gained((3 * l + 1, 1), p0 + FFN_PANELS - 1, 0, False)
                mixer1(l, p0 + FFN_PANELS)
                gained((3 * l + 2, 2), p0 + LAYER1_PANELS - FFN_PANELS - 1, 0, True)
                feed_forward(2 * l + 1, p0 + LAYER1_PANELS - FFN_PANELS, 1)
                split_after(p0 + LAYER1_PANELS - 1, 1)
            act.dma_start(memn[:].rearrange("p k n -> p (k n)"), mem).then_inc(in_two, 16)
            act.dma_start(mask[:].rearrange("p a n -> p (a n)"), masks).then_inc(in_two, 16)
            act.dma_start(rope_sb[:].rearrange("p a n -> p (a n)"), rope).then_inc(in_two, 16)
            norm(3 * LAYERS)
            act.wait_ge(in_two, 48)
            for i in range(KB):
                if i >= 2:
                    act.wait_ge(mem_sum, i - 1)
                act.activation(sq[:, i % 2, 0:256], memn[:, i, :], ACT.Square).then_inc(mem_sq, 1)
            act.wait_ge(mem_sum, KB)
            act.wait_ge(x_ready, 8 * (3 * LAYERS + 2))
            guesses(ps[:, 5, 0:256], 256, mem_guess)
            act.wait_ge(mem_normed, 1)
            with act.Fori(0, LAYERS) as l:
                stack2(l)

        @block.vector
        def _(dve):
            rstd = guess[:, 0, :]

            def newton(width, slots=1):
                at = (slice(None), slice(0, slots), slice(0, width))
                dve.scalar_tensor_tensor(out=newt[at], in0=ms[at], scalar=0.5, in1=newt[at], op0=ALU.mult, op1=ALU.mult)
                dve.drain()
                dve.scalar_tensor_tensor(out=guess[at], in0=newt[at], scalar=1.5, in1=guess[at],
                                         op0=ALU.subtract, op1=ALU.mult, reverse0=True)
                dve.drain()

            def remainder(dst, src, hi):
                return dve.tensor_tensor(dst, src, hi.bitcast(F32), ALU.subtract)

            def norm(n, gain):
                dve.wait_ge(guess_ready, n + 1)
                newton(T)

                wholes = [hraw[:, 0, :], hraw[:, 1, :], newt[:, 1, :]]

                def whole(k):
                    dve.scalar_tensor_tensor(out=wholes[k % 3], in0=x_sb[:, k, :], scalar=gain[:, k:k + 1],
                                             in1=rstd, op0=ALU.mult, op1=ALU.mult)
                whole(0)
                dve.drain()
                for k in range(KB):
                    dve.tensor_copy(h_hi[:, k, :], wholes[k % 3])
                    if k + 1 < KB:
                        whole(k + 1)
                    dve.drain()
                    remainder(h_lo[:, k, :], wholes[k % 3], h_hi[:, k, :]).then_inc(h_ready, 1)

            def low(n, i, gain):
                m = DONE_ORDER[i]
                dve.wait_ge(h_hi_ready, 8 * n + i + 1)
                dve.scalar_tensor_tensor(out=h_lo[:, m, :], in0=x_sb[:, m, :], scalar=gain[:, m:m + 1],
                                         in1=h_hi[:, m, :].bitcast(F32), op0=ALU.mult,
                                         op1=ALU.subtract).then_inc(h_ready, 1)

            def update(done, scale, n=None, gain=None, lag=1):
                for i in range(KB + lag):
                    if i < KB:
                        m = DONE_ORDER[i]
                        dve.wait_ge(*done(i))
                        dve.scalar_tensor_tensor(out=x_sb[:, m, :], in0=ps[:, m, :], scalar=scale, in1=x_sb[:, m, :],
                                                 op0=ALU.mult, op1=ALU.add).then_inc(x_ready, 1)
                    if n is not None and 0 <= i - lag < KB:
                        low(n, i - lag, gain)

            def feed_forward(n, F, p0, o0, next_n, next_gain):
                dve.wait_ge(guess_ready, n + 1)
                newton(T)
                with dve.Fori(0, FB // 2) as i:
                    for e in range(2):
                        dve.wait_ge(panel_done, p0 + 2 * i + e + 1)
                        c = bass.ds(2 * i + e, 1)
                        dve.tensor_tensor(hraw[:, e, :], ps[:, 2 * e, :], rstd, ALU.mult).then_inc(gate_in, 1)
                        dve.tensor_tensor(sq[:, e, :], ps[:, 2 * e + 1, :], rstd, ALU.mult).then_inc(gate_up_out, 1)
                        dve.drain()
                        dve.wait_ge(silu_ready, FB * F + 2 * i + e + 1)
                        dve.tensor_tensor(sq[:, e, :], hraw[:, e, :], sq[:, e, :], ALU.mult)
                        dve.drain()
                        dve.tensor_copy(hid_hi[:, c, :], sq[:, e:e + 1, :])
                        dve.drain()
                        remainder(hid_lo[:, c, :], sq[:, e:e + 1, :], hid_hi[:, c, :]).then_inc(hid_ready, 1)
                update(lambda i: (panel_done, p0 + FFN_PANELS) if i == KB - 1 else (out_ready, o0 + i + 1),
                       0.5, next_n, next_gain)

            def project_out(p0, o0, next_n=None, next_gain=None):
                update(lambda i: (panel_done, p0 + i // 2 + 1) if i % 2 else (out_ready, o0 + i // 2 + 1),
                       1.0, next_n, next_gain, KB)

            def pool_block(l, c):
                n = T + 2 * PAD
                up = slice(64, P)
                a = apad[:, c, :]

                w0, w1 = win[:, 0, :], win[:, 1, :]
                dve.tensor_tensor(w0[:, 1:n], a[:, 0:n - 1], a[:, 1:n], ALU.add)
                dve.drain()
                if c == 0:
                    dve.tensor_tensor(w1[up, 2:n - 1], w0[up, 1:n - 2], w0[up, 3:n], ALU.add)
                else:
                    dve.tensor_tensor(w1[:, 2:n - 1], w0[:, 1:n - 2], w0[:, 3:n], ALU.add)
                    dve.drain()
                    dve.tensor_tensor(w0[:, 4:n - 3], w1[:, 2:n - 5], w1[:, 6:n - 1], ALU.add)
                    dve.drain()
                    dve.tensor_tensor(w1[up, 8:n - 7], w0[up, 4:n - 11], w0[up, 12:n - 3], ALU.add)
                dve.drain()
                t = slice(PAD, PAD + T)
                if c == 0:
                    dve.wait_ge(in_mix, 32 * l + 32)
                for rows, w in ((slice(0, 64), w0), (up, w1)):
                    dve.tensor_tensor(hraw[rows, c, :], w[rows, t], rec_sb[rows, c, :], ALU.mult)
                dve.drain()
                dve.tensor_tensor(hraw[:, c, :], hraw[:, c, :], a[:, t], ALU.subtract)
                dve.drain()
                dve.tensor_copy(m_hi[:, c, :], hraw[:, c, :])
                dve.drain()
                remainder(m_lo[:, c, :], hraw[:, c, :], m_hi[:, c, :]).then_inc(pooled, 1)

            def mixer1(l, n, p0):
                dve.wait_ge(guess_ready, n + 1)
                newton(T)
                dve.engine_nop().then_inc(rstd_ready, 1)
                dve.memset(apad[:, :, 0:PAD], 0.0)
                dve.memset(apad[:, :, PAD + T:], 0.0)
                dve.drain()
                for i, (kind, c, bank, ends) in enumerate(MIX_UNITS):
                    src = ps[:, bank, :]
                    if (kind, c) in (("q", 2), ("k", 1)):
                        pool_block(l, int(kind == "k"))
                        dve.drain()
                    if (kind, c) == ("q", 0):
                        dve.wait_ge(rstd_turned, l + 1)
                        dve.tensor_copy(tok_rstd[:], ps[:, SUM_BANK, :].rearrange("p (t n) -> p t n", t=TB)[:, :, 0])
                    if kind in NORMED:
                        if ends is None:
                            dve.wait_ge(unit_ready, READY1 * l + READY_BEFORE[i + 1])
                        else:
                            dve.wait_ge(panel_done, p0 + ends + 1)
                        normed = hraw[:, i % 2, :]
                        if kind == "v":
                            ins = dve.tensor_scalar(normed[:, 0:256], src[:, 0:256], tok_rstd[:, c % 4:c % 4 + 1],
                                                    None, ALU.mult)
                        else:
                            ins = dve.scalar_tensor_tensor(out=normed, in0=src, scalar=0.125 if kind == "q" else 1.0,
                                                           in1=rstd, op0=ALU.mult, op1=ALU.mult)
                        ins.then_inc(unit_in, 1)
                        dve.drain()
                        src = normed
                    dve.wait_ge(unit_hi, NU * l + i + 1)
                    if kind == "a":
                        dve.memset(tick[:], 0.0).then_inc(unit_lo, 1)
                        continue
                    if kind in ("f", "yf"):
                        ins = remainder(f_lo[:, c, :], src, f_hi[:, c, :])
                    elif kind == "q":
                        ins = remainder(q_lo[:, c, :], src, q_hi[:, c, :])
                    elif kind == "k":
                        ins = remainder(k_lo[:, c, :], src, k_hi[:, c, :])
                    elif kind == "v":
                        s = slice(256 * (c // 4), 256 * (c // 4) + 256)
                        ins = remainder(v_lo[:, c % 4, s], src[:, 0:256], v_hi[:, c % 4, s])
                    elif kind == "fc":
                        ins = remainder(fc_lo[:, c, :], src, fc_hi[:, c, :])
                    elif kind == "four":
                        ins = remainder(h_lo[:, 2 + c, :], src, h_hi[:, 2 + c, :])
                    else:
                        ins = dve.scalar_tensor_tensor(out=h_lo[:, c, :], in0=src,
                                                       scalar=v1[:, G_POOL + c:G_POOL + c + 1],
                                                       in1=h_hi[:, c, :].bitcast(F32), op0=ALU.mult, op1=ALU.subtract)
                    ins.then_inc(unit_lo, 1)
                u0 = UNITS1 * l
                for s in range(UNITS1 + 8):
                    if s < UNITS1:
                        h, b = units1[s]
                        dve.wait_ge(s_scores, u0 + s + 1)
                        if b == 0:
                            dve.wait_ge(bias_ready, HEADS1 * l + h + 1)
                        if s >= 2:
                            dve.wait_ge(s_att, u0 + s - 1)
                        dve.memset(tick[:], 0.0)
                        for j in range(2):
                            dve.tensor_tensor_reduce(prob1[:, s % 2, j, :], ps[:, 2 * (s % 2) + j, :],
                                                     bias[:, h % 2, T - P - P * b:2 * T - P - P * b],
                                                     1.0, -3e38, ALU.add, ALU.max, mx[:, s % 2, j:j + 1])
                        dve.drain()
                        dve.tensor_scalar(nmx[:, s % 2, :], mx[:, s % 2, :], -1.0, None, ALU.mult).then_inc(s_max, 1)
                    if 1 <= s <= UNITS1:
                        u = s - 1
                        dve.wait_ge(s_exp, u0 + u + 1)
                        if u >= 2:
                            dve.wait_ge(s_tr, u0 + u - 1)
                        dve.reciprocal(rsum[:, u % 2, :], ssum[:, u % 2, :])
                        dve.drain()
                        dve.tensor_scalar(att1[:, u % 2, :], prob1[:, u % 2, 0, :], rsum[:, u % 2, 0:1], None, ALU.mult)
                        dve.tensor_tensor(rsum[:, u % 2, 1:2], rsum[:, u % 2, 1:2], nlam[:], ALU.mult)
                        dve.drain()
                        dve.scalar_tensor_tensor(out=att1[:, u % 2, :], in0=prob1[:, u % 2, 1, :],
                                                 scalar=rsum[:, u % 2, 1:2], in1=att1[:, u % 2, :],
                                                 op0=ALU.mult, op1=ALU.add).then_inc(s_att, 1)
                    if 3 <= s <= UNITS1 + 2:
                        u = s - 3
                        q = slice(P * units1[u][1], P * units1[u][1] + P)
                        dve.wait_ge(s_thi, u0 + u + 1)
                        remainder(at_lo[:, :, q], ps[:, 4 + u % 2, :].rearrange("p (k n) -> p k n", k=TB),
                                  at_hi[:, :, q]).then_inc(s_tlo, 1)
                    if s >= 7 and (s - 7) % TB == TB - 1 and s - 7 < UNITS1:
                        h = (s - 7) // TB
                        dve.wait_ge(s_oguess, HEADS1 * l + h + 1)
                        newton(T)
                        dve.scalar_tensor_tensor(out=hraw[:, 0, :], in0=ps[:, 6 + h % 2, :], scalar=v1[:, G_HEAD + h:G_HEAD + h + 1],
                                                 in1=rstd, op0=ALU.mult, op1=ALU.mult)
                        dve.drain()
                        dve.tensor_copy(h_hi[:, 4 + h, :], hraw[:, 0, :])
                        dve.drain()
                        remainder(h_lo[:, 4 + h, :], hraw[:, 0, :], h_hi[:, 4 + h, :]).then_inc(s_y, 1)
                project_out(p0 + MIX_PANELS, 18 * l + KB - 1, n + 1, v1[:, G_FFN2:G_FFN2 + KB])

            def head_norm(G, width, scales):
                dve.wait_ge(hn_guess, G + 1)
                newton(width, 2)
                w = slice(0, width)
                for j in range(2):
                    dve.scalar_tensor_tensor(out=xs[:, j, w], in0=xs[:, j, w], scalar=scales[j], in1=guess[:, j, w],
                                             op0=ALU.mult, op1=ALU.mult)
                dve.drain()

            def head_split(width, dst_hi, dst_lo):
                w = slice(0, width)
                dve.tensor_copy(dst_hi[:, :, w], xs[:, :, w])
                dve.drain()
                remainder(dst_lo[:, :, w], xs[:, :, w], dst_hi[:, :, w]).then_inc(hn_out, 1)

            def attention_step(here, before, s, produce, part):
                if here:
                    w, b = slice(0, here.widths[s]), s % TB
                    dve.wait_ge(t_scores, here.u0 + s + 1)
                    if lagged(here, before, s, 2):
                        dve.wait_ge(t_att, here.u0 + s - 1)
                    if here.memory:
                        dve.tensor_reduce(mx[:, s % 2, 0:1], ps[:, s % 2, w], AX_X, ALU.max)
                    else:
                        dve.memset(tick[:], 0.0)
                        dve.tensor_tensor_reduce(prob2[:, s % 2, w], ps[:, s % 2, w],
                                                 mask[:, here.branch, T - P - P * b:T],
                                                 1.0, -3e38, ALU.add, ALU.max, mx[:, s % 2, 0:1])
                    dve.drain()
                    dve.tensor_scalar(nmx[:, s % 2, 0:1], mx[:, s % 2, 0:1], -1.0, None, ALU.mult).then_inc(t_max, 1)
                if here and s == here.n - 1 and not here.last:
                    head_split(T, qk_hi, qk_lo)
                unit = lagged(here, before, s, 1)
                if unit:
                    stage, u = unit
                    w = slice(0, stage.widths[u])
                    dve.wait_ge(t_exp, stage.u0 + u + 1)
                    if u >= 2 or not stage.memory:
                        dve.wait_ge(t_tr, stage.u0 + u - 1)
                    dve.reciprocal(rsum[:, u % 2, 0:1], ssum[:, u % 2, 0:1])
                    dve.drain()
                    dve.tensor_scalar(att2[:, u % 2, w], prob2[:, u % 2, w], rsum[:, u % 2, 0:1], None,
                                      ALU.mult).then_inc(t_att, 1)
                unit = lagged(here, before, s, LAG_TR)
                if unit:
                    stage, u = unit
                    q, kbs = slice(P * (u % TB), P * (u % TB) + P), stage.widths[u] // P
                    dve.wait_ge(t_thi, stage.u0 + u + 1)
                    remainder(pt_lo[:, 0:kbs, q], ps[:, 2 + u % 2, 0:P * kbs].rearrange("p (k n) -> p k n", k=kbs),
                              pt_hi[:, 0:kbs, q]).then_inc(t_tlo, 1)
                unit = lagged(here, before, s, LAG_GATE)
                if unit and unit[1] % PAIR_UNITS == PAIR_UNITS - 1:
                    stage, u = unit
                    dve.wait_ge(t_o, stage.heads0 + u // TB + 1)
                    if stage.memory:
                        c = slice(6 + u // PAIR_UNITS, 7 + u // PAIR_UNITS)
                    elif isinstance(stage.gi, int):
                        c = slice(stage.gi - 2, stage.gi - 1)
                    else:
                        c = bass.ds(stage.gi - 2, 1)
                    dve.tensor_tensor(y[:, c, :], y[:, c, :], ps[:, 5:6, :], ALU.mult).then_inc(t_y, 1)
                if here and not here.memory and s == 5:
                    dve.wait_ge(v_thi, 7 * here.l + here.gi)
                    for h in range(2):
                        c = slice(64 * h, 64 * h + 64)
                        ins = remainder(vp_lo[:, :, h, c], ps[:, 5, :].rearrange("p (t n) -> p t n", t=TB)[:, :, c],
                                        vp_hi[:, :, h, c])
                    ins.then_inc(v_tlo, 1)
                if produce and part is not None:
                    produce(part)

            def producer(l, gi, beside):
                G = GROUPS * l + gi

                def step(s):
                    if s in (3, 5):
                        j = (s - 3) // 2
                        dve.wait_ge(hn_mm, 2 * G + j + 1)
                        dve.tensor_tensor(xs[:, j, :], xs[:, j, :], rope_sb[:, 0, :], ALU.mult)
                        dve.tensor_tensor(hraw[:, 1, :], ps[:, 6, :], rope_sb[:, 1, :], ALU.mult)
                        dve.drain()
                        dve.tensor_tensor(xs[:, j, :], xs[:, j, :], hraw[:, 1, :], ALU.add).then_inc(hn_rot, 1)
                    if s == 6:
                        head_norm(G, T, (0.125, 1.0))
                return step

            def memory_norm(l):
                for k in range(KB):
                    g = v2_all[:, bass.ds(NV2 * l + G_MEM + k, 1)]
                    dve.tensor_scalar(mh_hi[:, k, :], memn[:, k, :], g, None, ALU.mult)
                    dve.drain()
                    dve.scalar_tensor_tensor(out=mh_lo[:, k, :], in0=memn[:, k, :], scalar=g,
                                             in1=mh_hi[:, k, :].bitcast(F32), op0=ALU.mult,
                                             op1=ALU.subtract).then_inc(memh_ready, 1)

            def stack2(l):
                n = 3 * LAYERS + 1 + l
                p0 = BASE2 + LAYER2_PANELS * l
                g0 = GROUPS * l
                dve.tensor_copy(v2[:], v2_all[:, bass.ds(NV2 * l, NV2)]).then_inc(v2_ready, 1)
                dve.drain()
                norm(n, v2[:, G_NORM:G_NORM + KB])
                head_norm(g0, 256, (1.0, 1.0))
                head_split(256, km_hi, km_lo)
                dve.wait_ge(v_thi, 7 * l + 1)
                for h in range(2):
                    s = slice(64 * h, 64 * h + 64)
                    ins = remainder(vm_lo[:, :, :, h, s],
                                    ps[:, 4, :].rearrange("p (t c n) -> p t c n", t=2, c=2)[:, :, :, s],
                                    vm_hi[:, :, :, h, s])
                ins.then_inc(v_tlo, 1)
                head_norm(g0 + 1, T, (0.125, 0.125))
                head_split(T, qk_hi, qk_lo)

                def split_y(i):
                    k = Y_ORDER[i]
                    dve.drain()
                    if i == 0:
                        dve.wait_ge(panel_done, p0 + 2 * GROUPS)
                    dve.tensor_copy(h_hi[:, k, :], y[:, k, :])
                    dve.drain()
                    remainder(h_lo[:, k, :], y[:, k, :], h_hi[:, k, :]).then_inc(y_ready, 1)

                def beside_last(s):
                    if s >= 1:
                        split_y(s - 1)

                run_stages(l, dve.Fori, attention_step, producer, beside_last,
                           lambda s: split_y(KB - 1) if s == LAG_GATE - 1 else None)
                memory_norm(l + 1)
                project_out(p0 + 2 * GROUPS, 18 * LAYERS + OUT_PANELS * l)

            dve.wait_ge(in_small, 16 * 5)
            dve.memset(newt[0:64, 0, 0:P], 1.0)
            dve.drain()
            dve.tensor_tensor(hraw[0:64, 0, 0:4], hraw[0:64, 1, 0:4], hraw[0:64, 1, 4:8], ALU.mult).then_inc(lam_in, 1)
            dve.wait_ge(lam_exp, 1)
            e = hraw[:, 1, 8:12].rearrange("p (l n) -> p l n", l=LAYERS)
            dve.tensor_tensor(nlam_all[:], e[:, :, 1], e[:, :, 0], ALU.subtract)
            dve.drain()
            dve.tensor_tensor(nlam_all[:], nlam_all[:],
                              v1_all[:].rearrange("p (l n) -> p l n", l=LAYERS)[:, :, G_LAM], ALU.subtract)
            dve.wait_ge(in_x, 16)
            for i in range(KB):
                dve.engine_nop().then_inc(x_ready, 1)
            with dve.Fori(0, LAYERS) as l:
                p0 = LAYER1_PANELS * l
                dve.drain()
                dve.tensor_copy(v1[:], v1_all[:, bass.ds(NV1 * l, NV1)])
                dve.tensor_copy(nlam[:], nlam_all[:, bass.ds(l, 1)])
                dve.drain()
                dve.tensor_scalar(v1[:, G_HEAD:G_HEAD + HEADS1], v1[:, G_HEAD:G_HEAD + HEADS1],
                                  v1[:, G_KEEP:G_KEEP + 1], None, ALU.mult)
                dve.drain()
                dve.engine_nop().then_inc(v1_ready, 1)
                for i in range(KB):
                    low(3 * l, i, v1[:, G_FFN1:G_FFN1 + KB])
                feed_forward(3 * l, 2 * l, p0, 18 * l, 3 * l + 1, v1[:, G_MIX:G_MIX + KB])
                mixer1(l, 3 * l + 1, p0 + FFN_PANELS)
                feed_forward(3 * l + 2, 2 * l + 1, p0 + LAYER1_PANELS - FFN_PANELS,
                             18 * l + KB - 1 + OUT_PANELS, None, None)
            for z in (vp_hi, vp_lo, vm_hi, vm_lo):
                dve.memset(z[:].bitcast(F32), 0.0)
            dve.wait_ge(guess_ready, 3 * LAYERS + 1)
            newton(T)
            for m in DONE_ORDER:
                dve.scalar_tensor_tensor(out=x_sb[:, m, :], in0=x_sb[:, m, :], scalar=fin_g[:, m:m + 1], in1=rstd,
                                         op0=ALU.mult, op1=ALU.mult).then_inc(x_ready, 1)
            dve.drain()
            dve.wait_ge(mem_guess, 1)
            newton(256)
            for k in range(KB):
                ins = dve.tensor_tensor(memn[:, k, :], memn[:, k, :], guess[:, 0, 0:256], ALU.mult)
            ins.then_inc(mem_normed, 1)
            dve.drain()
            memory_norm(0)
            with dve.Fori(0, LAYERS) as l:
                stack2(l)


def blocks(w, cols):
    r, n = w.shape
    return w.reshape(r // P, P, n // cols, cols).transpose(2, 1, 0, 3).reshape(n // cols, P, -1)


def weight_stream(inp, const):
    out = np.zeros((ALL_PANELS + SPARE_PANELS, P, PANEL), np.float32)
    at = 0

    def put(panels):
        nonlocal at
        out[at:at + len(panels), :, :panels.shape[2]] = panels
        at += len(panels)

    def feed_forward(gate, up, down):
        both = np.stack([gate.reshape(D, FB, P), up.reshape(D, FB, P)], 2).reshape(D, 2 * FF)
        put(blocks(both, 2 * P))
        put(down.reshape(DOWN_PANELS, 2, P, D).transpose(0, 2, 1, 3).reshape(DOWN_PANELS, P, PANEL))

    def out_blocks(w):
        put(blocks(w.reshape(D, KB, P)[:, DONE_ORDER].reshape(D, D), 2 * P))

    for l in range(LAYERS):
        feed_forward(inp["ffn1_w_gate"][l], inp["ffn1_w_up"][l], inp["ffn1_w_down"][l])
        w_in = blocks(inp["w_in"][l], 2 * P)
        put(w_in[:4])
        put(const["chan"][None])
        put(w_in[4:6])
        put(const["seq"])
        put(w_in[6:])
        four = inp["fourier_w"][l].reshape(2, P, 2 * P).transpose(1, 0, 2).reshape(P, 4 * P)
        pool = np.zeros((P, 2, P), np.float32)
        for g in range(4):
            s = slice(64 * (g % 2), 64 * (g % 2) + 64)
            pool[s, g // 2, s] = inp["pool_w"][l][g]
        put(np.concatenate([four, pool.reshape(P, 2 * P)], 1)[None])
        out_blocks(inp["w_out"][l])
        feed_forward(inp["ffn2_w_gate"][l], inp["ffn2_w_up"][l], inp["ffn2_w_down"][l])
    for l in range(LAYERS):
        w = inp["w_in_2"][l]
        put(blocks(inp["w_mem_kv_2"][l], 2 * P))
        put(blocks(w[:, 3072:3584], 2 * P))
        for branch in range(2):
            for j in range(3):
                q, k, v, g = (w[:, 1536 * branch + 384 * i + P * j:][:, :P] for i in range(4))
                put(blocks(np.concatenate([q, k, v, g], 1), 2 * P))
        out_blocks(inp["w_out_2"][l])
    assert at == ALL_PANELS
    return out


def columns(v):
    return v.reshape(-1, P).T


def kernel(**inputs):
    import concourse.bacc as bacc
    from concourse.bass_utils import run_bass_kernel_spmd as run

    inp = {k: np.asarray(v) for k, v in inputs.items()}
    const = shape_constants()
    start = [0.8 - 0.6 * math.exp(-0.3 * l) for l in range(LAYERS)]
    f = np.float32
    vecs1 = [np.concatenate([
        columns(inp["ffn1_norm"][l]), columns(inp["mix_norm"][l]), columns(inp["ffn2_norm"][l]),
        columns(inp["pool_scale"][l]), columns(inp["attn_head_norm"][l]),
        np.full((P, 1), 1.0 - start[l], f), np.full((P, 1), start[l], f)], 1) for l in range(LAYERS)]
    vecs2 = [np.concatenate([
        columns(inp["norm_g_2"][l]), columns(inp["mem_norm_g_2"][l]),
        np.concatenate([inp["qk_g_2"][l][[5, 5, 4, 4] + 3 * [0, 1] + 3 * [2, 3]].T] * 2, 0)], 1) for l in range(LAYERS)]
    lamv = np.stack([inp[n][l] for a in "qk" for l in range(LAYERS) for n in (f"lam_{a}1", f"lam_{a}2")], 1)
    feature_major = lambda a: a[0].T.reshape(KB, P, -1).transpose(1, 0, 2).reshape(P, -1)
    arrays = {
        "x": feature_major(inp["x"]), "mem": feature_major(inp["mem_2"]),
        "stream": weight_stream(inp, const),
        "vecs1": np.concatenate(vecs1, 1), "vecs2": np.concatenate(vecs2 + vecs2[:1], 1),
        "final_g": columns(inp["final_norm"]), "lamv": lamv, "consts": const["consts"],
        "dist": const["dist"], "masks": const["masks"].reshape(P, 2, TOE)[:, :, :T].reshape(P, 2 * T),
        "recip": const["recip"], "rope": const["rope"],
    }
    arrays = {k: np.ascontiguousarray(v) for k, v in arrays.items()}
    nc = bacc.Bacc("TRN2", target_bir_lowering=False, num_devices=1)
    args = [nc.dram_tensor(f"in_{k}", a.shape, mybir.dt.from_np(a.dtype), kind="ExternalInput").ap()
            for k, a in arrays.items()]
    args.append(nc.dram_tensor("out_x", (P, KB, T), F32, kind="ExternalOutput").ap())
    names = dict(zip(arrays, args))
    build(nc, **names, out=args[-1])
    r = run(nc, [{f"in_{k}": a for k, a in arrays.items()}], core_ids=[0])
    got = np.asarray(r.results[0]["out_x"])
    return np.ascontiguousarray(got.transpose(1, 0, 2).reshape(D, T).T)[None]
```
